# Optimizing a Trainium2 kernel written in Bass

```python
import math
import jax, jax.numpy as jnp
from jax import lax
import numpy as np

D_MODEL = 1024
BATCH = 1
SEQ = 1024
DEPTH = 1

PLE_DIM = 256
D_POOL = D_MODEL // 2
POOL_WINDOWS = (2, 4, 8, 16)
N_POOL_GROUPS = len(POOL_WINDOWS)
POOL_GROUP_DIM = D_POOL // N_POOL_GROUPS
SB_HEADS = 8
SB_HEAD_DIM = 64
D_SB = SB_HEADS * SB_HEAD_DIM
Q_BLOCK = 128
D_FF = ((8 * D_MODEL // 3 + 255) // 256) * 256
D_IN = D_POOL + 3 * D_SB + 2 * D_MODEL
RMS_EPS = 1e-6


def rms_norm(x, gain):
    xf = x.astype(jnp.float32)
    inv = lax.rsqrt(jnp.mean(xf * xf, axis=-1, keepdims=True) + RMS_EPS)
    return (xf * inv * gain.astype(jnp.float32)).astype(x.dtype)

def pool_mixer(u, w_pool, pool_scale):
    B, S, _ = u.shape
    uf = u.astype(jnp.float32)
    csum = jnp.cumsum(uf, axis=1)
    t = jnp.arange(S, dtype=jnp.int32)
    outs = []
    for g, w in enumerate(POOL_WINDOWS):
        sl = slice(g * POOL_GROUP_DIM, (g + 1) * POOL_GROUP_DIM)
        cg = csum[..., sl]
        prev = jnp.pad(cg, ((0, 0), (w, 0), (0, 0)))[:, :S]
        count = jnp.minimum(t + 1, w).astype(jnp.float32)[None, :, None]
        outs.append((cg - prev) / count - uf[..., sl])
    pooled = jnp.stack(outs, axis=2).astype(u.dtype)
    mixed = jnp.einsum('bsgc,gcd->bsgd', pooled, w_pool).reshape(B, S, D_POOL)
    return mixed * pool_scale

def stick_breaking_attention(q, k, v):
    B, H, S, dh = q.shape
    n_blk = S // Q_BLOCK
    scale = 1.0 / math.sqrt(dh)
    q_blocks = q.reshape(B, H, n_blk, Q_BLOCK, dh).transpose(2, 0, 1, 3, 4)
    starts = jnp.arange(n_blk, dtype=jnp.int32) * Q_BLOCK
    k_pos = jnp.arange(S, dtype=jnp.int32)

    def one_block(args):
        q_i, start = args
        z = jnp.einsum('bhqd,bhkd->bhqk', q_i, k).astype(jnp.float32) * scale
        t_pos = start + jnp.arange(Q_BLOCK, dtype=jnp.int32)
        mask = k_pos[None, :] < t_pos[:, None]
        log_fail = jnp.where(mask, jax.nn.log_sigmoid(-z), 0.0)
        suffix = lax.cumsum(log_fail, axis=3, reverse=True) - log_fail
        a = jnp.where(mask, jnp.exp(jax.nn.log_sigmoid(z) + suffix), 0.0)
        return jnp.einsum('bhqk,bhkd->bhqd', a.astype(v.dtype), v)

    out = lax.map(one_block, (q_blocks, starts))
    return out.transpose(1, 2, 0, 3, 4).reshape(B, H, S, dh)

def first_inputs(seed: int = 0) -> dict:
    key = jax.random.key(seed)
    ks = jax.random.split(key, 20)
    f32 = jnp.float32

    def nrm(k, shape, fan_in):
        return jax.random.normal(k, shape, f32) * (fan_in ** -0.5)

    def gain(k, shape):
        return jnp.ones(shape, f32) + 0.02 * jax.random.normal(k, shape, f32)

    return {
        "x": jax.random.normal(ks[0], (BATCH, SEQ, D_MODEL), f32),
        "p": jax.random.normal(ks[1], (DEPTH, BATCH, SEQ, PLE_DIM), f32),
        "norm_mix": gain(ks[2], (DEPTH, D_MODEL)),
        "w_in": nrm(ks[3], (DEPTH, D_MODEL, D_IN), D_MODEL),
        "w_pool": nrm(ks[4], (DEPTH, N_POOL_GROUPS, POOL_GROUP_DIM, POOL_GROUP_DIM), POOL_GROUP_DIM),
        "pool_scale": gain(ks[5], (DEPTH, D_POOL)),
        "w_branch_a": nrm(ks[6], (DEPTH, D_POOL, D_MODEL), D_POOL),
        "w_branch_b": nrm(ks[7], (DEPTH, D_SB, D_MODEL), D_SB),
        "w_out": nrm(ks[8], (DEPTH, D_MODEL, D_MODEL), D_MODEL),
        "norm_ffn": gain(ks[9], (DEPTH, D_MODEL)),
        "w_ffn_gate": nrm(ks[10], (DEPTH, D_MODEL, D_FF), D_MODEL),
        "w_ffn_up": nrm(ks[11], (DEPTH, D_MODEL, D_FF), D_MODEL),
        "w_ffn_down": nrm(ks[12], (DEPTH, D_FF, D_MODEL), D_FF),
        "norm_ple": gain(ks[13], (DEPTH, D_MODEL)),
        "w_ple_gate": nrm(ks[14], (DEPTH, D_MODEL, D_MODEL), D_MODEL),
        "w_ple_proj": nrm(ks[15], (DEPTH, PLE_DIM, D_MODEL), PLE_DIM),
        "norm_final": gain(ks[16], (D_MODEL,)),
    }

def first_block(x, p, norm_mix, w_in, w_pool, pool_scale, w_branch_a, w_branch_b, w_out,
              norm_ffn, w_ffn_gate, w_ffn_up, w_ffn_down, norm_ple, w_ple_gate, w_ple_proj,
              norm_final):
    B, S, _ = x.shape
    split_at = [D_POOL, D_POOL + D_SB, D_POOL + 2 * D_SB, D_POOL + 3 * D_SB,
                D_POOL + 3 * D_SB + D_MODEL]
    for i in range(DEPTH):
        h = rms_norm(x, norm_mix[i])
        proj = h @ w_in[i]
        u_pool, q, k, v, g_a, g_b = jnp.split(proj, split_at, axis=-1)
        y_a = pool_mixer(u_pool, w_pool[i], pool_scale[i])
        to_heads = lambda t: t.reshape(B, S, SB_HEADS, SB_HEAD_DIM).transpose(0, 2, 1, 3)
        y_b = stick_breaking_attention(to_heads(q), to_heads(k), to_heads(v))
        y_b = y_b.transpose(0, 2, 1, 3).reshape(B, S, D_SB)
        merged = (jax.nn.sigmoid(g_a) * (y_a @ w_branch_a[i])
                  + jax.nn.sigmoid(g_b) * (y_b @ w_branch_b[i]))
        x = x + merged @ w_out[i]
        h = rms_norm(x, norm_ffn[i])
        x = x + (jax.nn.silu(h @ w_ffn_gate[i]) * (h @ w_ffn_up[i])) @ w_ffn_down[i]
        gate = jax.nn.sigmoid(rms_norm(x, norm_ple[i]) @ w_ple_gate[i])
        x = x + gate * (p[i] @ w_ple_proj[i])
    return rms_norm(x, norm_final)


ML_H = 4
ML_HD = D_MODEL // 8
ML_W = ML_H * ML_HD
ML_CONV = 4
ML_CHUNK = 64
ATT_H = 8
ATT_KV = 2
ATT_HD = 64
ATT_W = ATT_H * ATT_HD
WINDOW = 128
ATT_BLOCK = WINDOW
ROPE_THETA = 10000.0
MIX_W = ML_W + ATT_W
IN_COLS = 4 * ML_W + 2 * ML_H + ATT_W + 2 * ATT_KV * ATT_HD
D_FF_2 = 2816
FFN_CONV = 3
N_MOD = 6


def rms_norm_2(x, g):
    xf = x.astype(jnp.float32)
    y = xf * lax.rsqrt(jnp.mean(xf * xf, axis=-1, keepdims=True) + RMS_EPS)
    return (y * g.astype(jnp.float32)).astype(x.dtype)

def causal_dwconv(x, w, b):
    k_len, ch = w.shape
    y = lax.conv_general_dilated(
        x, w[:, None, :].astype(x.dtype), window_strides=(1,),
        padding=((k_len - 1, 0),), dimension_numbers=("NWC", "WIO", "NWC"),
        feature_group_count=ch)
    return y + b.astype(x.dtype)

def rope(x, pos):
    half = x.shape[-1] // 2
    inv = ROPE_THETA ** (-jnp.arange(half, dtype=jnp.float32) / half)
    ang = pos.astype(jnp.float32)[:, None] * inv[None, :]
    cos = jnp.cos(ang)[None, :, None, :]
    sin = jnp.sin(ang)[None, :, None, :]
    xf = x.astype(jnp.float32)
    x1, x2 = xf[..., :half], xf[..., half:]
    return jnp.concatenate([x1 * cos - x2 * sin, x2 * cos + x1 * sin], axis=-1)

def sliding_window_attention(q, k, v, sinks):
    B, S, H, D = q.shape
    G = k.shape[2]
    R = H // G
    nb = S // ATT_BLOCK
    qb = q.reshape(B, nb, ATT_BLOCK, G, R, D)
    kb = k.reshape(B, nb, ATT_BLOCK, G, D)
    vb = v.reshape(B, nb, ATT_BLOCK, G, D)
    pad = ((0, 0), (1, 0), (0, 0), (0, 0), (0, 0))
    kband = jnp.concatenate([jnp.pad(kb, pad)[:, :-1], kb], axis=2)
    vband = jnp.concatenate([jnp.pad(vb, pad)[:, :-1], vb], axis=2)
    s = jnp.einsum('bnqgrd,bnkgd->bngrqk', qb, kband) * (1.0 / math.sqrt(D))
    qi = jnp.arange(ATT_BLOCK)[:, None] + ATT_BLOCK
    kj = jnp.arange(2 * ATT_BLOCK)[None, :]
    rel = qi - kj
    band = (rel >= 0) & (rel < WINDOW)
    kpos = jnp.arange(nb)[:, None, None] * ATT_BLOCK + kj[None] - ATT_BLOCK
    valid = band[None] & (kpos >= 0)
    s = jnp.where(valid[None, :, None, None], s, -jnp.inf)
    sk = sinks.astype(jnp.float32).reshape(G, R)[None, None, :, :, None, None]
    m = jnp.maximum(jnp.max(s, axis=-1, keepdims=True), sk)
    p = jnp.exp(s - m)
    denom = jnp.sum(p, axis=-1, keepdims=True) + jnp.exp(sk - m)
    p = p / denom
    o = jnp.einsum('bngrqk,bnkgd->bnqgrd', p, vband)
    return o.reshape(B, S, H, D)

def mlstm_chunkwise(q, k, v, i_pre, logf):
    B, S, H, D = q.shape
    L = ML_CHUNK
    nc = S // L
    to_c = lambda t: t.reshape(B, nc, L, H, D).transpose(1, 0, 3, 2, 4)
    to_cg = lambda t: t.reshape(B, nc, L, H).transpose(1, 0, 3, 2)
    causal = jnp.tril(jnp.ones((L, L), dtype=bool))

    def step(carry, xs):
        C, n, m = carry
        qc, kc, vc, ic, fc = xs
        b = jnp.cumsum(fc, axis=-1)
        dmat = jnp.where(causal, b[..., :, None] - b[..., None, :] + ic[..., None, :], -jnp.inf)
        m_inter = b + m[..., None]
        m_t = jnp.maximum(m_inter, jnp.max(dmat, axis=-1))
        w_inter = jnp.exp(m_inter - m_t)
        sqk = jnp.einsum('bhtd,bhsd->bhts', qc, kc) * jnp.exp(dmat - m_t[..., None])
        num = jnp.einsum('bhts,bhsd->bhtd', sqk, vc) + \
            w_inter[..., None] * jnp.einsum('bhvk,bhtk->bhtv', C, qc)
        den = jnp.sum(sqk, axis=-1) + w_inter * jnp.einsum('bhk,bhtk->bht', n, qc)
        h = num / jnp.maximum(jnp.abs(den), jnp.exp(-m_t))[..., None]
        b_last = b[..., -1]
        g = b_last[..., None] - b + ic
        m_new = jnp.maximum(b_last + m, jnp.max(g, axis=-1))
        decay = jnp.exp(b_last + m - m_new)
        ws = jnp.exp(g - m_new[..., None])
        C_new = decay[..., None, None] * C + jnp.einsum('bhsv,bhsk->bhvk', vc * ws[..., None], kc)
        n_new = decay[..., None] * n + jnp.einsum('bhs,bhsk->bhk', ws, kc)
        return (C_new, n_new, m_new), h

    init = (jnp.zeros((B, H, D, D), jnp.float32), jnp.zeros((B, H, D), jnp.float32),
            jnp.zeros((B, H), jnp.float32))
    _, hs = lax.scan(step, init, (to_c(q), to_c(k), to_c(v), to_cg(i_pre), to_cg(logf)))
    return hs.transpose(1, 0, 3, 2, 4).reshape(B, S, H, D)

def token_mixer(h, w_in, ml_conv_w, ml_conv_b, ml_i_b, ml_f_b, ml_norm_g,
                attn_sinks, attn_norm_g, w_out):
    B, S, _ = h.shape
    proj = h @ w_in
    cuts = [2 * ML_W, 3 * ML_W, 4 * ML_W, 4 * ML_W + 2 * ML_H, 4 * ML_W + 2 * ML_H + ATT_W]
    qk_ml, v_ml, o_ml, gates, q_at, kv_at = jnp.split(proj, cuts, axis=-1)
    qk_ml = jax.nn.silu(causal_dwconv(qk_ml, ml_conv_w, ml_conv_b)).astype(jnp.float32)
    q_ml = qk_ml[..., :ML_W].reshape(B, S, ML_H, ML_HD)
    k_ml = qk_ml[..., ML_W:].reshape(B, S, ML_H, ML_HD) * (1.0 / math.sqrt(ML_HD))
    v_ml = v_ml.astype(jnp.float32).reshape(B, S, ML_H, ML_HD)
    gates = gates.astype(jnp.float32)
    i_pre = gates[..., :ML_H] + ml_i_b.astype(jnp.float32)
    logf = jax.nn.log_sigmoid(gates[..., ML_H:] + ml_f_b.astype(jnp.float32))
    h_ml = mlstm_chunkwise(q_ml, k_ml, v_ml, i_pre, logf)
    h_ml = rms_norm_2(h_ml, ml_norm_g)
    h_ml = h_ml * jax.nn.sigmoid(o_ml.astype(jnp.float32).reshape(B, S, ML_H, ML_HD))
    h_ml = h_ml.reshape(B, S, ML_W).astype(h.dtype)
    pos = jnp.arange(S)
    q_at = rope(q_at.reshape(B, S, ATT_H, ATT_HD), pos)
    k_at = rope(kv_at[..., :ATT_KV * ATT_HD].reshape(B, S, ATT_KV, ATT_HD), pos)
    v_at = kv_at[..., ATT_KV * ATT_HD:].astype(jnp.float32).reshape(B, S, ATT_KV, ATT_HD)
    o_at = sliding_window_attention(q_at, k_at, v_at, attn_sinks).reshape(B, S, ATT_W)
    o_at = rms_norm_2(o_at, attn_norm_g).astype(h.dtype)
    return jnp.concatenate([h_ml, o_at], axis=-1) @ w_out

def conv_ffn(h, w_up, conv_w, conv_b, w_down):
    u = causal_dwconv(h @ w_up, conv_w, conv_b)
    g, val = u[..., :D_FF_2], u[..., D_FF_2:]
    return (jax.nn.gelu(g, approximate=True) * val) @ w_down

def second_inputs(seed: int = 0) -> dict:
    key = jax.random.key(seed)
    ks = jax.random.split(key, 24)
    f32 = jnp.float32
    nrm = lambda k, shp, s: jax.random.normal(k, shp, f32) * s
    gain = lambda k, shp: 1.0 + 0.05 * jax.random.normal(k, shp, f32)
    L = DEPTH
    f_bias = jnp.linspace(3.0, 6.0, ML_H, dtype=f32)[None, :] + nrm(ks[7], (L, ML_H), 0.1)
    return {
        "x": nrm(ks[0], (BATCH, SEQ, D_MODEL), 1.0),
        "c": nrm(ks[1], (BATCH, D_MODEL), 1.0),
        "w_ada": nrm(ks[2], (L, D_MODEL, N_MOD * D_MODEL), 0.5 * D_MODEL ** -0.5),
        "b_ada": nrm(ks[3], (L, N_MOD * D_MODEL), 0.02),
        "pre_mix_g": gain(ks[4], (L, D_MODEL)),
        "w_in": nrm(ks[5], (L, D_MODEL, IN_COLS), D_MODEL ** -0.5),
        "ml_conv_w": nrm(ks[6], (L, ML_CONV, 2 * ML_W), ML_CONV ** -0.5),
        "ml_conv_b": nrm(ks[8], (L, 2 * ML_W), 0.02),
        "ml_i_b": nrm(ks[9], (L, ML_H), 0.1),
        "ml_f_b": f_bias,
        "ml_norm_g": gain(ks[10], (L, ML_H, ML_HD)),
        "attn_sinks": nrm(ks[11], (L, ATT_H), 1.0),
        "attn_norm_g": gain(ks[12], (L, ATT_W)),
        "w_out": nrm(ks[13], (L, MIX_W, D_MODEL), MIX_W ** -0.5),
        "post_mix_g": gain(ks[14], (L, D_MODEL)),
        "pre_ffn_g": gain(ks[15], (L, D_MODEL)),
        "w_up": nrm(ks[16], (L, D_MODEL, 2 * D_FF_2), D_MODEL ** -0.5),
        "ffn_conv_w": nrm(ks[17], (L, FFN_CONV, 2 * D_FF_2), FFN_CONV ** -0.5),
        "ffn_conv_b": nrm(ks[18], (L, 2 * D_FF_2), 0.02),
        "w_down": nrm(ks[19], (L, D_FF_2, D_MODEL), D_FF_2 ** -0.5),
        "post_ffn_g": gain(ks[20], (L, D_MODEL)),
    }

def second_block(x, c, w_ada, b_ada, pre_mix_g, w_in, ml_conv_w, ml_conv_b, ml_i_b,
              ml_f_b, ml_norm_g, attn_sinks, attn_norm_g, w_out, post_mix_g,
              pre_ffn_g, w_up, ffn_conv_w, ffn_conv_b, w_down, post_ffn_g):
    c_act = jax.nn.silu(c)
    for l in range(DEPTH):
        mod = c_act @ w_ada[l] + b_ada[l]
        sh1, sc1, g1, sh2, sc2, g2 = [t[:, None, :] for t in jnp.split(mod, N_MOD, axis=-1)]
        h = rms_norm_2(x, pre_mix_g[l]) * (1.0 + sc1) + sh1
        y = token_mixer(h, w_in[l], ml_conv_w[l], ml_conv_b[l], ml_i_b[l], ml_f_b[l],
                        ml_norm_g[l], attn_sinks[l], attn_norm_g[l], w_out[l])
        x = x + g1 * rms_norm_2(y, post_mix_g[l])
        h = rms_norm_2(x, pre_ffn_g[l]) * (1.0 + sc2) + sh2
        y = conv_ffn(h, w_up[l], ffn_conv_w[l], ffn_conv_b[l], w_down[l])
        x = x + g2 * rms_norm_2(y, post_ffn_g[l])
    return x


def setup_inputs(seed=0):
    out = dict(first_inputs(seed))
    for name, value in second_inputs(seed + 1).items():
        if name != "x":
            out[name + "_2"] = value
    return out


def reference(
    x, p, norm_mix, w_in, w_pool, pool_scale, w_branch_a, w_branch_b, w_out, norm_ffn,
    w_ffn_gate, w_ffn_up, w_ffn_down, norm_ple, w_ple_gate, w_ple_proj, norm_final, c_2,
    w_ada_2, b_ada_2, pre_mix_g_2, w_in_2, ml_conv_w_2, ml_conv_b_2, ml_i_b_2, ml_f_b_2,
    ml_norm_g_2, attn_sinks_2, attn_norm_g_2, w_out_2, post_mix_g_2, pre_ffn_g_2, w_up_2,
    ffn_conv_w_2, ffn_conv_b_2, w_down_2, post_ffn_g_2,
):
    x = first_block(
        x, p, norm_mix, w_in, w_pool, pool_scale, w_branch_a, w_branch_b, w_out, norm_ffn,
        w_ffn_gate, w_ffn_up, w_ffn_down, norm_ple, w_ple_gate, w_ple_proj, norm_final,
    )
    return second_block(
        x, c_2, w_ada_2, b_ada_2, pre_mix_g_2, w_in_2, ml_conv_w_2, ml_conv_b_2, ml_i_b_2,
        ml_f_b_2, ml_norm_g_2, attn_sinks_2, attn_norm_g_2, w_out_2, post_mix_g_2, pre_ffn_g_2,
        w_up_2, ffn_conv_w_2, ffn_conv_b_2, w_down_2, post_ffn_g_2,
    )


_drawn_inputs = setup_inputs


def setup_inputs(seed=0):
    import zlib

    import numpy as np

    out = dict(_drawn_inputs(seed))
    spreads = {}
    factors = {'norm_mix': 4.479,
     'pool_scale': 6.354,
     'norm_ffn': 4.471,
     'norm_ple': 200.0,
     'norm_final': 2.759,
     'pre_mix_g_2': 3.991,
     'ml_conv_b_2': 64.0,
     'ml_i_b_2': 200.0,
     'ml_norm_g_2': 24.983,
     'attn_sinks_2': 51.912,
     'attn_norm_g_2': 15.416,
     'post_mix_g_2': 10.343,
     'pre_ffn_g_2': 2.919,
     'ffn_conv_b_2': 7.697,
     'post_ffn_g_2': 11.192}
    for name, (base, spread) in spreads.items():
        noise = np.random.default_rng([zlib.crc32(name.encode()), seed]).standard_normal(out[name].shape)
        drawn = base * np.exp(spread * noise) if base else spread * noise
        out[name] = __import__('jax').numpy.asarray(drawn.astype(out[name].dtype))
    for name, factor in factors.items():
        out[name] = (out[name] * factor).astype(out[name].dtype)
    return out
```

```python
from contextlib import ExitStack

import numpy as np

import concourse.bass as bass
from concourse import mybir

F32 = mybir.dt.float32
F32R = mybir.dt.float32r
BF16 = mybir.dt.bfloat16
ACT = mybir.ActivationFunctionType
ALU = mybir.AluOpType
AX = mybir.AxisListType

P = 128
T = 1024
D = 1024
KD = D // P
NB = T // P
HALF = 512
NH = T // HALF
EPS = 1e-6
NEG = -1e30

D_POOL = 512
WINDOWS = (2, 4, 8, 16)
D_SB = 512
SB_DIM = 64
D_FF = 2816
KF = D_FF // P
PLE = 256

ML_H, ML_D = 4, 128
ML_CONV = 4
AT_H, AT_KV, AT_DIM = 8, 2, 64
FFN_CONV = 3
FFN_GROUP = 2

EXACT_FROM = 16.0

VEC = {}


def _columns():
    at = 0
    for name, n in (
        ("norm_mix", KD), ("norm_ffn", KD), ("norm_ple", KD), ("norm_final", KD), ("pool_scale", 4),
        ("pre_mix_g", KD), ("ml_conv_w", ML_CONV * 8), ("ml_conv_b", 8), ("gate_b", 1), ("ml_norm_g", ML_H),
        ("attn_norm_g", 4), ("post_mix_g", KD), ("pre_ffn_g", KD), ("ffn_conv_w", FFN_CONV * 2 * KF),
        ("ffn_conv_b", 2 * KF), ("post_ffn_g", KD), ("b_ada", 6 * KD), ("c", KD), ("sinks", AT_H),
    ):
        VEC[name] = at
        at += n
    return at


N_VEC = _columns()

CONST = {}
N_CONST = 0
for _name, _n in (("ident", P), ("ones", P), ("minus_tri", P), ("minus_ones", P), ("causal_neg", P),
                  ("band_neg", 2 * P), ("later_neg", P), ("rotate", P), ("inv_count", 4 * 16), ("one", P)):
    CONST[_name] = N_CONST
    N_CONST += _n


def constants():
    p, j = np.arange(P)[:, None], np.arange(P)[None, :]
    table = np.zeros((P, N_CONST), np.float32)

    def put(name, value):
        table[:, CONST[name]:CONST[name] + value.shape[1]] = value

    put("ident", (p == j).astype(np.float32))
    put("ones", np.ones((P, P), np.float32))
    put("minus_tri", -(p >= j).astype(np.float32))
    put("minus_ones", -np.ones((P, P), np.float32))
    put("causal_neg", np.where(p >= j, NEG, 0.0).astype(np.float32))
    k2 = np.arange(2 * P)[None, :]
    put("band_neg", np.where((k2 > p) & (k2 <= p + P), 0.0, NEG).astype(np.float32))
    put("later_neg", np.where(p > j, NEG, 0.0).astype(np.float32))
    half = AT_DIM // 2
    rot = np.zeros((P, P), np.float32)
    for to in range(P):
        d = to % AT_DIM
        rot[to + half if d < half else to - half, to] = -1.0 if d < half else 1.0
    put("rotate", rot)
    counts = np.concatenate([1.0 / np.minimum(np.arange(16) + 1, w) for w in WINDOWS])
    put("inv_count", np.broadcast_to(counts.astype(np.float32), (P, 64)))
    put("one", np.ones((P, P), np.float32))
    inv = (np.float32(10000.0) ** (-np.arange(half, dtype=np.float32) / np.float32(half))).astype(np.float32)
    ang = (np.arange(T, dtype=np.float32)[None, :] * inv[:, None]).astype(np.float32).astype(np.float64)
    cos, sin = np.cos(ang).astype(np.float32), np.sin(ang).astype(np.float32)
    rope = np.concatenate([np.tile(cos, (4, 1)), np.tile(sin, (4, 1))], axis=1)
    return table, np.ascontiguousarray(rope)


class Queue:

    def __init__(self, sem):
        self.sem, self.count, self.steps, self.passed = sem, 0, [], {}

    def wait(self, *tokens):
        for t in tokens:
            if t is None:
                continue
            if isinstance(t, list):
                self.wait(*t)
            elif self.passed.get(id(t[0]), 0) < t[1]:
                self.passed[id(t[0])] = t[1]
                self.steps.append(("wait", t[0], t[1]))

    def do(self, step, *tokens):
        self.wait(*tokens)
        self.steps.append(("do", step, None))

    def mark(self, step, *tokens):
        self.wait(*tokens)
        self.count += 1
        self.steps.append(("do", step, (self.sem, 1)))
        return (self.sem, self.count)

    def now(self):
        return (self.sem, self.count) if self.count else None

    def play(self, engine):
        for kind, a, b in self.steps:
            if kind == "wait":
                engine.wait_ge(a, b)
            else:
                made = a(engine)
                if b is not None:
                    made.then_inc(b[0], b[1])


class Buf:

    def __init__(self, ap, busy=None):
        self.ap, self.ready, self.busy = ap, [], list(busy or [])

    def written(self, *tokens):
        self.ready, self.busy = list(tokens), []

    def used(self, *tokens):
        self.busy += tokens


class Ring:
    def __init__(self, bufs):
        self.bufs, self.at = bufs, 0

    def take(self):
        b = self.bufs[self.at % len(self.bufs)]
        self.at += 1
        return b


def two_blocks(nc, io, stages=99):
    with ExitStack() as ctx:
        def sb_in(scope, name, shape, dt=F32):
            return scope.enter_context(nc.sbuf_tensor(name, shape, dt))

        def sb(name, shape, dt=F32):
            return sb_in(ctx, name, shape, dt)

        def sem(name):
            return ctx.enter_context(nc.semaphore(name))

        sync = Queue(sem("s_sync"))
        act = Queue(sem("s_scalar"))
        dve = Queue(sem("s_vector"))
        pe = Queue(sem("s_tensor"))
        pool = Queue(sem("s_gpsimd"))

        class Dma:

            def __init__(self, name):
                self.sem, self.count = sem(name), 0

            def start(self, queue, out, in_, *tokens):
                queue.wait(*tokens)
                self.count += 16
                queue.steps.append(("do", lambda e: e.dma_start(out, in_), (self.sem, 16)))
                return (self.sem, self.count)

        def fence():
            return [q.now() for q in (act, dve, pe, pool) if q.now()]

        consts = sb("consts", [P, N_CONST])
        vecs = sb("vecs", [P, N_VEC])
        ident_bf = sb("ident_bf", [P, P], BF16)
        causal_bf = sb("causal_bf", [P, P], BF16)
        band_bf = sb("band_bf", [P, 2 * P], BF16)
        mod = sb("mod", [P, 6 * KD])
        gain = sb("gain", [P, 4 * KD])
        w_raw = sb("w_raw", [P, 2, 1024])
        w_hi = sb("w_hi", [P, 2, 1024], F32R)
        w_lo = sb("w_lo", [P, 2, 1024], F32R)
        tmp_mem = sb("tmp_mem", [P, 2, T])
        norm_row = Buf(sb("norm_row", [P, T])[:, :])
        h_hi = sb("h_hi", [P, KD, T], F32R)
        h_lo = sb("h_lo", [P, KD, T], F32R)
        psum_mem = ctx.enter_context(nc.psum_tensor("psum_mem", [P, 8, HALF], F32))

        tmps = Ring([Buf(tmp_mem[:, i, :]) for i in range(2)])
        banks = [Buf(psum_mem[:, b, :]) for b in range(8)]

        class Pair:

            def __init__(self, i):
                self.i = i
                self.ap = psum_mem[:, 2 * i:2 * i + 2, :].rearrange("p a b -> p (a b)")

            @property
            def busy(self):
                return banks[2 * self.i].busy + banks[2 * self.i + 1].busy

            def half(self, n):
                return psum_mem[:, 2 * self.i + n, :]

            def written(self, *tokens):
                for b in (2 * self.i, 2 * self.i + 1):
                    banks[b].written(*tokens)

            @property
            def ready(self):
                return banks[2 * self.i].ready

            def used(self, *tokens):
                for b in (2 * self.i, 2 * self.i + 1):
                    banks[b].used(*tokens)

        pairs = Ring([Pair(i) for i in range(4)])

        def const(name, n=P, rows=P):
            return consts[0:rows, CONST[name]:CONST[name] + n]

        def vec(name, i=0, n=1):
            return vecs[:, VEC[name] + i:VEC[name] + i + n]

        def load(dma, out, in_, *w):
            return dma.start(sync, out, in_, *w)

        def a_act(out, in_, func, *w, bias=0.0, scale=1.0):
            return act.mark(lambda e: e.activation(out, in_, func, bias=bias, scale=scale), *w)

        def a_copy(out, in_, *w):
            return act.mark(lambda e: e.copy(out, in_), *w)

        def v_copy(out, in_, *w):
            return dve.mark(lambda e: e.tensor_copy(out, in_), *w)

        def v_tt(out, a, b, op, *w):
            return dve.mark(lambda e: e.tensor_tensor(out, a, b, op), *w)

        def v_ts(out, a, s1, op0, *w, s2=None, op1=None):
            if op1 is None:
                return dve.mark(lambda e: e.tensor_scalar(out, a, s1, None, op0), *w)
            return dve.mark(lambda e: e.tensor_scalar(out, a, s1, s2, op0, op1), *w)

        def v_stt(out, a, s, b, op0, op1, *w):
            return dve.mark(lambda e: e.scalar_tensor_tensor(out=out, in0=a, scalar=s, in1=b, op0=op0, op1=op1), *w)

        def g_tt(out, a, b, op, *w):
            return pool.mark(lambda e: e.tensor_tensor(out, a, b, op), *w)

        def mm(out, lhsT, rhs, start, stop, *w):
            pe.do(lambda e: e.matmul(out, lhsT, rhs, start=start, stop=stop, skip_group_check=True), *w)

        def mm_mark(out, lhsT, rhs, start, stop, *w):
            return pe.mark(lambda e: e.matmul(out, lhsT, rhs, start=start, stop=stop, skip_group_check=True), *w)

        def transpose(out, in_, *w, rows=P):
            ident = consts[0:rows, CONST["ident"]:CONST["ident"] + rows]
            return pe.mark(lambda e: e.transpose(out, in_, ident), *w)

        def split(hi, lo, src, *w, bias=None):
            if bias is None:
                t_hi = a_copy(hi, src, *w)
                t_lo = v_tt(lo, src, hi.bitcast(F32), ALU.subtract, t_hi)
            else:
                t_hi = a_act(hi, src, ACT.Identity, *w, bias=bias)
                t_lo = v_stt(lo, src, bias, hi.bitcast(F32), ALU.add, ALU.subtract, t_hi)
            return [t_hi, t_lo]

        units = []
        for j in range(4):
            for part in range(3):
                units.append(("w_qkv", io["w_in_a"][4 + 4 * part + j]))
        for g in range(5):
            if g < 4:
                units.append(("w_u", io["w_in_a"][g]))
            if g > 0:
                units.append(("w_pool", io["w_pool"][g - 1]))
        for m in range(KD):
            units.append(("w_ga", io["w_in_a"][16 + m]))
            units.append(("w_gb", io["w_in_a"][24 + m]))
            units.append(("w_ba", io["w_branch_a"][m]))
            units.append(("w_bb", io["w_branch_b"][m]))
        for m in range(KD):
            units.append(("w_out", io["w_out"][m]))
        n_groups = KF // FFN_GROUP

        def ffn_order(names, down):
            order = []
            for g in range(n_groups + 1):
                if g < n_groups:
                    for i in range(g * FFN_GROUP, (g + 1) * FFN_GROUP):
                        for name, source in names:
                            order.append((name, source[i]))
                if g > 0:
                    for m in range(2):
                        order.append(("w_down", down[2 * (g - 1) + m]))
            return order

        units += ffn_order([("w_gate", io["w_ffn_gate"]), ("w_up", io["w_ffn_up"])], io["w_ffn_down"])
        for m in range(KD):
            if m % 4 == 0:
                units.append(("w_pp", io["w_ple_proj"][m // 4]))
            units.append(("w_pg", io["w_ple_gate"][m]))
        for s in range(5):
            units.append(("w_qk_at", io["w_in_b_at"][s]))
        units.append(("w_v_at", io["w_in_b_at"][5]))
        for s in range(16):
            units.append(("w_ml", io["w_in_b_ml"][s]))
        units.append(("w_gates", io["w_in_b_gates"]))
        for m in range(KD):
            units.append(("w_out2", io["w_out_b"][m]))
        units += ffn_order([("w_gate2", io["w_up_b"][0:KF]), ("w_up2", io["w_up_b"][KF:2 * KF])], io["w_down_b"])

        class Weights:
            def __init__(self):
                self.raw = [Buf(w_raw[:, i, :]) for i in range(2)]
                self.dma = [Dma(f"w_load{i}") for i in range(2)]
                self.hi = [Buf(w_hi[:, i, :]) for i in range(2)]
                self.lo = [Buf(w_lo[:, i, :]) for i in range(2)]
                self.loaded = self.cut = self.taken = 0

            def load(self):
                n, i = self.loaded, self.loaded % 2
                if n >= len(units):
                    return
                self.loaded += 1
                width = units[n][1].shape[-1]
                t = load(self.dma[i], self.raw[i].ap[:, 0:width], units[n][1], self.raw[i].busy)
                self.raw[i].written(t)

            def split(self):
                n, i = self.cut, self.cut % 2
                if n >= len(units):
                    return
                self.load()
                self.cut += 1
                width = units[n][1].shape[-1]
                raw, hi, lo = self.raw[i], self.hi[i], self.lo[i]
                t_hi = a_copy(hi.ap[:, 0:width], raw.ap[:, 0:width], raw.ready, hi.busy)
                t_lo = g_tt(lo.ap[:, 0:width], raw.ap[:, 0:width], hi.ap[:, 0:width].bitcast(F32), ALU.subtract,
                            t_hi, raw.ready, lo.busy)
                raw.used(t_hi, t_lo)
                hi.written(t_hi)
                lo.written(t_lo)

            def take(self, name):
                n, i = self.taken, self.taken % 2
                assert units[n][0] == name, (units[n][0], name)
                self.taken += 1
                while self.cut < min(self.taken + 1, len(units)):
                    self.split()
                return self.hi[i], self.lo[i]

        weights = Weights()

        def project_steps(out, unit, blocks, rhs, waits):
            hi, lo = unit
            mark = None
            n = len(blocks)
            for k, b in enumerate(blocks):
                w_h, w_l = hi.ap[:, b * P:(b + 1) * P], lo.ap[:, b * P:(b + 1) * P]
                x_h, x_l, ready = rhs[k]
                for part, (w, x) in enumerate(((w_h, x_h), (w_h, x_l), (w_l, x_h))):
                    for half in range(NH):
                        cols = slice(half * HALF, (half + 1) * HALF)
                        last = k == n - 1 and part == 2
                        args = (out.half(half), w, x[:, cols], k == 0 and part == 0, last,
                                waits, ready, lo.ready if part == 2 else hi.ready)
                        if last and half == NH - 1:
                            mark = mm_mark(*args)
                        else:
                            mm(*args)
                yield
            hi.used(mark)
            lo.used(mark)
            out.written(mark)

        def one(name, rhs, blocks=tuple(range(KD)), unit=None):
            out = pairs.take()
            unit = unit or weights.take(name)
            for _ in project_steps(out, unit, blocks, rhs, out.busy):
                pass
            return out, out.ready[0]

        dma_const, dma_vec = Dma("dma_const"), Dma("dma_vec")
        t_const = load(dma_const, consts[:, :], io["consts"])
        t_vec = load(dma_vec, vecs[:, :], io["vecs"])
        dma_x = [Dma(f"dma_x{k}") for k in range(KD)]
        out_dma = Dma("dma_out")
        dma_misc = Dma("dma_misc")
        t_ib = v_copy(ident_bf[:, :], const("ident"), t_const)
        t_cb = v_copy(causal_bf[:, :], const("causal_neg"), t_const)
        t_bb = v_copy(band_bf[:, :], const("band_neg", 2 * P), t_const)
        for q in (pe, act, dve, pool):
            q.wait(t_const, t_vec)
        pe.wait(t_ib, t_cb, t_bb)

        h_busy = [[] for _ in range(KD)]
        h_ready = [[] for _ in range(KD)]

        def h_rhs(ks=range(KD)):
            return [(h_hi[:, k, :], h_lo[:, k, :], h_ready[k]) for k in ks]

        def h_used(mark):
            for k in range(KD):
                h_busy[k].append(mark)

        def inverse_rms(chunks):
            row = norm_row
            total = None
            for k, c in enumerate(chunks):
                if k == 0:
                    total = a_act(row.ap, c.ap, ACT.Square, c.ready, row.busy)
                    c.used(total)
                    continue
                t = tmps.take()
                t_sq = a_act(t.ap, c.ap, ACT.Square, c.ready, t.busy)
                c.used(t_sq)
                total = v_tt(row.ap, row.ap, t.ap, ALU.add, total, t_sq)
                t.written(t_sq)
                t.used(total)
            out = pairs.take()
            mark = None
            for half in range(NH):
                cols = slice(half * HALF, (half + 1) * HALF)
                mark = mm_mark(out.half(half), const("ones"), row.ap[:, cols], True, True, total, out.busy)
            out.written(mark)
            t_std = a_act(row.ap, out.ap, ACT.Sqrt, mark, bias=eps_col[:, :], scale=1.0 / D)
            out.used(t_std)
            t_inv = dve.mark(lambda e: e.reciprocal(row.ap, row.ap), t_std)
            row.written(t_inv)

        eps_col = sb("eps_col", [P, 1])
        t_eps = dve.mark(lambda e: e.memset(eps_col[:, :], EPS))
        act.wait(t_eps)

        def normed_to_h(chunks, gains, shifts=None):
            for k, c in enumerate(chunks):
                t = tmps.take()
                t_h = v_stt(t.ap, c.ap, gains(k), norm_row.ap, ALU.mult, ALU.mult, c.ready, norm_row.ready, t.busy)
                c.used(t_h)
                t.written(t_h)
                made = split(h_hi[:, k, :], h_lo[:, k, :], t.ap, t_h, h_busy[k],
                             bias=None if shifts is None else shifts(k))
                t.used(*made)
                h_ready[k], h_busy[k] = made, []
                norm_row.used(t_h)

        def load_x(scope, name, source, busy):
            mem = sb_in(scope, name, [P, KD, T])
            chunks = []
            for k in range(KD):
                c = Buf(mem[:, k, :])
                c.written(load(dma_x[k], c.ap, source[k], busy))
                chunks.append(c)
            return chunks

        def finish(chunks):
            for k, c in enumerate(chunks):
                t = out_dma.start(sync, io["out"][k], c.ap, c.ready)
            sync.wait(t)

        scope = ExitStack()
        x = load_x(scope, "x_first", io["x"], None)
        inverse_rms(x)
        normed_to_h(x, lambda k: vec("norm_mix", k))
        scope.close()

        outer = ExitStack()
        yb_hi = sb_in(outer, "yb_hi", [P, 4, T], F32R)
        yb_lo = sb_in(outer, "yb_lo", [P, 4, T], F32R)
        attn = ExitStack()
        free = fence()
        act.wait(free)
        dve.wait(free)
        pool.wait(free)
        pads = [[Buf(sb_in(attn, f"q_pad{i}{par}", [P, T])[:, :]) for par in range(2)] for i in range(2)]
        k_feat = [Buf(sb_in(attn, f"k_feat{i}", [P, T])[:, :]) for i in range(2)]
        v_tok = [Buf(sb_in(attn, f"v_tok{i}", [P, T])[:, :]) for i in range(2)]
        pad_zero = []
        for side in pads:
            for par in range(2):
                other = slice(64, 128) if par == 0 else slice(0, 64)
                pad_zero.append(dve.mark((lambda o: lambda e: e.memset(o, 0.0))(side[par].ap[other, :])))
        pe.wait(pad_zero)
        proj_pair = Pair(3)

        def head_rows(par):
            return slice(64 * par, 64 * par + 64)

        def qkv_steps(j):
            side = j % 2
            for part in range(3):
                unit = weights.take("w_qkv")
                yield from project_steps(proj_pair, unit, tuple(range(KD)), h_rhs(), proj_pair.busy)
                mark = proj_pair.ready
                h_used(mark[0])
                if part == 0:
                    done = []
                    for par in range(2):
                        rows, pad = head_rows(par), pads[side][par]
                        t = a_act(pad.ap[rows, :], proj_pair.ap[rows, :], ACT.Copy, mark, pad.busy,
                                  scale=SB_DIM ** -0.5)
                        pad.written(t)
                        done.append(t)
                    proj_pair.used(*done)
                elif part == 1:
                    t = a_copy(k_feat[side].ap, proj_pair.ap, mark, k_feat[side].busy)
                    proj_pair.used(t)
                    k_feat[side].written(t)
                else:
                    v_t, v = tmps.take(), v_tok[side]
                    t = a_copy(v_t.ap, proj_pair.ap, mark, v_t.busy)
                    proj_pair.used(t)
                    v_t.written(t)
                    yield
                    for b in range(NB):
                        mark = transpose(proj_pair.ap[:, b * P:(b + 1) * P], v_t.ap[:, b * P:(b + 1) * P], t,
                                         proj_pair.busy)
                    v_t.used(mark)
                    proj_pair.written(mark)
                    t = a_copy(v.ap, proj_pair.ap, mark, v.busy)
                    proj_pair.used(t)
                    v.written(t)

        e_ring = Ring([Buf(sb_in(attn, f"e_tile{i}", [P, HALF])[:, :]) for i in range(3)])
        sp_ring = Ring([Buf(sb_in(attn, f"sp_tile{i}", [P, HALF])[:, :]) for i in range(3)])
        a_ring = Ring([Buf(sb_in(attn, f"a_tile{i}", [P, HALF])[:, :]) for i in range(3)])
        acc = [[Buf(sb_in(attn, f"acc{par}{i}", [P, HALF])[:, :]) for i in range(2)] for par in range(2)]
        zbanks = Ring([banks[i] for i in range(4)])
        yb_split = [[] for _ in range(4)]
        act.do(lambda e: e.preload_act_table_set("natural_log_exp_and_others"))

        def score(tile):
            j, par, g, kb, c0, n = tile["at"]
            z = tile["z"] = zbanks.take()
            pad, k = pads[j % 2][par], k_feat[j % 2]
            mark = mm_mark(z.ap[:, 0:n], k.ap[:, kb * P:(kb + 1) * P],
                           pad.ap[:, g * HALF + c0:(g + 1) * HALF], True, not tile["diag"],
                           z.busy, pad.ready, k.ready)
            if tile["diag"]:
                mark = mm_mark(z.ap[:, 0:P], ident_bf[:, :], causal_bf[:, :], False, True)
            pad.used(mark)
            k.used(mark)
            z.written(mark)

        def softplus(tile):
            n, z = tile["at"][5], tile["z"]
            e_t, sp_t = e_ring.take(), sp_ring.take()
            tile["sp"] = sp_t
            t1 = v_ts(e_t.ap[:, 0:n], z.ap[:, 0:n], EXACT_FROM, ALU.min, z.ready, e_t.busy)
            t2 = a_act(e_t.ap[:, 0:n], e_t.ap[:, 0:n], ACT.Exp, t1)
            t3 = a_act(e_t.ap[:, 0:n], e_t.ap[:, 0:n], ACT.Ln, t2, bias=1.0)
            tile["ln"] = (e_t, t3)

        def softplus_end(tile):
            n, z, sp_t = tile["at"][5], tile["z"], tile["sp"]
            e_t, t3 = tile["ln"]
            t4 = v_tt(sp_t.ap[:, 0:n], e_t.ap[:, 0:n], z.ap[:, 0:n], ALU.max, t3, sp_t.busy)
            e_t.written(t3)
            e_t.used(t4)
            sp_t.written(t4)
            z.ready = [t4]

        def sums(tile):
            j, par, g, kb, c0, n = tile["at"]
            z, sp_t = tile["z"], tile["sp"]
            old, new = acc[par]
            first = kb == 4 * g + 3
            wide = P if tile["diag"] else 0
            mark = mm_mark(z.ap[:, 0:n], const("minus_tri"), sp_t.ap[:, 0:n], False, first, sp_t.ready, z.ready)
            if not first:
                mark = mm_mark(z.ap[:, wide:n], const("minus_ones"), old.ap[:, c0 + wide:HALF], False, True, old.ready)
                old.used(mark)
            sp_t.used(mark)
            z.written(mark)
            if kb > 0:
                tokens = []
                if wide:
                    tokens.append(pool.mark(
                        lambda e: e.tensor_copy(new.ap[:, c0:c0 + P], sp_t.ap[:, 0:P]), sp_t.ready, new.busy))
                if not first:
                    tokens.append(g_tt(new.ap[:, c0 + wide:HALF], old.ap[:, c0 + wide:HALF], sp_t.ap[:, wide:n],
                                       ALU.add, sp_t.ready, old.ready, new.busy))
                    old.used(tokens[-1])
                sp_t.used(*tokens)
                new.written(*tokens)
                acc[par] = [new, old]

        def weigh(tile):
            n, z = tile["at"][5], tile["z"]
            a_t = tile["a"] = a_ring.take()
            t = a_act(a_t.ap[:, 0:n], z.ap[:, 0:n], ACT.Exp, z.ready, a_t.busy)
            z.used(t)
            a_t.written(t)

        def mix(tile):
            j, par, g, kb, c0, n = tile["at"]
            a_t, o, v = tile["a"], banks[4 + par], v_tok[j % 2]
            mark = mm_mark(o.ap[:, c0:HALF], v.ap[:, kb * P:(kb + 1) * P], a_t.ap[:, 0:n],
                           kb == 4 * g + 3, kb == 0, a_t.ready, v.ready, o.busy if kb == 4 * g + 3 else None)
            a_t.used(mark)
            v.used(mark)
            if kb == 0:
                o.written(mark)
                rows, cols = head_rows(par), slice(g * HALF, (g + 1) * HALF)
                made = split(yb_hi[rows, j, cols], yb_lo[rows, j, cols], o.ap[rows, :], mark)
                o.used(*made)
                yb_split[j] += made

        tiles = []
        for j in range(4):
            for g in range(NH):
                for kb in range(4 * g + 3, -1, -1):
                    for par in range(2):
                        c0 = max(0, kb - 4 * g) * P
                        tiles.append({"at": (j, par, g, kb, c0, HALF - c0), "diag": kb >= 4 * g})
        for _ in qkv_steps(0):
            pass
        filler = iter(())
        for i in range(len(tiles) + 4):
            if i < len(tiles):
                if i % (len(tiles) // 4) == 0:
                    for _ in filler:
                        pass
                    j = tiles[i]["at"][0]
                    filler = qkv_steps(j + 1) if j < 3 else iter(())
                score(tiles[i])
                softplus(tiles[i])
                next(filler, None)
            if 0 <= i - 1 < len(tiles):
                softplus_end(tiles[i - 1])
            if 0 <= i - 2 < len(tiles):
                sums(tiles[i - 2])
                weigh(tiles[i - 2])
            if 0 <= i - 4 < len(tiles):
                mix(tiles[i - 4])
        attn.close()

        free = fence()
        for q in (act, dve, pool):
            q.wait(free)
        ya_hi = sb_in(outer, "ya_hi", [P, 4, T], F32R)
        ya_lo = sb_in(outer, "ya_lo", [P, 4, T], F32R)
        pool_scope = ExitStack()
        PAD = 16
        u_mem = [sb_in(pool_scope, f"u_mem{i}", [P, PAD + T]) for i in range(3)]
        pl_hi = [Buf(sb_in(pool_scope, f"pl_hi{i}", [P, T], F32R)[:, :]) for i in range(2)]
        pl_lo = [Buf(sb_in(pool_scope, f"pl_lo{i}", [P, T], F32R)[:, :]) for i in range(2)]
        t_zero = [dve.mark((lambda o: lambda e: e.memset(o, 0.0))(u[:, 0:PAD])) for u in u_mem]
        u_busy = []
        ya_ready = []

        def map_group(g):
            hi, lo = pl_hi[g % 2], pl_lo[g % 2]
            ps, mark = one("w_pool", [(hi.ap, lo.ap, [hi.ready, lo.ready])], (0,))
            hi.used(mark)
            lo.used(mark)
            s = tmps.take()
            t = v_ts(s.ap, ps.ap, vec("pool_scale", g), ALU.mult, mark, s.busy)
            ps.used(t)
            s.written(t)
            made = split(ya_hi[:, g, :], ya_lo[:, g, :], s.ap, t)
            s.used(*made)
            ya_ready.append(made)

        for g, window in enumerate(WINDOWS):
            ps, mark = one("w_u", h_rhs())
            h_used(mark)
            u, a, b = u_mem
            t = a_copy(u[:, PAD:], ps.ap, mark, u_busy)
            ps.used(t)
            src, width = u, 1
            dst = a
            t = v_tt(dst[:, PAD:], src[:, PAD:], src[:, PAD - 1:PAD - 1 + T], ALU.add, t, t_zero)
            width = 2
            while width < window:
                src, dst = dst, (b if dst is a else a)
                t = v_tt(dst[:, PAD:], src[:, PAD:], src[:, PAD - width:PAD - width + T], ALU.add, t)
                width *= 2
            s = tmps.take()
            t1 = v_ts(s.ap, dst[:, PAD:], 1.0 / window, ALU.mult, t, s.busy)
            t1 = v_tt(s.ap[:, 0:window], dst[:, PAD:PAD + window],
                      consts[:, CONST["inv_count"] + 16 * g:CONST["inv_count"] + 16 * g + window], ALU.mult, t1)
            t1 = v_tt(s.ap, s.ap, u[:, PAD:], ALU.subtract, t1)
            s.written(t1)
            hi, lo = pl_hi[g % 2], pl_lo[g % 2]
            made = split(hi.ap, lo.ap, s.ap, t1, hi.busy, lo.busy)
            s.used(*made)
            hi.written(made[0])
            lo.written(made[1])
            u_busy = made
            if g > 0:
                map_group(g - 1)
        map_group(3)
        pool_scope.close()

        free = fence()
        act.wait(free)
        dve.wait(free)
        merged = sb_in(outer, "merged", [P, KD, T])
        merged_ready = []
        rhs_a = [(ya_hi[:, k, :], ya_lo[:, k, :], ya_ready[k]) for k in range(4)]
        rhs_b = [(yb_hi[:, k, :], yb_lo[:, k, :], yb_split[k]) for k in range(4)]
        for m in range(KD):
            gates = []
            for gate in ("w_ga", "w_gb"):
                ps, mark = one(gate, h_rhs())
                h_used(mark)
                g = tmps.take()
                t = a_act(g.ap, ps.ap, ACT.Sigmoid, mark, g.busy)
                ps.used(t)
                g.written(t)
                gates.append(g)
            g_a, g_b = gates
            ps, mark = one("w_ba", rhs_a, tuple(range(4)))
            t = v_tt(merged[:, m, :], g_a.ap, ps.ap, ALU.mult, mark, g_a.ready)
            ps.used(t)
            g_a.used(t)
            ps, mark = one("w_bb", rhs_b, tuple(range(4)))
            t2 = v_tt(g_b.ap, g_b.ap, ps.ap, ALU.mult, mark, g_b.ready)
            ps.used(t2)
            t3 = v_tt(merged[:, m, :], merged[:, m, :], g_b.ap, ALU.add, t, t2)
            g_b.used(t3)
            merged_ready.append(t3)

        for k in range(KD):
            made = split(h_hi[:, k, :], h_lo[:, k, :], merged[:, k, :], merged_ready[k], h_busy[k])
            h_ready[k], h_busy[k] = made, []
        outer.close()
        free = fence()
        resident = ExitStack()
        x = load_x(resident, "x_block1", io["x"], free)

        def add_projected(name, rhs, n_out, blocks=tuple(range(KD)), use_h=True):
            for m in range(n_out):
                ps, mark = one(name, rhs, blocks)
                if use_h:
                    h_used(mark)
                t = v_tt(x[m].ap, x[m].ap, ps.ap, ALU.add, mark, x[m].ready, x[m].busy)
                ps.used(t)
                x[m].written(t)

        add_projected("w_out", h_rhs(), KD)
        if stages == 1:
            finish(x)
            resident.close()
            return play(nc, sync, act, dve, pe, pool)

        inverse_rms(x)
        normed_to_h(x, lambda k: vec("norm_ffn", k))

        def feed_forward(names, activate, add):
            with ExitStack() as s:
                hid_hi = [sb_in(s, f"hid_hi_{names[0]}{i}", [P, FFN_GROUP, T], F32R) for i in range(2)]
                hid_lo = [sb_in(s, f"hid_lo_{names[0]}{i}", [P, FFN_GROUP, T], F32R) for i in range(2)]
                free = fence()
                act.wait(free)
                dve.wait(free)
                ready = [[None] * FFN_GROUP for _ in range(2)]
                busy = [[], []]
                for g in range(n_groups + 1):
                    if g < n_groups:
                        side = g % 2
                        for i in range(FFN_GROUP):
                            t = activate(g * FFN_GROUP + i)
                            made = split(hid_hi[side][:, i, :], hid_lo[side][:, i, :], t.ap, t.ready, busy[side])
                            t.used(*made)
                            ready[side][i] = made
                    if g > 0:
                        side = (g - 1) % 2
                        rhs = [(hid_hi[side][:, i, :], hid_lo[side][:, i, :], ready[side][i])
                               for i in range(FFN_GROUP)]
                        for half in range(2):
                            unit = weights.take("w_down")
                            for mi in range(4):
                                m = 4 * half + mi
                                ps, mark = one("w_down", rhs, tuple(mi * FFN_GROUP + i for i in range(FFN_GROUP)), unit)
                                add(g - 1, m, ps, mark)
                        busy[side] = [mark]

        def gated_chunk(i):
            ps, mark = one("w_gate", h_rhs())
            h_used(mark)
            s = tmps.take()
            t = a_act(s.ap, ps.ap, ACT.Silu, mark, s.busy)
            ps.used(t)
            ps, mark = one("w_up", h_rhs())
            h_used(mark)
            t = v_tt(s.ap, s.ap, ps.ap, ALU.mult, mark, t)
            ps.used(t)
            s.written(t)
            return s

        def add_to_x(g, m, ps, mark):
            t = v_tt(x[m].ap, x[m].ap, ps.ap, ALU.add, mark, x[m].ready, x[m].busy)
            ps.used(t)
            x[m].written(t)

        feed_forward(("a",), gated_chunk, add_to_x)
        if stages == 2:
            finish(x)
            resident.close()
            return play(nc, sync, act, dve, pe, pool)

        ple = ExitStack()
        p_raw = sb_in(ple, "p_raw", [P, 2, T])
        p_hi = sb_in(ple, "p_hi", [P, 2, T], F32R)
        p_lo = sb_in(ple, "p_lo", [P, 2, T], F32R)
        free = fence()
        act.wait(free)
        dve.wait(free)
        p_ready = []
        for k in range(2):
            t = load(Dma(f"dma_p{k}"), p_raw[:, k, :], io["p"][k], free)
            p_ready.append(split(p_hi[:, k, :], p_lo[:, k, :], p_raw[:, k, :], t))
        rhs_p = [(p_hi[:, k, :], p_lo[:, k, :], p_ready[k]) for k in range(2)]
        inverse_rms(x)
        normed_to_h(x, lambda k: vec("norm_ple", k))
        emb = [Buf(sb_in(ple, f"emb{i}", [P, T])[:, :]) for i in range(4)]
        for m in range(KD):
            if m % 4 == 0:
                unit = weights.take("w_pp")
                for mi in range(4):
                    ps, mark = one("w_pp", rhs_p, (2 * mi, 2 * mi + 1), unit)
                    t = a_copy(emb[mi].ap, ps.ap, mark, emb[mi].busy)
                    ps.used(t)
                    emb[mi].written(t)
            ps, mark = one("w_pg", h_rhs())
            h_used(mark)
            s = tmps.take()
            t = a_act(s.ap, ps.ap, ACT.Sigmoid, mark, s.busy)
            ps.used(t)
            t = v_tt(s.ap, s.ap, emb[m % 4].ap, ALU.mult, t, emb[m % 4].ready)
            emb[m % 4].used(t)
            t2 = v_tt(x[m].ap, x[m].ap, s.ap, ALU.add, t, x[m].ready, x[m].busy)
            s.written(t)
            s.used(t2)
            x[m].written(t2)
        ple.close()
        if stages == 3:
            finish(x)
            resident.close()
            return play(nc, sync, act, dve, pe, pool)

        inverse_rms(x)
        for k in range(KD):
            t = v_stt(x[k].ap, x[k].ap, vec("norm_final", k), norm_row.ap, ALU.mult, ALU.mult,
                      x[k].ready, x[k].busy, norm_row.ready)
            x[k].written(t)
            norm_row.used(t)

        ada = ExitStack()
        ada_raw = [Buf(sb_in(ada, f"ada_raw{i}", [P, 2 * 1024])[:, :], fence()) for i in range(3)]
        ada_dma = [Dma(f"ada_dma{i}") for i in range(3)]
        c_silu = sb_in(ada, "c_silu", [P, KD])
        t_c = a_act(c_silu[:, :], vec("c", 0, KD), ACT.Silu, fence())
        ada_bank = banks[7]
        for n in range(3 * KD):
            raw = ada_raw[n % 3]
            t = load(ada_dma[n % 3], raw.ap.rearrange("p (m q) -> p m q", m=2),
                     io["w_ada"][2 * n:2 * n + 2].rearrange("m p q -> p m q"), raw.busy)
            raw.written(t)
            for mi in range(2):
                for k in range(KD):
                    mark = mm_mark(ada_bank.ap[:, 2 * n + mi:2 * n + mi + 1],
                                   raw.ap[:, mi * 1024 + k * P:mi * 1024 + (k + 1) * P],
                                   c_silu[:, k:k + 1], k == 0, k == KD - 1, t, t_c, ada_bank.busy)
            raw.used(mark)
        ada_bank.written(mark)
        t_mod = v_tt(mod[:, :], ada_bank.ap[:, 0:6 * KD], vec("b_ada", 0, 6 * KD), ALU.add, mark)
        ada_bank.used(t_mod)
        ada.close()
        t = v_stt(gain[:, 0:KD], mod[:, KD:2 * KD], 1.0, vec("pre_mix_g", 0, KD), ALU.add, ALU.mult, t_mod)
        t = v_tt(gain[:, KD:2 * KD], mod[:, 2 * KD:3 * KD], vec("post_mix_g", 0, KD), ALU.mult, t_mod)
        t = v_stt(gain[:, 2 * KD:3 * KD], mod[:, 4 * KD:5 * KD], 1.0, vec("pre_ffn_g", 0, KD), ALU.add, ALU.mult, t_mod)
        t = v_tt(gain[:, 3 * KD:4 * KD], mod[:, 5 * KD:6 * KD], vec("post_ffn_g", 0, KD), ALU.mult, t_mod)
        act.wait(t, t_mod)
        dve.wait(t)

        inverse_rms(x)
        normed_to_h(x, lambda k: gain[:, k:k + 1], lambda k: mod[:, k:k + 1])

        def park(chunks):
            done = []
            for k, c in enumerate(chunks):
                t = dma_x[k].start(sync, io["x_park"][k], c.ap, c.ready)
                c.used(t)
                done.append(t)
            return done

        if stages == 4:
            finish(x)
            resident.close()
            return play(nc, sync, act, dve, pe, pool)
        parked = park(x)
        resident.close()
        mixer = ExitStack()
        o_at = sb_in(mixer, "o_at", [P, 4, T])
        at = ExitStack()
        free = fence() + parked
        for q in (act, dve, pool):
            q.wait(free)
        rope_mem = sb_in(at, "rope_mem", [P, 2 * T])
        dma_rope = Dma("dma_rope")
        t_rope = load(dma_rope, rope_mem[:, :], io["rope"], free)
        q_at = [Buf(sb_in(at, f"q_at{i}", [P, T])[:, :]) for i in range(4)]
        k_pad = [[Buf(sb_in(at, f"k_pad{g}{par}", [P, T])[:, :]) for par in range(2)] for g in range(AT_KV)]
        v_at = Buf(sb_in(at, "v_at", [P, T])[:, :])
        plain = Ring([Buf(sb_in(at, f"rope_in{i}", [P, T])[:, :]) for i in range(1)])
        pairs4 = pairs
        for s in range(5):
            ps, mark = one("w_qk_at", h_rhs())
            h_used(mark)
            raw = plain.take()
            t = a_copy(raw.ap, ps.ap, mark, raw.busy)
            ps.used(t)
            raw.written(t)
            rot = pairs.take()
            for half in range(NH):
                cols = slice(half * HALF, (half + 1) * HALF)
                mark = mm_mark(rot.half(half), const("rotate"), raw.ap[:, cols], True, True, t, rot.busy)
            rot.written(mark)
            w = tmps.take()
            t_s = v_tt(w.ap, rot.ap, rope_mem[:, T:2 * T], ALU.mult, mark, t_rope, w.busy)
            rot.used(t_s)
            t_c = v_tt(raw.ap, raw.ap, rope_mem[:, 0:T], ALU.mult, mark, t)
            if s < 4:
                t = v_tt(q_at[s].ap, raw.ap, w.ap, ALU.add, t_s, t_c)
                q_at[s].written(t)
            else:
                t = v_tt(w.ap, raw.ap, w.ap, ALU.add, t_s, t_c)
                for g in range(AT_KV):
                    for par in range(2):
                        rows, other = head_rows(par), head_rows(1 - par)
                        pad = k_pad[g][par]
                        t0 = dve.mark((lambda o: lambda e: e.memset(o, 0.0))(pad.ap[other, :]))
                        t1 = v_copy(pad.ap[rows, :], w.ap[head_rows(g), :], t)
                        pad.written(t0, t1)
                t = t1
            raw.written()
            raw.used(t)
            w.written(t_s)
            w.used(t)

        def turn_to_tokens(ps, mark, write):
            f = tmps.take()
            t = a_copy(f.ap, ps.ap, mark, f.busy)
            ps.used(t)
            f.written(t)
            turned = pairs.take()
            for b in range(NB):
                mark = transpose(turned.ap[:, b * P:(b + 1) * P], f.ap[:, b * P:(b + 1) * P], t, turned.busy)
            f.used(mark)
            turned.written(mark)
            t = write(turned.ap.rearrange("p (b d) -> p b d", b=NB), mark)
            turned.used(t)
            return t

        ps, mark = one("w_v_at", h_rhs())
        h_used(mark)
        v_at.written(turn_to_tokens(ps, mark, lambda ap, m: a_copy(v_at.ap.rearrange("p (b d) -> p b d", b=NB), ap, m)))

        at_scale = AT_DIM ** -0.5
        prob = [Buf(sb_in(at, f"prob{i}", [P, 2 * P])[:, :]) for i in range(AT_H)]
        prob_t = Ring([Buf(sb_in(at, f"prob_t{i}", [P, 4 * P])[:, :]) for i in range(2)])
        small = sb_in(at, "at_small", [P, 8 * AT_H])
        o_tok = Buf(sb_in(at, "o_tok", [P, D_SB])[:, :])
        sq_tok = Buf(sb_in(at, "sq_tok", [P, D_SB])[:, :])

        def col8(i):
            return small[:, i * AT_H:(i + 1) * AT_H]

        row_max, neg_max, row_sum, sink_e, den, ssq, inv = (col8(i) for i in range(7))
        o_at_ready = []
        t_prev = fence()
        for n in range(NB):
            first = P if n == 0 else 0
            k0 = (n - 1) * P + first
            width = 2 * P - first
            for h in range(AT_H):
                bank, off = banks[h // 2], (h % 2) * 2 * P
                g, par = h // (AT_H // AT_KV), h % 2
                pad = k_pad[g][par]
                s_ap = bank.ap[:, off:off + width]
                mm(s_ap, q_at[h // 2].ap[:, n * P:(n + 1) * P], pad.ap[:, k0:k0 + width], True, False,
                   q_at[h // 2].ready, pad.ready, bank.busy)
                mark = mm_mark(s_ap, ident_bf[:, :], band_bf[:, first:2 * P], False, True)
                if h % 2:
                    bank.written(mark)
            ts = []
            for b in range(4):
                s_ap = banks[b].ap.rearrange("p (a c) -> p a c", a=2)[:, :, 0:width]
                ts.append(dve.mark((lambda o, i: lambda e: e.tensor_reduce(o, i, AX.X, ALU.max))(
                    row_max[:, 2 * b:2 * b + 2], s_ap), banks[b].ready, t_prev))
                banks[b].ready = [ts[-1]]
            t = v_stt(neg_max, row_max, at_scale, vec("sinks", 0, AT_H), ALU.mult, ALU.max, ts)
            t_sk = v_tt(sink_e, vec("sinks", 0, AT_H), neg_max, ALU.subtract, t)
            t_m = v_ts(neg_max, neg_max, -1.0, ALU.mult, t, t_sk)
            t_sk = a_act(sink_e, sink_e, ACT.Exp, t_sk)
            exps = []
            for h in range(AT_H):
                bank, off = banks[h // 2], (h % 2) * 2 * P
                pr = prob[h]
                t = act.mark((lambda o, i, b, a: lambda e: e.activation(o, i, ACT.Exp, bias=b, scale=at_scale,
                                                                         accum_out=a))(
                    pr.ap[:, 0:width], bank.ap[:, off:off + width], neg_max[:, h:h + 1], row_sum[:, h:h + 1]),
                    bank.ready, t_m, pr.busy)
                bank.used(t)
                pr.written(t)
                exps.append(t)
            o_bank = banks[6]
            for hp in range(AT_H // 2):
                bank, pt = banks[4 + hp % 2], prob_t.take()
                for hh in range(2):
                    pr = prob[2 * hp + hh]
                    for kb in range(width // P):
                        mark = transpose(bank.ap[:, hh * 2 * P + kb * P:hh * 2 * P + (kb + 1) * P],
                                         pr.ap[:, kb * P:(kb + 1) * P], pr.ready, bank.busy)
                    pr.used(mark)
                bank.written(mark)
                i3, o3 = (x_.rearrange("p (a c) -> p a c", a=2)[:, :, 0:width] for x_ in (bank.ap, pt.ap))
                t = (a_copy if hp % 2 else v_copy)(o3, i3, mark, pt.busy)
                bank.used(t)
                pt.written(t)
                for hh in range(2):
                    h = 2 * hp + hh
                    g = h // (AT_H // AT_KV)
                    kbs = range(width // P)
                    for kb in kbs:
                        vb = (k0 // P + kb) * P + g * AT_DIM
                        mark = mm_mark(o_bank.ap[:, h * AT_DIM:(h + 1) * AT_DIM],
                                       pt.ap[:, hh * 2 * P + kb * P:hh * 2 * P + (kb + 1) * P],
                                       v_at.ap[:, vb:vb + AT_DIM], kb == 0, kb == kbs[-1], t, v_at.ready,
                                       o_bank.busy)
                pt.used(mark)
            o_bank.written(mark)
            t = v_tt(den, row_sum, sink_e, ALU.add, exps, t_sk)
            t = dve.mark(lambda e: e.reciprocal(den, den), t)
            t_o = v_tt(o_tok.ap.rearrange("p (h d) -> p h d", h=AT_H), o_bank.ap.rearrange("p (h d) -> p h d", h=AT_H),
                       den.unsqueeze(2).to_broadcast([P, AT_H, AT_DIM]), ALU.mult, t, mark, o_tok.busy)
            o_bank.used(t_o)
            t = act.mark(lambda e: e.activation(sq_tok.ap, o_tok.ap, ACT.Square, accum_out=ssq[:, 0:1]),
                         t_o, sq_tok.busy)
            sq_tok.written(t)
            t = a_act(inv[:, 0:1], ssq[:, 0:1], ACT.Ln, t, bias=eps_col[:, :], scale=1.0 / D_SB)
            t = a_act(inv[:, 0:1], inv[:, 0:1], ACT.Exp, t, scale=-0.5)
            t = v_ts(o_tok.ap, o_tok.ap, inv[:, 0:1], ALU.mult, t)
            o_tok.written(t)
            t_prev = [t]
            bank = banks[7]
            for j in range(4):
                mark = transpose(bank.ap[:, j * P:(j + 1) * P], o_tok.ap[:, j * P:(j + 1) * P], t, bank.busy)
            o_tok.used(mark)
            bank.written(mark)
            for j in range(4):
                t = v_ts(o_at[:, j, n * P:(n + 1) * P], bank.ap[:, j * P:(j + 1) * P], vec("attn_norm_g", j),
                         ALU.mult, mark)
                o_at_ready.append(t)
            bank.used(t)
        at.close()

        free = fence()
        for q in (act, dve, pool):
            q.wait(free)
        ml = ExitStack()
        conv = ExitStack()
        q_ml = [Buf(sb_in(ml, f"q_ml{i}", [P, T])[:, :]) for i in range(ML_H)]
        k_ml = [Buf(sb_in(ml, f"k_ml{i}", [P, T])[:, :]) for i in range(ML_H)]
        sig_o = [Buf(sb_in(ml, f"sig_o{i}", [P, T])[:, :]) for i in range(ML_H)]
        W1 = ML_D + 1
        v_ml = sb_in(ml, "v_ml", [P, NB, ML_H, W1])
        cols = sb_in(ml, "gate_cols", [P, 4, 32])
        decay = sb_in(ml, "decay", [P, 32])
        CP = ML_CONV - 1
        conv_in = Ring([Buf(sb_in(conv, f"conv_in{i}", [P, CP + T])[:, :]) for i in range(2)])
        for b in conv_in.bufs:
            b.zero = dve.mark((lambda o: lambda e: e.memset(o, 0.0))(b.ap[:, 0:CP]))
        t_ones = pool.mark(lambda e: e.memset(v_ml[:, :, :, ML_D:W1], 1.0))
        v_ml_ready = [t_ones]

        def conv_taps(src, dst, taps, weight, bias, *w):
            t = v_ts(dst.ap, src.ap[:, 0:T], weight(0), ALU.mult, *w, s2=bias, op1=ALU.add)
            for i in range(1, taps):
                t = v_stt(dst.ap, src.ap[:, i:i + T], weight(i), dst.ap, ALU.mult, ALU.add, t)
            return t

        for s in range(16):
            ps, mark = one("w_ml", h_rhs())
            h_used(mark)
            if s < 8:
                src, acc_ = conv_in.take(), tmps.take()
                t = a_copy(src.ap[:, CP:], ps.ap, mark, src.busy)
                ps.used(t)
                t1 = conv_taps(src, acc_, ML_CONV, lambda i: vec("ml_conv_w", 8 * i + s), vec("ml_conv_b", s),
                               t, src.zero, acc_.busy)
                src.written(t)
                src.used(t1)
                out = q_ml[s] if s < 4 else k_ml[s - 4]
                t = a_act(out.ap, acc_.ap, ACT.Silu, t1)
                acc_.written(t1)
                acc_.used(t)
                out.written(t)
            elif s < 12:
                t = turn_to_tokens(ps, mark, lambda ap, m: a_copy(v_ml[:, :, s - 8, 0:ML_D], ap, m))
                v_ml_ready.append(t)
            else:
                t = a_act(sig_o[s - 12].ap, ps.ap, ACT.Sigmoid, mark)
                ps.used(t)
                sig_o[s - 12].written(t)
        conv.close()

        free = fence()
        gs = ExitStack()
        rows_mem = sb_in(gs, "gate_rows", [36, T])
        rows_e = sb_in(gs, "gate_rows_e", [36, T])
        g_mem = sb_in(gs, "gate_mem", [32, 8, P])
        g_small = sb_in(gs, "gate_small", [32, 16])
        m_mem = sb_in(gs, "m_mem", [4, 64])
        dve.wait(free)
        act.wait(free)
        ps, mark = one("w_gates", h_rhs())
        h_used(mark)
        F = slice(32, 36)
        t_i = v_ts(rows_mem[0:4, :], ps.ap[0:4, :], vec("gate_b")[0:4, :], ALU.add, mark)
        t_f = v_ts(rows_mem[F, :], ps.ap[F, :], vec("gate_b")[F, :], ALU.add, mark, s2=-1.0, op1=ALU.mult)
        ps.used(t_i, t_f)
        t = v_ts(rows_e[F, :], rows_mem[F, :], EXACT_FROM, ALU.min, t_f)
        act.do(lambda e: e.preload_act_table_set("natural_log_exp_and_others"))
        t = a_act(rows_e[F, :], rows_e[F, :], ACT.Exp, t)
        t = a_act(rows_e[F, :], rows_e[F, :], ACT.Ln, t, bias=1.0)
        t_f = v_tt(rows_mem[F, :], rows_e[F, :], rows_mem[F, :], ALU.max, t)
        dma_g = Dma("dma_gates")
        t = dma_g.start(sync, io["gate_i"], rows_mem[0:4, :], t_i)
        t = dma_g.start(sync, io["gate_f"], rows_mem[F, :], t_f)
        t = dma_g.start(sync, g_mem[:, 0, :], io["gate_i"].rearrange("h (c t) -> (h c) t", t=P), t)
        t_g = dma_g.start(sync, g_mem[:, 1, :], io["gate_f"].rearrange("h (c t) -> (h c) t", t=P), t)
        I, NF, B, G, CM, M, W, X = (g_mem[:, i, :] for i in range(8))
        t_one = dve.mark(lambda e: e.memset(X, 1.0))
        t = dve.mark(lambda e: e.tensor_tensor_scan(B, X, NF, 0.0, ALU.mult, ALU.subtract), t_g, t_one)
        t = v_tt(G, I, B, ALU.subtract, t)
        t_cm = dve.mark(lambda e: e.tensor_tensor_scan(CM, X, G, -3e38, ALU.mult, ALU.max), t)
        t1 = v_copy(g_small[:, 0:1], CM[:, P - 1:P], t_cm)
        t2 = v_copy(g_small[:, 1:2], B[:, P - 1:P], t_cm)
        dma_g.start(sync, io["chunk_end"][0].rearrange("(r o) -> r o", o=1), g_small[:, 0:1], t1)
        t = dma_g.start(sync, io["chunk_end"][1].rearrange("(r o) -> r o", o=1), g_small[:, 1:2], t2)
        t = dma_g.start(sync, m_mem[:, 0:8], io["chunk_end"][0:1, :].rearrange("a (h c) -> (a h) c", c=8), t)
        t = dma_g.start(sync, m_mem[:, 8:16], io["chunk_end"][1:2, :].rearrange("a (h c) -> (a h) c", c=8), t)
        t0 = dve.mark(lambda e: e.memset(m_mem[:, 16:17], 0.0))
        t = dve.mark(lambda e: e.tensor_tensor_scan(m_mem[:, 17:25], m_mem[:, 0:8], m_mem[:, 8:16], 0.0,
                                                    ALU.max, ALU.add), t, t0)
        t = dma_g.start(sync, io["chunk_m"][0], m_mem[:, 16:24], t)
        t = dma_g.start(sync, io["chunk_m"][1], m_mem[:, 17:25])
        t = dma_g.start(sync, g_small[:, 2:3], io["chunk_m"][0].rearrange("h (c o) -> (h c) o", o=1), t)
        t = dma_g.start(sync, g_small[:, 3:4], io["chunk_m"][1].rearrange("h (c o) -> (h c) o", o=1), t)
        m_old, m_new, end_b, shift_c, dec = (g_small[:, i:i + 1] for i in (2, 3, 1, 4, 5))
        t_M = v_ts(M, CM, m_old, ALU.max, t)
        dma_m = Dma("dma_m")
        t_m_dram = dma_m.start(sync, io["m_rows"], M, t_M)
        t_w = a_act(W, M, ACT.Exp, t_M, bias=m_old, scale=-1.0)
        t = v_tt(NF, B, M, ALU.add, t_M)
        t_nm = a_act(NF, NF, ACT.Exp, t, scale=-1.0)
        t = v_tt(shift_c, end_b, m_new, ALU.subtract, t_M)
        t_ws = a_act(I, G, ACT.Exp, t, bias=shift_c)
        t_d = a_act(dec, shift_c, ACT.Exp, t, bias=m_old)
        t = dma_g.start(sync, io["decay_row"].rearrange("(r o) -> r o", o=1), dec, t_d)
        t_dec = dma_g.start(sync, decay[:, :], io["decay_row"].partition_broadcast(P), t)
        bank = banks[0]
        for i, (row, tok) in enumerate(((G, t_cm), (W, t_w), (NF, t_nm), (I, t_ws))):
            mark = transpose(bank.ap[:, 32 * i:32 * i + 32], row, tok, bank.busy, free, rows=32)
        bank.written(mark)
        t_cols = v_copy(cols[:, :, :].rearrange("p a b -> p (a b)"), bank.ap[:, 0:128], mark)
        bank.used(t_cols)
        gs_tokens = [t_m_dram, t_dec]
        gs.close()

        free = fence() + gs_tokens
        for q in (act, dve, pool):
            q.wait(free)
        state = Buf(sb_in(ml, "state", [P, ML_H, W1])[:, :, :])
        t_state = pool.mark(lambda e: e.memset(state.ap, 0.0))
        state.written(t_state)

        def ring(name, shape, n):
            return Ring([Buf(sb_in(ml, f"{name}{i}", shape)[tuple(slice(None) for _ in shape)]) for i in range(n)])

        d_ring = ring("d_tile", [P, ML_H, P], 2)
        p_ring = ring("p_tile", [P, ML_H, P], 1)
        kt_ring = ring("k_tok", [P, ML_H, P], 1)
        vw_ring = ring("v_weighted", [P, ML_H, W1], 1)
        num_ring = ring("num", [P, ML_H, W1], 1)
        hn_ring = ring("h_norm", [P, ML_H, P], 2)
        d_dma = [Dma(f"d_dma{i}") for i in range(2)]
        sml = sb_in(ml, "ml_small", [P, 8 * ML_H])
        for k in range(KD):
            h_ready[k] = []
        s_bank, tr_bank = banks[0], banks[7]
        k_scale = ML_D ** -0.5
        later = const("later_neg").unsqueeze(1).to_broadcast([P, ML_H, P])
        m_rows = io["m_rows"].rearrange("(h c) t -> c h t", c=NB)
        pe.wait(free)

        def chunk_cols(kind, c, n):
            v = cols[:, kind, :].rearrange("p (h c) -> p h c", c=NB)[:, :, c:c + 1]
            return v if n == 1 else v.to_broadcast([P, ML_H, n])

        t_small = None
        h_parts = [[] for _ in range(KD)]
        for c in range(NB):
            tok = slice(c * P, (c + 1) * P)
            d, d_i = d_ring.take(), c % 2
            t = d_dma[d_i].start(sync, d.ap, m_rows[c].partition_broadcast(P), d.busy, free)
            t = v_tt(d.ap, later, d.ap, ALU.subtract, t)
            t = v_tt(d.ap, d.ap, chunk_cols(0, c, P), ALU.add, t, t_cols)
            t = a_act(d.ap, d.ap, ACT.Exp, t)
            d.written(t)
            for h in range(ML_H):
                mark = mm_mark(s_bank.ap[:, h * P:(h + 1) * P], k_ml[h].ap[:, tok], q_ml[h].ap[:, tok], True, True,
                               s_bank.busy, k_ml[h].ready, q_ml[h].ready)
            s_bank.written(mark)
            p = p_ring.take()
            t = v_stt(p.ap, s_bank.ap.rearrange("p (h t) -> p h t", h=ML_H), k_scale, d.ap, ALU.mult, ALU.mult,
                      mark, d.ready, p.busy)
            s_bank.used(t)
            d.used(t)
            p.written(t)
            for h in range(ML_H):
                mark = transpose(tr_bank.ap[:, h * P:(h + 1) * P], k_ml[h].ap[:, tok], tr_bank.busy)
            tr_bank.written(mark)
            kt = kt_ring.take()
            t = act.mark((lambda o, i: lambda e: e.activation(o, i, ACT.Copy, scale=k_scale))(
                kt.ap.rearrange("p h t -> p (h t)"), tr_bank.ap), mark, kt.busy)
            tr_bank.used(t)
            kt.written(t)
            vw = vw_ring.take()
            t = g_tt(vw.ap, v_ml[:, c, :, :], chunk_cols(3, c, W1), ALU.mult, v_ml_ready, t_cols, vw.busy)
            vw.written(t)

            def four(first_bank, lhsT, rhs, *w):
                mark = None
                for h in range(ML_H):
                    bank = banks[first_bank + h // 2]
                    mark = mm_mark(bank.ap[:, (h % 2) * W1:(h % 2 + 1) * W1], lhsT(h), rhs(h), True, True,
                                   bank.busy if h % 2 == 0 else None, *w)
                    if h % 2:
                        bank.written(mark)
                return mark

            t_inter = four(3, lambda h: q_ml[h].ap[:, tok], lambda h: state.ap[:, h, :], state.ready)
            state.used(t_inter)
            t_intra = four(1, lambda h: p.ap[:, h, :], lambda h: v_ml[:, c, h, :], p.ready, v_ml_ready)
            p.used(t_intra)
            t_next = four(5, lambda h: kt.ap[:, h, :], lambda h: vw.ap[:, h, :], kt.ready, vw.ready)
            kt.used(t_next)
            vw.used(t_next)
            num = num_ring.take()
            ts = []
            for h in range(ML_H):
                bank = banks[3 + h // 2]
                t = act.mark((lambda o, i, s: lambda e: e.activation(o, i, ACT.Copy, scale=s))(
                    num.ap[:, h, :], bank.ap[:, (h % 2) * W1:(h % 2 + 1) * W1],
                    cols[:, 1, h * NB + c:h * NB + c + 1]), t_inter, t_cols, num.busy)
                bank.used(t)
                ts.append(t)
            t_st = []
            for h in range(ML_H):
                bank = banks[5 + h // 2]
                t = v_stt(state.ap[:, h, :], state.ap[:, h, :], decay[:, h * NB + c:h * NB + c + 1],
                          bank.ap[:, (h % 2) * W1:(h % 2 + 1) * W1], ALU.mult, ALU.add, t_next, state.busy, state.ready)
                bank.used(t)
                t_st.append(t)
            state.written(*t_st)
            t_n = []
            for b in range(2):
                bank = banks[1 + b]
                part = num.ap[:, 2 * b:2 * b + 2, :]
                t = v_tt(part, part, bank.ap[:, 0:2 * W1].rearrange("p (h w) -> p h w", h=2), ALU.add, ts, t_intra)
                bank.used(t)
                t_n.append(t)
            den_c = num.ap[:, :, ML_D:W1]
            dn, r, ss, sc = (sml[:, i * ML_H:(i + 1) * ML_H] for i in range(4))

            def as3(a):
                return a.unsqueeze(2)

            t = v_stt(as3(dn), den_c, -1.0, den_c, ALU.mult, ALU.max, t_n, t_small)
            t = v_tt(as3(dn), as3(dn), chunk_cols(2, c, 1), ALU.max, t)
            t_r = dve.mark((lambda o, i: lambda e: e.reciprocal(o, i))(r, dn), t)
            hn = hn_ring.take()
            t = v_tt(hn.ap, num.ap[:, :, 0:ML_D], num.ap[:, :, 0:ML_D], ALU.mult, t_n, hn.busy)
            t = dve.mark((lambda o, i: lambda e: e.tensor_reduce(o, i, AX.X, ALU.add))(ss, hn.ap), t, t_small)
            t = v_tt(sc, r, r, ALU.mult, t_r)
            t = v_tt(ss, ss, sc, ALU.mult, t)
            t = a_act(ss, ss, ACT.Ln, t, bias=eps_col[:, :], scale=1.0 / ML_D)
            t = a_act(ss, ss, ACT.Exp, t, scale=-0.5)
            t = v_tt(sc, ss, r, ALU.mult, t)
            t_small = v_tt(hn.ap, num.ap[:, :, 0:ML_D], as3(sc).to_broadcast([P, ML_H, ML_D]), ALU.mult, t)
            hn.written(t_small)
            num.written()
            num.used(t_small)
            for h in range(ML_H):
                mark = transpose(tr_bank.ap[:, h * P:(h + 1) * P], hn.ap[:, h, :], hn.ready, tr_bank.busy)
            tr_bank.written(mark)
            ts = []
            for h in range(ML_H):
                t = v_stt(hn.ap[:, h, :], tr_bank.ap[:, h * P:(h + 1) * P], vec("ml_norm_g", h),
                          sig_o[h].ap[:, tok], ALU.mult, ALU.mult, mark, sig_o[h].ready)
                ts.append(t)
            tr_bank.used(t)
            made = split(h_hi[:, 0:ML_H, tok], h_lo[:, 0:ML_H, tok], hn.ap, ts, h_busy[0])
            hn.used(*made)
            for k in range(ML_H):
                h_parts[k] += made
        ml.close()
        for k in range(ML_H):
            h_ready[k], h_busy[k] = h_parts[k], []
        for k in range(4):
            made = split(h_hi[:, 4 + k, :], h_lo[:, 4 + k, :], o_at[:, k, :], o_at_ready, h_busy[4 + k])
            h_ready[4 + k], h_busy[4 + k] = made, []
        mixer.close()

        def normed_sum(name, y, keep_x):
            inverse_rms(y)
            for k in range(KD):
                t = tmps.take()
                g0 = KD if name == "mix" else 3 * KD
                t1 = v_stt(t.ap, y[k].ap, gain[:, g0 + k:g0 + k + 1], norm_row.ap, ALU.mult, ALU.mult,
                           y[k].ready, norm_row.ready, t.busy)
                norm_row.used(t1)
                t2 = v_tt(keep_x[k].ap, keep_x[k].ap, t.ap, ALU.add, t1, keep_x[k].ready, keep_x[k].busy)
                t.written(t1)
                t.used(t2)
                keep_x[k].written(t2)

        ys = ExitStack()
        free = fence()
        act.wait(free)
        dve.wait(free)
        y_mem = sb_in(ys, "y_mem", [P, KD, T])
        y = [Buf(y_mem[:, k, :]) for k in range(KD)]
        xs = ExitStack()
        x = load_x(xs, "x_mid", io["x_park"], free + parked)
        for m in range(KD):
            ps, mark = one("w_out2", h_rhs())
            h_used(mark)
            t = a_copy(y[m].ap, ps.ap, mark)
            ps.used(t)
            y[m].written(t)
        normed_sum("mix", y, x)
        if stages == 5:
            finish(x)
            xs.close()
            ys.close()
            return play(nc, sync, act, dve, pe, pool)
        inverse_rms(x)
        normed_to_h(x, lambda k: gain[:, 2 * KD + k:2 * KD + k + 1], lambda k: mod[:, 3 * KD + k:3 * KD + k + 1])
        parked = park(x)
        xs.close()

        ff = ExitStack()
        free = fence() + parked
        act.wait(free)
        dve.wait(free)
        FP = FFN_CONV - 1
        conv_in = Ring([Buf(sb_in(ff, f"ffn_conv_in{i}", [P, FP + T])[:, :]) for i in range(2)])
        val = Ring([Buf(sb_in(ff, "ffn_value", [P, T])[:, :])])
        for b in conv_in.bufs:
            b.zero = dve.mark((lambda o: lambda e: e.memset(o, 0.0))(b.ap[:, 0:FP]))

        def convolved_chunk(i):
            outs = []
            for name, c, ring_ in (("w_gate2", i, tmps), ("w_up2", KF + i, val)):
                ps, mark = one(name, h_rhs())
                h_used(mark)
                src, dst = conv_in.take(), ring_.take()
                t = a_copy(src.ap[:, FP:], ps.ap, mark, src.busy)
                ps.used(t)
                t1 = conv_taps(src, dst, FFN_CONV, lambda j: vec("ffn_conv_w", 2 * KF * j + c), vec("ffn_conv_b", c),
                               t, src.zero, dst.busy)
                src.written(t)
                src.used(t1)
                dst.written(t1)
                if name == "w_gate2":
                    t1 = a_act(dst.ap, dst.ap, ACT.Gelu_apprx_tanh, t1)
                    dst.written(t1)
                outs.append(dst)
            a, b = outs
            t = v_tt(a.ap, a.ap, b.ap, ALU.mult, a.ready, b.ready)
            b.used(t)
            a.written(t)
            return a

        def add_to_y(g, m, ps, mark):
            if g == 0:
                t = a_copy(y[m].ap, ps.ap, mark, y[m].busy, y[m].ready)
            else:
                t = v_tt(y[m].ap, y[m].ap, ps.ap, ALU.add, mark, y[m].ready)
            ps.used(t)
            y[m].written(t)

        feed_forward(("b",), convolved_chunk, add_to_y)
        ff.close()
        xs = ExitStack()
        x = load_x(xs, "x_last", io["x_park"], fence() + parked)
        normed_sum("ffn", y, x)
        finish(x)
        xs.close()
        ys.close()
        return play(nc, sync, act, dve, pe, pool)


def play(nc, sync, act, dve, pe, pool):
    with nc.Block() as block:
        @block.sync
        def _(e):
            sync.play(e)

        @block.scalar
        def _(e):
            act.play(e)

        @block.vector
        def _(e):
            dve.play(e)

        @block.tensor
        def _(e):
            pe.play(e)

        @block.gpsimd
        def _(e):
            pool.play(e)


def stripes(w, first=0, last=None, k=KD, m=1):
    w = w[:, first:last]
    kk, mm_ = w.shape[0] // (P * k), w.shape[1] // (P * m)
    w = w.reshape(kk, k, P, mm_, m, P).transpose(0, 3, 2, 4, 1, 5)
    return np.ascontiguousarray(w.reshape(kk * mm_, P, m * k * P))


def columns(v):
    return v.reshape(-1, P).T


def layout(a):
    out = {}
    out["x"] = np.ascontiguousarray(a["x"][0].T).reshape(KD, P, T)
    out["p"] = np.ascontiguousarray(a["p"][0, 0].T).reshape(2, P, T)
    out["w_in_a"] = stripes(a["w_in"][0])
    out["w_pool"] = a["w_pool"][0]
    out["w_branch_a"] = stripes(a["w_branch_a"][0], k=4)
    out["w_branch_b"] = stripes(a["w_branch_b"][0], k=4)
    out["w_out"] = stripes(a["w_out"][0])
    out["w_ffn_gate"] = stripes(a["w_ffn_gate"][0])
    out["w_ffn_up"] = stripes(a["w_ffn_up"][0])
    out["w_ffn_down"] = stripes(a["w_ffn_down"][0], k=FFN_GROUP, m=8 // FFN_GROUP)
    out["w_ple_gate"] = stripes(a["w_ple_gate"][0])
    out["w_ple_proj"] = stripes(a["w_ple_proj"][0], k=2, m=4)
    w = a["w_in_2"][0]
    out["w_in_b_ml"] = stripes(w, 0, 2048)
    out["w_in_b_at"] = stripes(w, 2056, 2824)
    g = np.zeros((KD, P, P), w.dtype)
    g[:, :, 0:4] = w[:, 2048:2052].reshape(KD, P, 4)
    g[:, :, 32:36] = w[:, 2052:2056].reshape(KD, P, 4)
    out["w_in_b_gates"] = np.ascontiguousarray(g.transpose(1, 0, 2).reshape(P, KD * P))
    out["w_out_b"] = stripes(a["w_out_2"][0])
    out["w_up_b"] = stripes(a["w_up_2"][0])
    out["w_down_b"] = stripes(a["w_down_2"][0], k=FFN_GROUP, m=8 // FFN_GROUP)
    out["w_ada"] = stripes(a["w_ada_2"][0])
    vecs = np.zeros((P, N_VEC), np.float32)

    def put(name, value, rows=P):
        vecs[0:rows, VEC[name]:VEC[name] + value.shape[1]] = value

    for name, key in (("norm_mix", "norm_mix"), ("norm_ffn", "norm_ffn"), ("norm_ple", "norm_ple"),
                      ("norm_final", "norm_final"), ("pool_scale", "pool_scale"), ("pre_mix_g", "pre_mix_g_2"),
                      ("ml_conv_w", "ml_conv_w_2"), ("ml_conv_b", "ml_conv_b_2"), ("ml_norm_g", "ml_norm_g_2"),
                      ("attn_norm_g", "attn_norm_g_2"), ("post_mix_g", "post_mix_g_2"),
                      ("pre_ffn_g", "pre_ffn_g_2"), ("ffn_conv_w", "ffn_conv_w_2"), ("ffn_conv_b", "ffn_conv_b_2"),
                      ("post_ffn_g", "post_ffn_g_2"), ("b_ada", "b_ada_2"), ("c", "c_2")):
        put(name, columns(a[key].reshape(-1)))
    vecs[0:4, VEC["gate_b"]] = a["ml_i_b_2"][0]
    vecs[32:36, VEC["gate_b"]] = a["ml_f_b_2"][0]
    put("sinks", np.broadcast_to(a["attn_sinks_2"], (P, AT_H)))
    out["vecs"] = vecs
    out["consts"], out["rope"] = constants()
    return out


SCRATCH = {"x_park": (KD, P, T), "gate_i": (4, T), "gate_f": (4, T), "chunk_end": (2, 32), "chunk_m": (2, 4, 8),
           "m_rows": (32, P), "decay_row": (32,)}


def build(nc, arrays, **kw):
    io = {}
    for name, v in arrays.items():
        io[name] = nc.dram_tensor(f"in_{name}", v.shape, F32, kind="ExternalInput").ap()
    for name, shape in SCRATCH.items():
        io[name] = nc.dram_tensor(name, shape, F32, kind="Internal").ap()
    io["out"] = nc.dram_tensor("out_dram", (KD, P, T), F32, kind="ExternalOutput").ap()
    two_blocks(nc, io, **kw)


def kernel(**inputs):
    import concourse.bacc as bacc
    from concourse.bass_utils import run_bass_kernel_spmd

    nc = bacc.Bacc("TRN2", target_bir_lowering=False, num_devices=1)
    arrays = layout({k: np.asarray(v) for k, v in inputs.items()})
    build(nc, arrays)
    r = run_bass_kernel_spmd(nc, [{f"in_{k}": v for k, v in arrays.items()}], core_ids=[0])
    return np.ascontiguousarray(r.results[0]["out_dram"].reshape(D, T).T)[None]
```

```python
from contextlib import ExitStack

import numpy as np

import concourse.bass as bass
from concourse import mybir

F32 = mybir.dt.float32
F32R = mybir.dt.float32r
BF16 = mybir.dt.bfloat16
ACT = mybir.ActivationFunctionType
ALU = mybir.AluOpType
AX = mybir.AxisListType

P = 128
T = 1024
D = 1024
KD = D // P
NB = T // P
HALF = 512
NH = T // HALF
EPS = 1e-6
NEG = -1e30

D_POOL = 512
WINDOWS = (2, 4, 8, 16)
D_SB = 512
SB_DIM = 64
D_FF = 2816
KF = D_FF // P
PLE = 256

ML_H, ML_D = 4, 128
ML_CONV = 4
AT_H, AT_KV, AT_DIM = 8, 2, 64
FFN_CONV = 3
FFN_GROUP = 2

EXACT_FROM = 16.0

VEC = {}


def _columns():
    at = 0
    for name, n in (
        ("norm_mix", KD), ("norm_ffn", KD), ("norm_ple", KD), ("norm_final", KD), ("pool_scale", 4),
        ("pre_mix_g", KD), ("ml_conv_w", ML_CONV * 8), ("ml_conv_b", 8), ("gate_b", 1), ("ml_norm_g", ML_H),
        ("attn_norm_g", 4), ("post_mix_g", KD), ("pre_ffn_g", KD), ("ffn_conv_w", FFN_CONV * 2 * KF),
        ("ffn_conv_b", 2 * KF), ("post_ffn_g", KD), ("b_ada", 6 * KD), ("c", KD), ("sinks", AT_H),
    ):
        VEC[name] = at
        at += n
    return at


N_VEC = _columns()

CONST = {}
N_CONST = 0
for _name, _n in (("ident", P), ("ones", P), ("minus_tri", P), ("minus_ones", P), ("causal_neg", P),
                  ("band_neg", 2 * P), ("later_neg", P), ("rotate", P), ("inv_count", 4 * 16), ("one", P)):
    CONST[_name] = N_CONST
    N_CONST += _n


def constants():
    p, j = np.arange(P)[:, None], np.arange(P)[None, :]
    table = np.zeros((P, N_CONST), np.float32)

    def put(name, value):
        table[:, CONST[name]:CONST[name] + value.shape[1]] = value

    put("ident", (p == j).astype(np.float32))
    put("ones", np.ones((P, P), np.float32))
    put("minus_tri", -(p >= j).astype(np.float32))
    put("minus_ones", -np.ones((P, P), np.float32))
    put("causal_neg", np.where(p >= j, NEG, 0.0).astype(np.float32))
    k2 = np.arange(2 * P)[None, :]
    put("band_neg", np.where((k2 > p) & (k2 <= p + P), 0.0, NEG).astype(np.float32))
    put("later_neg", np.where(p > j, NEG, 0.0).astype(np.float32))
    half = AT_DIM // 2
    rot = np.zeros((P, P), np.float32)
    for to in range(P):
        d = to % AT_DIM
        rot[to + half if d < half else to - half, to] = -1.0 if d < half else 1.0
    put("rotate", rot)
    counts = np.concatenate([1.0 / np.minimum(np.arange(16) + 1, w) for w in WINDOWS])
    put("inv_count", np.broadcast_to(counts.astype(np.float32), (P, 64)))
    put("one", np.ones((P, P), np.float32))
    inv = (np.float32(10000.0) ** (-np.arange(half, dtype=np.float32) / np.float32(half))).astype(np.float32)
    ang = (np.arange(T, dtype=np.float32)[None, :] * inv[:, None]).astype(np.float32).astype(np.float64)
    cos, sin = np.cos(ang).astype(np.float32), np.sin(ang).astype(np.float32)
    rope = np.concatenate([np.tile(cos, (4, 1)), np.tile(sin, (4, 1))], axis=1)
    return table, np.ascontiguousarray(rope)


class Queue:

    def __init__(self, sem):
        self.sem, self.count, self.steps, self.passed = sem, 0, [], {}

    def wait(self, *tokens):
        for t in tokens:
            if t is None:
                continue
            if isinstance(t, list):
                self.wait(*t)
            elif self.passed.get(id(t[0]), 0) < t[1]:
                self.passed[id(t[0])] = t[1]
                self.steps.append(("wait", t[0], t[1]))

    def do(self, step, *tokens):
        self.wait(*tokens)
        self.steps.append(("do", step, None))

    def mark(self, step, *tokens):
        self.wait(*tokens)
        self.count += 1
        self.steps.append(("do", step, (self.sem, 1)))
        return (self.sem, self.count)

    def now(self):
        return (self.sem, self.count) if self.count else None

    def play(self, engine):
        for kind, a, b in self.steps:
            if kind == "wait":
                engine.wait_ge(a, b)
            else:
                made = a(engine)
                if b is not None:
                    made.then_inc(b[0], b[1])


class Buf:

    def __init__(self, ap, busy=None):
        self.ap, self.ready, self.busy = ap, [], list(busy or [])

    def written(self, *tokens):
        self.ready, self.busy = list(tokens), []

    def used(self, *tokens):
        self.busy += tokens


class Ring:
    def __init__(self, bufs):
        self.bufs, self.at = bufs, 0

    def take(self):
        b = self.bufs[self.at % len(self.bufs)]
        self.at += 1
        return b


def two_blocks(nc, io):
    with ExitStack() as ctx:
        def sb_in(scope, name, shape, dt=F32):
            return scope.enter_context(nc.sbuf_tensor(name, shape, dt))

        def sb(name, shape, dt=F32):
            return sb_in(ctx, name, shape, dt)

        def sem(name):
            return ctx.enter_context(nc.semaphore(name))

        sync = Queue(sem("s_sync"))
        act = Queue(sem("s_scalar"))
        dve = Queue(sem("s_vector"))
        pe = Queue(sem("s_tensor"))
        pool = Queue(sem("s_gpsimd"))

        class Dma:

            def __init__(self, name):
                self.sem, self.count = sem(name), 0

            def start(self, queue, out, in_, *tokens):
                queue.wait(*tokens)
                self.count += 16
                queue.steps.append(("do", lambda e: e.dma_start(out, in_), (self.sem, 16)))
                return (self.sem, self.count)

        def fence():
            return [q.now() for q in (act, dve, pe, pool) if q.now()]

        consts = sb("consts", [P, N_CONST])
        vecs = sb("vecs", [P, N_VEC])
        ident_bf = sb("ident_bf", [P, P], BF16)
        causal_bf = sb("causal_bf", [P, P], BF16)
        band_bf = sb("band_bf", [P, 2 * P], BF16)
        mod = sb("mod", [P, 6 * KD])
        gain = sb("gain", [P, 4 * KD])
        w_raw = sb("w_raw", [P, 2, 1024])
        w_hi = sb("w_hi", [P, 2, 1024], F32R)
        w_lo = sb("w_lo", [P, 2, 1024], F32R)
        tmp_mem = sb("tmp_mem", [P, 2, T])
        norm_row = Buf(sb("norm_row", [P, T])[:, :])
        h_hi = sb("h_hi", [P, KD, T], F32R)
        h_lo = sb("h_lo", [P, KD, T], F32R)
        psum_mem = ctx.enter_context(nc.psum_tensor("psum_mem", [P, 8, HALF], F32))

        tmps = Ring([Buf(tmp_mem[:, i, :]) for i in range(2)])
        banks = [Buf(psum_mem[:, b, :]) for b in range(8)]

        class Pair:

            def __init__(self, i):
                self.i = i
                self.ap = psum_mem[:, 2 * i:2 * i + 2, :].rearrange("p a b -> p (a b)")

            @property
            def busy(self):
                return banks[2 * self.i].busy + banks[2 * self.i + 1].busy

            def half(self, n):
                return psum_mem[:, 2 * self.i + n, :]

            def written(self, *tokens):
                for b in (2 * self.i, 2 * self.i + 1):
                    banks[b].written(*tokens)

            @property
            def ready(self):
                return banks[2 * self.i].ready

            def used(self, *tokens):
                for b in (2 * self.i, 2 * self.i + 1):
                    banks[b].used(*tokens)

        pairs = Ring([Pair(i) for i in range(4)])

        def const(name, n=P, rows=P):
            return consts[0:rows, CONST[name]:CONST[name] + n]

        def vec(name, i=0, n=1):
            return vecs[:, VEC[name] + i:VEC[name] + i + n]

        def load(dma, out, in_, *w):
            return dma.start(sync, out, in_, *w)

        def a_act(out, in_, func, *w, bias=0.0, scale=1.0):
            return act.mark(lambda e: e.activation(out, in_, func, bias=bias, scale=scale), *w)

        def a_copy(out, in_, *w):
            return act.mark(lambda e: e.copy(out, in_), *w)

        def v_copy(out, in_, *w):
            return dve.mark(lambda e: e.tensor_copy(out, in_), *w)

        def v_tt(out, a, b, op, *w):
            return dve.mark(lambda e: e.tensor_tensor(out, a, b, op), *w)

        def v_ts(out, a, s1, op0, *w, s2=None, op1=None):
            if op1 is None:
                return dve.mark(lambda e: e.tensor_scalar(out, a, s1, None, op0), *w)
            return dve.mark(lambda e: e.tensor_scalar(out, a, s1, s2, op0, op1), *w)

        def v_stt(out, a, s, b, op0, op1, *w):
            return dve.mark(lambda e: e.scalar_tensor_tensor(out=out, in0=a, scalar=s, in1=b, op0=op0, op1=op1), *w)

        def g_tt(out, a, b, op, *w):
            return pool.mark(lambda e: e.tensor_tensor(out, a, b, op), *w)

        def mm(out, lhsT, rhs, start, stop, *w):
            pe.do(lambda e: e.matmul(out, lhsT, rhs, start=start, stop=stop, skip_group_check=True), *w)

        def mm_mark(out, lhsT, rhs, start, stop, *w):
            return pe.mark(lambda e: e.matmul(out, lhsT, rhs, start=start, stop=stop, skip_group_check=True), *w)

        def transpose(out, in_, *w, rows=P):
            ident = consts[0:rows, CONST["ident"]:CONST["ident"] + rows]
            return pe.mark(lambda e: e.transpose(out, in_, ident), *w)

        def split(hi, lo, src, *w, bias=None):
            if bias is None:
                t_hi = a_copy(hi, src, *w)
                t_lo = v_tt(lo, src, hi.bitcast(F32), ALU.subtract, t_hi)
            else:
                t_hi = a_act(hi, src, ACT.Identity, *w, bias=bias)
                t_lo = v_stt(lo, src, bias, hi.bitcast(F32), ALU.add, ALU.subtract, t_hi)
            return [t_hi, t_lo]

        units = []
        for j in range(4):
            for part in range(3):
                units.append(("w_qkv", io["w_in_a"][4 + 4 * part + j]))
        for g in range(4):
            units.append(("w_u", io["w_in_a"][g]))
            if g > 0:
                units.append(("w_pool", io["w_pool"][g - 1]))
        for m in range(KD):
            units.append(("w_ga", io["w_in_a"][16 + m]))
            units.append(("w_gb", io["w_in_a"][24 + m]))
            if m == 0:
                units.append(("w_pool", io["w_pool"][3]))
            units.append(("w_ba", io["w_branch_a"][m]))
            units.append(("w_bb", io["w_branch_b"][m]))
        for m in range(KD):
            units.append(("w_out", io["w_out"][m]))
        n_groups = KF // FFN_GROUP

        def ffn_order(names, down):
            order = []
            for g in range(n_groups + 1):
                if g < n_groups:
                    for i in range(g * FFN_GROUP, (g + 1) * FFN_GROUP):
                        for name, source in names:
                            order.append((name, source[i]))
                if g > 0:
                    for m in range(2):
                        order.append(("w_down", down[2 * (g - 1) + m]))
            return order

        units += ffn_order([("w_gate", io["w_ffn_gate"]), ("w_up", io["w_ffn_up"])], io["w_ffn_down"])
        for m in range(KD):
            if m % 4 == 0:
                units.append(("w_pp", io["w_ple_proj"][m // 4]))
            units.append(("w_pg", io["w_ple_gate"][m]))
        for s in range(5):
            units.append(("w_qk_at", io["w_in_b_at"][s]))
        units.append(("w_v_at", io["w_in_b_at"][5]))
        for s in range(8, 16):
            units.append(("w_ml", io["w_in_b_ml"][s]))
        units.append(("w_gates", io["w_in_b_gates"]))
        for s in range(8):
            units.append(("w_ml", io["w_in_b_ml"][s]))
        for m in range(KD):
            units.append(("w_out2", io["w_out_b"][m]))
        units += ffn_order([("w_gate2", io["w_up_b"][0:KF]), ("w_up2", io["w_up_b"][KF:2 * KF])], io["w_down_b"])

        class Weights:
            def __init__(self):
                self.raw = [Buf(w_raw[:, i, :]) for i in range(2)]
                self.dma = [Dma(f"w_load{i}") for i in range(2)]
                self.hi = [Buf(w_hi[:, i, :]) for i in range(2)]
                self.lo = [Buf(w_lo[:, i, :]) for i in range(2)]
                self.loaded = self.cut = self.taken = 0

            def load(self):
                n, i = self.loaded, self.loaded % 2
                if n >= len(units):
                    return
                self.loaded += 1
                width = units[n][1].shape[-1]
                t = load(self.dma[i], self.raw[i].ap[:, 0:width], units[n][1], self.raw[i].busy)
                self.raw[i].written(t)

            def split(self):
                n, i = self.cut, self.cut % 2
                if n >= len(units):
                    return
                self.load()
                self.cut += 1
                width = units[n][1].shape[-1]
                raw, hi, lo = self.raw[i], self.hi[i], self.lo[i]
                t_hi = a_copy(hi.ap[:, 0:width], raw.ap[:, 0:width], raw.ready, hi.busy)
                t_lo = g_tt(lo.ap[:, 0:width], raw.ap[:, 0:width], hi.ap[:, 0:width].bitcast(F32), ALU.subtract,
                            t_hi, raw.ready, lo.busy)
                raw.used(t_hi, t_lo)
                hi.written(t_hi)
                lo.written(t_lo)

            def take(self, name):
                n, i = self.taken, self.taken % 2
                assert units[n][0] == name, (units[n][0], name)
                self.taken += 1
                while self.cut < self.taken:
                    self.split()
                return self.hi[i], self.lo[i]

            def ahead(self):
                while self.cut < min(self.taken + 1, len(units)):
                    self.split()

        weights = Weights()

        def project_steps(out, unit, blocks, rhs, waits):
            hi, lo = unit
            mark = None
            n = len(blocks)
            for k, b in enumerate(blocks):
                w_h, w_l = hi.ap[:, b * P:(b + 1) * P], lo.ap[:, b * P:(b + 1) * P]
                x_h, x_l, ready = rhs[k]
                for part, (w, x) in enumerate(((w_h, x_h), (w_h, x_l), (w_l, x_h))):
                    for half in range(NH):
                        cols = slice(half * HALF, (half + 1) * HALF)
                        last = k == n - 1 and part == 2
                        args = (out.half(half), w, x[:, cols], k == 0 and part == 0, last,
                                waits, ready, lo.ready if part == 2 else hi.ready)
                        if last and half == NH - 1:
                            mark = mm_mark(*args)
                        else:
                            mm(*args)
                yield
            hi.used(mark)
            lo.used(mark)
            out.written(mark)

        def one(name, rhs, blocks=tuple(range(KD)), unit=None):
            out = pairs.take()
            if unit is None:
                unit = weights.take(name)
                weights.ahead()
            for _ in project_steps(out, unit, blocks, rhs, out.busy):
                pass
            return out, out.ready[0]

        def two(names, rhs):
            outs, steps = [], []
            for name in names:
                out = pairs.take()
                outs.append(out)
                steps.append(project_steps(out, weights.take(name), tuple(range(KD)), rhs, out.busy))
            for _ in range(KD):
                for st in steps:
                    next(st)
            for st in steps:
                for _ in st:
                    pass
            weights.ahead()
            return [(out, out.ready[0]) for out in outs]

        dma_const, dma_vec = Dma("dma_const"), Dma("dma_vec")
        t_const = load(dma_const, consts[:, :], io["consts"])
        t_vec = load(dma_vec, vecs[:, :], io["vecs"])
        dma_x = [Dma(f"dma_x{k}") for k in range(KD)]
        out_dma = Dma("dma_out")
        dma_misc = Dma("dma_misc")
        t_ib = v_copy(ident_bf[:, :], const("ident"), t_const)
        t_cb = v_copy(causal_bf[:, :], const("causal_neg"), t_const)
        t_bb = v_copy(band_bf[:, :], const("band_neg", 2 * P), t_const)
        for q in (pe, act, dve, pool):
            q.wait(t_const, t_vec)
        pe.wait(t_ib, t_cb, t_bb)

        h_busy = [[] for _ in range(KD)]
        h_ready = [[] for _ in range(KD)]

        def h_rhs(ks=range(KD)):
            return [(h_hi[:, k, :], h_lo[:, k, :], h_ready[k]) for k in ks]

        def h_used(mark):
            for k in range(KD):
                h_busy[k].append(mark)

        class SquareSum:

            def __init__(self, row):
                self.row, self.n, self.total = row, 0, None

            def add(self, ap, ready, scale=1.0):
                row = self.row
                self.n += 1
                if self.n == 1:
                    self.total = t_sq = a_act(row.ap, ap, ACT.Square, ready, row.busy, scale=scale)
                else:
                    t = tmps.take()
                    t_sq = a_act(t.ap, ap, ACT.Square, ready, t.busy, scale=scale)
                    add = v_tt if self.n >= KD - 1 else g_tt
                    self.total = add(row.ap, row.ap, t.ap, ALU.add, self.total, t_sq)
                    t.written(t_sq)
                    t.used(self.total)
                return t_sq

            def inverse(self, eps=None, total=None):
                row, total = self.row, total or self.total
                out = pairs.take()
                mark = None
                for half in range(NH):
                    cols = slice(half * HALF, (half + 1) * HALF)
                    mark = mm_mark(out.half(half), const("ones"), row.ap[:, cols], True, True, total, out.busy)
                out.written(mark)
                t_std = a_act(row.ap, out.ap, ACT.Sqrt, mark, bias=eps or eps_col[:, 0:1], scale=1.0 / D)
                out.used(t_std)
                t_inv = dve.mark(lambda e: e.reciprocal(row.ap, row.ap), t_std)
                row.written(t_inv)

        eps_col = sb("eps_col", [P, 2])
        t_eps = [dve.mark(lambda e: e.memset(eps_col[:, 0:1], EPS)),
                 dve.mark(lambda e: e.memset(eps_col[:, 1:2], EPS * EPS))]
        act.wait(t_eps)

        def scaled_to_h(k, c, g):
            t_hi = a_act(h_hi[:, k, :], c.ap, ACT.Copy, c.ready, h_busy[k], scale=g)
            t_lo = v_stt(h_lo[:, k, :], c.ap, g, h_hi[:, k, :].bitcast(F32), ALU.mult, ALU.subtract, t_hi,
                         h_busy[k])
            c.used(t_hi, t_lo)
            h_ready[k], h_busy[k] = [t_hi, t_lo], []

        def unscale(out, ps, *w, factor=1.0, rows=slice(0, P)):
            if factor == 1.0:
                t = v_tt(out, ps.ap[rows, :], norm_row.ap[rows, :], ALU.mult, norm_row.ready, *w)
            else:
                t = v_stt(out, ps.ap[rows, :], factor, norm_row.ap[rows, :], ALU.mult, ALU.mult, norm_row.ready, *w)
            norm_row.used(t)
            return t

        def normed_to_h(chunks, row, gains, shifts):
            for k, c in enumerate(chunks):
                t = tmps.take()
                t_h = v_stt(t.ap, c.ap, gains(k), row.ap, ALU.mult, ALU.mult, c.ready, row.ready, t.busy)
                c.used(t_h)
                t.written(t_h)
                made = split(h_hi[:, k, :], h_lo[:, k, :], t.ap, t_h, h_busy[k], bias=shifts(k))
                t.used(*made)
                h_ready[k], h_busy[k] = made, []

        def load_x(scope, name, source, busy):
            mem = sb_in(scope, name, [P, KD, T])
            chunks = []
            for k in range(KD):
                c = Buf(mem[:, k, :])
                c.written(load(dma_x[k], c.ap, source[k], busy))
                chunks.append(c)
            return chunks

        def finish(chunks):
            for k, c in enumerate(chunks):
                t = out_dma.start(sync, io["out"][k], c.ap, c.ready)
            sync.wait(t)

        weights.split()
        weights.split()
        scope = ExitStack()
        x = load_x(scope, "x_first", io["x"], None)
        total = SquareSum(norm_row)
        for k, c in enumerate(x):
            scaled_to_h(k, c, vec("norm_mix", k))
            c.used(total.add(c.ap, c.ready))
        first_qk = two(("w_qkv", "w_qkv"), h_rhs())
        total.inverse()
        scope.close()

        outer = ExitStack()
        yb_hi = sb_in(outer, "yb_hi", [P, 4, T], F32R)
        yb_lo = sb_in(outer, "yb_lo", [P, 4, T], F32R)
        attn = ExitStack()
        free = fence()
        act.wait(free)
        dve.wait(free)
        pool.wait(free)
        pads = [[Buf(sb_in(attn, f"q_pad{i}{par}", [P, T])[:, :]) for par in range(2)] for i in range(2)]
        k_feat = [Buf(sb_in(attn, f"k_feat{i}", [P, T])[:, :]) for i in range(2)]
        v_tok = [Buf(sb_in(attn, f"v_tok{i}", [P, T])[:, :]) for i in range(2)]
        pad_zero = []
        for side in pads:
            for par in range(2):
                other = slice(64, 128) if par == 0 else slice(0, 64)
                pad_zero.append(dve.mark((lambda o: lambda e: e.memset(o, 0.0))(side[par].ap[other, :])))
        pe.wait(pad_zero)
        proj_pair = Pair(3)

        def head_rows(par):
            return slice(64 * par, 64 * par + 64)

        def take_q(j, ps, mark):
            done = []
            for par in range(2):
                rows, pad = head_rows(par), pads[j % 2][par]
                t = unscale(pad.ap[rows, :], ps, mark, pad.busy, factor=SB_DIM ** -0.5, rows=rows)
                pad.written(t)
                done.append(t)
            ps.used(*done)

        def take_k(j, ps, mark):
            k = k_feat[j % 2]
            t = unscale(k.ap, ps, mark, k.busy)
            ps.used(t)
            k.written(t)

        def take_v(j, ps, mark):
            v_t, v = tmps.take(), v_tok[j % 2]
            t = unscale(v_t.ap, ps, mark, v_t.busy)
            ps.used(t)
            v_t.written(t)
            yield
            for b in range(NB):
                mark = transpose(ps.ap[:, b * P:(b + 1) * P], v_t.ap[:, b * P:(b + 1) * P], t, ps.busy)
            v_t.used(mark)
            ps.written(mark)
            t = a_copy(v.ap, ps.ap, mark, v.busy)
            ps.used(t)
            v.written(t)

        def qkv_steps(j):
            for part in range(3):
                unit = weights.take("w_qkv")
                weights.ahead()
                yield from project_steps(proj_pair, unit, tuple(range(KD)), h_rhs(), proj_pair.busy)
                mark = proj_pair.ready
                h_used(mark[0])
                if part == 0:
                    take_q(j, proj_pair, mark)
                elif part == 1:
                    take_k(j, proj_pair, mark)
                else:
                    yield from take_v(j, proj_pair, mark)

        e_ring = Ring([Buf(sb_in(attn, f"e_tile{i}", [P, HALF])[:, :]) for i in range(3)])
        sp_ring = Ring([Buf(sb_in(attn, f"sp_tile{i}", [P, HALF])[:, :]) for i in range(3)])
        a_ring = Ring([Buf(sb_in(attn, f"a_tile{i}", [P, HALF])[:, :]) for i in range(3)])
        acc = [[Buf(sb_in(attn, f"acc{par}{i}", [P, HALF])[:, :]) for i in range(2)] for par in range(2)]
        zbanks = Ring([banks[i] for i in range(4)])
        yb_split = [[] for _ in range(4)]
        act.do(lambda e: e.preload_act_table_set("natural_log_exp_and_others"))

        def score(tile):
            j, par, g, kb, c0, n = tile["at"]
            z = tile["z"] = zbanks.take()
            pad, k = pads[j % 2][par], k_feat[j % 2]
            mark = mm_mark(z.ap[:, 0:n], k.ap[:, kb * P:(kb + 1) * P],
                           pad.ap[:, g * HALF + c0:(g + 1) * HALF], True, not tile["diag"],
                           z.busy, pad.ready, k.ready)
            if tile["diag"]:
                mark = mm_mark(z.ap[:, 0:P], ident_bf[:, :], causal_bf[:, :], False, True)
            pad.used(mark)
            k.used(mark)
            z.written(mark)

        def softplus(tile):
            n, z = tile["at"][5], tile["z"]
            e_t, sp_t = e_ring.take(), sp_ring.take()
            tile["sp"] = sp_t
            t1 = v_ts(e_t.ap[:, 0:n], z.ap[:, 0:n], EXACT_FROM, ALU.min, z.ready, e_t.busy)
            t2 = a_act(e_t.ap[:, 0:n], e_t.ap[:, 0:n], ACT.Exp, t1)
            t3 = a_act(e_t.ap[:, 0:n], e_t.ap[:, 0:n], ACT.Ln, t2, bias=1.0)
            tile["ln"] = (e_t, t3)

        def softplus_end(tile):
            n, z, sp_t = tile["at"][5], tile["z"], tile["sp"]
            e_t, t3 = tile["ln"]
            t4 = v_tt(sp_t.ap[:, 0:n], e_t.ap[:, 0:n], z.ap[:, 0:n], ALU.max, t3, sp_t.busy)
            e_t.written(t3)
            e_t.used(t4)
            sp_t.written(t4)
            z.ready = [t4]

        def sums(tile):
            j, par, g, kb, c0, n = tile["at"]
            z, sp_t = tile["z"], tile["sp"]
            old, new = acc[par]
            first = kb == 4 * g + 3
            wide = P if tile["diag"] else 0
            mark = mm_mark(z.ap[:, 0:n], const("minus_tri"), sp_t.ap[:, 0:n], False, first, sp_t.ready, z.ready)
            if not first:
                mark = mm_mark(z.ap[:, wide:n], const("minus_ones"), old.ap[:, c0 + wide:HALF], False, True, old.ready)
                old.used(mark)
            sp_t.used(mark)
            z.written(mark)
            if kb > 0:
                tokens = []
                if wide:
                    tokens.append(pool.mark(
                        lambda e: e.tensor_copy(new.ap[:, c0:c0 + P], sp_t.ap[:, 0:P]), sp_t.ready, new.busy))
                if not first:
                    tokens.append(g_tt(new.ap[:, c0 + wide:HALF], old.ap[:, c0 + wide:HALF], sp_t.ap[:, wide:n],
                                       ALU.add, sp_t.ready, old.ready, new.busy))
                    old.used(tokens[-1])
                sp_t.used(*tokens)
                new.written(*tokens)
                acc[par] = [new, old]

        def weigh(tile):
            n, z = tile["at"][5], tile["z"]
            a_t = tile["a"] = a_ring.take()
            t = a_act(a_t.ap[:, 0:n], z.ap[:, 0:n], ACT.Exp, z.ready, a_t.busy)
            z.used(t)
            a_t.written(t)

        def mix(tile):
            j, par, g, kb, c0, n = tile["at"]
            a_t, o, v = tile["a"], banks[4 + par], v_tok[j % 2]
            mark = mm_mark(o.ap[:, c0:HALF], v.ap[:, kb * P:(kb + 1) * P], a_t.ap[:, 0:n],
                           kb == 4 * g + 3, kb == 0, a_t.ready, v.ready, o.busy if kb == 4 * g + 3 else None)
            a_t.used(mark)
            v.used(mark)
            if kb == 0:
                o.written(mark)
                rows, cols = head_rows(par), slice(g * HALF, (g + 1) * HALF)
                made = split(yb_hi[rows, j, cols], yb_lo[rows, j, cols], o.ap[rows, :], mark)
                o.used(*made)
                yb_split[j] += made

        tiles = []
        for j in range(4):
            for g in range(NH):
                for kb in range(4 * g + 3, -1, -1):
                    for par in range(2):
                        c0 = max(0, kb - 4 * g) * P
                        tiles.append({"at": (j, par, g, kb, c0, HALF - c0), "diag": kb >= 4 * g})
        (ps_q, mark_q), (ps_k, mark_k) = first_qk
        h_used(mark_k)
        ps, mark = one("w_qkv", h_rhs())
        h_used(mark)
        take_q(0, ps_q, mark_q)
        take_k(0, ps_k, mark_k)
        for _ in take_v(0, ps, mark):
            pass
        filler = iter(())
        for i in range(len(tiles) + 4):
            if i < len(tiles):
                if i % (len(tiles) // 4) == 0:
                    for _ in filler:
                        pass
                    j = tiles[i]["at"][0]
                    filler = qkv_steps(j + 1) if j < 3 else iter(())
                score(tiles[i])
                softplus(tiles[i])
                next(filler, None)
            if 0 <= i - 1 < len(tiles):
                softplus_end(tiles[i - 1])
            if 0 <= i - 2 < len(tiles):
                sums(tiles[i - 2])
                weigh(tiles[i - 2])
            if 0 <= i - 4 < len(tiles):
                mix(tiles[i - 4])
        attn.close()

        free = fence()
        for q in (act, dve, pool):
            q.wait(free)
        ya_hi = sb_in(outer, "ya_hi", [P, 4, T], F32R)
        ya_lo = sb_in(outer, "ya_lo", [P, 4, T], F32R)
        pool_scope = ExitStack()
        PAD = 16
        u_mem = [sb_in(pool_scope, f"u_mem{i}", [P, PAD + T]) for i in range(3)]
        pl_hi = [Buf(sb_in(pool_scope, f"pl_hi{i}", [P, T], F32R)[:, :]) for i in range(2)]
        pl_lo = [Buf(sb_in(pool_scope, f"pl_lo{i}", [P, T], F32R)[:, :]) for i in range(2)]
        t_zero = [dve.mark((lambda o: lambda e: e.memset(o, 0.0))(u[:, 0:PAD])) for u in u_mem]
        u_busy = []
        ya_ready = []

        def map_group(g):
            hi, lo = pl_hi[g % 2], pl_lo[g % 2]
            ps, mark = one("w_pool", [(hi.ap, lo.ap, [hi.ready, lo.ready])], (0,))
            hi.used(mark)
            lo.used(mark)
            s = tmps.take()
            t = v_ts(s.ap, ps.ap, vec("pool_scale", g), ALU.mult, mark, s.busy)
            ps.used(t)
            s.written(t)
            made = split(ya_hi[:, g, :], ya_lo[:, g, :], s.ap, t)
            s.used(*made)
            ya_ready.append(made)

        for g, window in enumerate(WINDOWS):
            ps, mark = one("w_u", h_rhs())
            h_used(mark)
            u, a, b = u_mem
            t = unscale(u[:, PAD:], ps, mark, u_busy)
            ps.used(t)
            src, width = u, 1
            dst = a
            t = v_tt(dst[:, PAD:], src[:, PAD:], src[:, PAD - 1:PAD - 1 + T], ALU.add, t, t_zero)
            width = 2
            while width < window:
                src, dst = dst, (b if dst is a else a)
                t = v_tt(dst[:, PAD:], src[:, PAD:], src[:, PAD - width:PAD - width + T], ALU.add, t)
                width *= 2
            s = tmps.take()
            t1 = v_ts(s.ap, dst[:, PAD:], 1.0 / window, ALU.mult, t, s.busy)
            t1 = v_tt(s.ap[:, 0:window], dst[:, PAD:PAD + window],
                      consts[:, CONST["inv_count"] + 16 * g:CONST["inv_count"] + 16 * g + window], ALU.mult, t1)
            t1 = v_tt(s.ap, s.ap, u[:, PAD:], ALU.subtract, t1)
            s.written(t1)
            hi, lo = pl_hi[g % 2], pl_lo[g % 2]
            made = split(hi.ap, lo.ap, s.ap, t1, hi.busy, lo.busy)
            s.used(*made)
            hi.written(made[0])
            lo.written(made[1])
            u_busy = made
            if g > 0:
                map_group(g - 1)

        merged_ready = []

        def merged_to_h(k):
            t_hi = a_copy(h_hi[:, k, :], merged[:, k, :], merged_ready[k], h_busy[k])
            sub = g_tt if k % 3 == 2 else v_tt
            t_lo = sub(h_lo[:, k, :], merged[:, k, :], h_hi[:, k, :].bitcast(F32), ALU.subtract, t_hi, h_busy[k],
                       merged_ready[k])
            h_ready[k], h_busy[k] = [t_hi, t_lo], []

        rhs_b = [(yb_hi[:, k, :], yb_lo[:, k, :], yb_split[k]) for k in range(4)]
        for m in range(KD):
            products = [one("w_ga", h_rhs()), one("w_gb", h_rhs())]
            h_used(products[1][1])
            if m == 0:
                map_group(3)
                pool_scope.close()
                free = fence()
                dve.wait(free)
                merged = sb_in(outer, "merged", [P, KD, T])
            gates = []
            for ps, mark in products:
                g = tmps.take()
                t = unscale(g.ap, ps, mark, g.busy)
                ps.used(t)
                t = a_act(g.ap, g.ap, ACT.Sigmoid, t)
                g.written(t)
                gates.append(g)
            g_a, g_b = gates
            if m == KD - 1:
                for k in range(KD - 1):
                    merged_to_h(k)
            rhs_a = [(ya_hi[:, k, :], ya_lo[:, k, :], ya_ready[k]) for k in range(4)]
            ps, mark = one("w_ba", rhs_a, tuple(range(4)))
            t = v_tt(merged[:, m, :], g_a.ap, ps.ap, ALU.mult, mark, g_a.ready)
            ps.used(t)
            g_a.used(t)
            ps, mark = one("w_bb", rhs_b, tuple(range(4)))
            t2 = v_tt(g_b.ap, g_b.ap, ps.ap, ALU.mult, mark, g_b.ready)
            ps.used(t2)
            t3 = v_tt(merged[:, m, :], merged[:, m, :], g_b.ap, ALU.add, t, t2)
            g_b.used(t3)
            merged_ready.append(t3)

        merged_to_h(KD - 1)
        outer.close()
        free = fence()
        resident = ExitStack()
        x = load_x(resident, "x_block1", io["x"], free)

        total = SquareSum(norm_row)
        for m in range(KD):
            ps, mark = one("w_out", h_rhs())
            h_used(mark)
            t = v_tt(x[m].ap, x[m].ap, ps.ap, ALU.add, mark, x[m].ready)
            ps.used(t)
            x[m].written(t)
            x[m].used(total.add(x[m].ap, t))

        for k in range(KD):
            scaled_to_h(k, x[k], vec("norm_ffn", k))

        def feed_forward(names, activate, add, start):
            with ExitStack() as s:
                hid_hi = [sb_in(s, f"hid_hi_{names[0]}{i}", [P, FFN_GROUP, T], F32R) for i in range(2)]
                hid_lo = [sb_in(s, f"hid_lo_{names[0]}{i}", [P, FFN_GROUP, T], F32R) for i in range(2)]
                free = fence()
                act.wait(free)
                dve.wait(free)
                ready = [[None] * FFN_GROUP for _ in range(2)]
                busy = [[], []]
                for g in range(n_groups + 1):
                    if g < n_groups:
                        side = g % 2
                        for i in range(FFN_GROUP):
                            t = activate(g * FFN_GROUP + i, start if g + i == 0 else None)
                            made = split(hid_hi[side][:, i, :], hid_lo[side][:, i, :], t.ap, t.ready, busy[side])
                            t.used(*made)
                            ready[side][i] = made
                    if g > 0:
                        side = (g - 1) % 2
                        rhs = [(hid_hi[side][:, i, :], hid_lo[side][:, i, :], ready[side][i])
                               for i in range(FFN_GROUP)]
                        for half in range(2):
                            unit = weights.take("w_down")
                            weights.ahead()
                            for mi in range(4):
                                m = 4 * half + mi
                                ps, mark = one("w_down", rhs, tuple(mi * FFN_GROUP + i for i in range(FFN_GROUP)), unit)
                                add(g - 1, m, ps, mark)
                        busy[side] = [mark]

        def gated_chunk(i, start):
            if start:
                (ps, mark), (ps2, mark2) = two(("w_gate", "w_up"), h_rhs())
                start()
            else:
                ps, mark = one("w_gate", h_rhs())
            h_used(mark)
            s = tmps.take()
            t = unscale(s.ap, ps, mark, s.busy)
            ps.used(t)
            t = a_act(s.ap, s.ap, ACT.Silu, t)
            t = v_tt(s.ap, s.ap, norm_row.ap, ALU.mult, norm_row.ready, t)
            norm_row.used(t)
            if not start:
                ps2, mark2 = one("w_up", h_rhs())
            h_used(mark2)
            t = v_tt(s.ap, s.ap, ps2.ap, ALU.mult, mark2, t)
            ps2.used(t)
            s.written(t)
            return s

        def add_to_x(g, m, ps, mark):
            t = v_tt(x[m].ap, x[m].ap, ps.ap, ALU.add, mark, x[m].ready, x[m].busy)
            ps.used(t)
            x[m].written(t)
            if g == n_groups - 1:
                x[m].used(ple_total.add(x[m].ap, t))
                scaled_to_h(m, x[m], vec("norm_ple", m))

        ple = ExitStack()
        p_hi = sb_in(ple, "p_hi", [P, 2, T], F32R)
        p_lo = sb_in(ple, "p_lo", [P, 2, T], F32R)
        p_dma = Dma("dma_p")
        free = fence()
        rhs_p = []

        def cut_p(k):
            t = tmps.take()
            t_in = p_dma.start(sync, t.ap, io["p"][k], free, t.busy)
            made = split(p_hi[:, k, :], p_lo[:, k, :], t.ap, t_in)
            t.written(t_in)
            t.used(*made)
            rhs_p.append((p_hi[:, k, :], p_lo[:, k, :], made))

        ada = ExitStack()
        ada_raw = Ring([Buf(sb_in(ada, f"ada_raw{i}", [P, 1024])[:, :], free) for i in range(2)])
        ada_dma = [Dma(f"ada_dma{i}") for i in range(2)]
        ada_sum = Buf(sb_in(ada, "ada_sum", [P, 1024])[:, :], free)
        c_silu = sb_in(ada, "c_silu", [P, KD])
        t_c = a_act(c_silu[:, :], vec("c", 0, KD), ACT.Silu, free)
        mod_ready = []

        def modulation_steps():
            for part in range(6):
                for k in range(KD):
                    n = part * KD + k
                    raw = ada_raw.take()
                    t = ada_dma[n % 2].start(sync, raw.ap, io["w_ada"][part, k], raw.busy)
                    raw.written(t)
                    if k == 0:
                        t = v_ts(ada_sum.ap, raw.ap, c_silu[:, 0:1], ALU.mult, t, t_c, ada_sum.busy)
                    else:
                        t = v_stt(ada_sum.ap, raw.ap, c_silu[:, k:k + 1], ada_sum.ap, ALU.mult, ALU.add, t,
                                  ada_sum.ready)
                    raw.used(t)
                    ada_sum.written(t)
                    yield
                out = pairs.take()
                for j in range(KD):
                    mark = mm_mark(out.ap[:, j:j + 1], ada_sum.ap[:, j * P:(j + 1) * P], const("ones", 1), True, True,
                                   ada_sum.ready, out.busy)
                ada_sum.used(mark)
                out.written(mark)
                cols_ = slice(part * KD, (part + 1) * KD)
                t = v_tt(mod[:, cols_], out.ap[:, 0:KD], vec("b_ada", part * KD, KD), ALU.add, mark)
                out.used(t)
                mod_ready.append(t)

        modulation = modulation_steps()

        def gated_chunk_and_more(i, start):
            out = gated_chunk(i, start)
            if 0 < i < KF - 2:
                for _ in range(3):
                    next(modulation, None)
            if KF - 3 < i:
                cut_p(i - (KF - 2))
            return out

        def park(chunks, ks=range(KD)):
            done = []
            for k in ks:
                c = chunks[k]
                t = dma_x[k].start(sync, io["x_park"][k], c.ap, c.ready)
                c.used(t)
                done.append(t)
            return done

        parked = []
        ple_total = SquareSum(norm_row)
        feed_forward(("a",), gated_chunk_and_more, add_to_x, total.inverse)
        for _ in modulation:
            pass
        ada.close()
        t = v_stt(gain[:, 0:KD], mod[:, KD:2 * KD], 1.0, vec("pre_mix_g", 0, KD), ALU.add, ALU.mult, mod_ready)
        t = [v_tt(gain[:, 0:KD], gain[:, 0:KD], vec("norm_final", 0, KD), ALU.mult, t),
             v_tt(gain[:, KD:2 * KD], mod[:, 2 * KD:3 * KD], vec("post_mix_g", 0, KD), ALU.mult),
             v_stt(gain[:, 2 * KD:3 * KD], mod[:, 4 * KD:5 * KD], 1.0, vec("pre_ffn_g", 0, KD), ALU.add, ALU.mult),
             v_tt(gain[:, 3 * KD:4 * KD], mod[:, 5 * KD:6 * KD], vec("post_ffn_g", 0, KD), ALU.mult)]
        act.wait(t, mod_ready)
        dve.wait(t)

        free = fence()
        dve.wait(free)
        act.wait(free)
        pool.wait(free)
        row2 = Buf(sb_in(ple, "norm_row2", [P, T])[:, :])
        plain_row = Buf(sb_in(ple, "plain_row", [P, T])[:, :])
        final_total, next_total = SquareSum(plain_row), SquareSum(row2)
        emb = [Buf(sb_in(ple, f"emb{i}", [P, T])[:, :]) for i in range(4)]
        for m in range(KD):
            if m % 4 == 0:
                unit = weights.take("w_pp")
                weights.ahead()
                for mi in range(4):
                    ps, mark = one("w_pp", rhs_p, (2 * mi, 2 * mi + 1), unit)
                    t = a_copy(emb[mi].ap, ps.ap, mark, emb[mi].busy)
                    ps.used(t)
                    emb[mi].written(t)
            if m == 0:
                ple_total.inverse()
            ps, mark = one("w_pg", h_rhs())
            h_used(mark)
            s = tmps.take()
            t = unscale(s.ap, ps, mark, s.busy)
            ps.used(t)
            t = a_act(s.ap, s.ap, ACT.Sigmoid, t)
            t = v_tt(s.ap, s.ap, emb[m % 4].ap, ALU.mult, t, emb[m % 4].ready)
            emb[m % 4].used(t)
            t2 = v_tt(x[m].ap, x[m].ap, s.ap, ALU.add, t, x[m].ready, x[m].busy)
            s.written(t)
            s.used(t2)
            x[m].written(t2)
            x[m].used(final_total.add(x[m].ap, t2), next_total.add(x[m].ap, t2, vec("norm_final", m)))
            parked += park(x, [m])

        t = v_stt(row2.ap, plain_row.ap, EPS, row2.ap, ALU.mult, ALU.add, final_total.total, next_total.total)
        plain_row.busy = [t]
        next_total.inverse(eps=eps_col[:, 1:2], total=t)
        normed_to_h(x, row2, lambda k: gain[:, k:k + 1], lambda k: mod[:, k:k + 1])
        first_at = two(("w_qk_at", "w_qk_at"), h_rhs())
        row_dma = Dma("row_dma")
        parked.append(row_dma.start(sync, io["row_park"], plain_row.ap, final_total.total))
        ple.close()

        resident.close()
        free = fence() + parked
        for q in (act, dve, pool):
            q.wait(free)
        ml = ExitStack()
        W1 = ML_D + 1
        v_ml = sb_in(ml, "v_ml", [P, NB, ML_H, W1])
        sig_o = [Buf(sb_in(ml, f"sig_o{i}", [P, T])[:, :]) for i in range(ML_H)]
        gate_cols = sb_in(ml, "gate_cols", [P, 4, 32])
        decay = sb_in(ml, "decay", [P, 32])
        gates_raw = sb_in(ml, "gates_raw", [36, T])
        t_ones = pool.mark(lambda e: e.memset(v_ml[:, :, :, ML_D:W1], 1.0))
        v_ml_ready = [t_ones]

        at = ExitStack()
        q_at = [Buf(sb_in(at, f"q_at{i}", [P, T])[:, :]) for i in range(4)]
        k_pad = [[Buf(sb_in(at, f"k_pad{g}{par}", [P, T])[:, :]) for par in range(2)] for g in range(AT_KV)]
        v_at = Buf(sb_in(at, "v_at", [P, T])[:, :])
        turn = ExitStack()
        rope_mem = sb_in(turn, "rope_mem", [P, 2 * T])
        dma_rope = Dma("dma_rope")
        t_rope = load(dma_rope, rope_mem[:, :], io["rope"], free)
        rope_in = Ring([Buf(sb_in(turn, f"rope_in{i}", [P, T])[:, :]) for i in range(2)])
        pad_zeros = []
        for g in range(AT_KV):
            for par in range(2):
                pad_zeros.append(dve.mark((lambda o: lambda e: e.memset(o, 0.0))(k_pad[g][par].ap[head_rows(1 - par), :])))

        def rotate(s, ps, mark):
            raw = rope_in.take()
            t = a_copy(raw.ap, ps.ap, mark, raw.busy)
            ps.used(t)
            raw.written(t)
            rot = pairs.take()
            for half in range(NH):
                cols = slice(half * HALF, (half + 1) * HALF)
                mark = mm_mark(rot.half(half), const("rotate"), raw.ap[:, cols], True, True, t, rot.busy)
            rot.written(mark)
            w = tmps.take()
            t_s = v_tt(w.ap, rot.ap, rope_mem[:, T:2 * T], ALU.mult, mark, t_rope, w.busy)
            rot.used(t_s)
            t_c = g_tt(raw.ap, raw.ap, rope_mem[:, 0:T], ALU.mult, mark, t, t_rope)
            if s < 4:
                t = v_tt(q_at[s].ap, raw.ap, w.ap, ALU.add, t_s, t_c)
                q_at[s].written(t)
            else:
                t = v_tt(w.ap, raw.ap, w.ap, ALU.add, t_s, t_c)
                for g in range(AT_KV):
                    for par in range(2):
                        pad = k_pad[g][par]
                        t1 = v_copy(pad.ap[head_rows(par), :], w.ap[head_rows(g), :], t)
                        pad.written(pad_zeros, t1)
                t = t1
            raw.written(t_c)
            raw.used(t)
            w.written(t_s)
            w.used(t)

        def turn_steps(ps, mark, turned, write):
            f = tmps.take()
            t = a_copy(f.ap, ps.ap, mark, f.busy)
            ps.used(t)
            f.written(t)
            yield
            for b in range(NB):
                mark = transpose(turned.ap[:, b * P:(b + 1) * P], f.ap[:, b * P:(b + 1) * P], t, turned.busy)
            f.used(mark)
            turned.written(mark)
            turned.used(write(turned.ap.rearrange("p (b d) -> p b d", b=NB), mark))

        for s in range(5):
            ps, mark = first_at[s] if s < 2 else one("w_qk_at", h_rhs())
            h_used(mark)
            if s > 0:
                rotate(s - 1, *previous)
            previous = (ps, mark)
        ps, mark = one("w_v_at", h_rhs())
        h_used(mark)
        rotate(4, *previous)
        for _ in turn_steps(ps, mark, pairs.take(), lambda ap, m: v_at.written(
                a_copy(v_at.ap.rearrange("p (b d) -> p b d", b=NB), ap, m)) or v_at.ready[0]):
            pass
        turn.close()

        def value_and_gate_steps():
            for s in range(8, 17):
                unit = weights.take("w_ml" if s < 16 else "w_gates")
                weights.ahead()
                ps = proj_pair
                yield from project_steps(ps, unit, tuple(range(KD)), h_rhs(), ps.busy)
                mark = ps.ready[0]
                h_used(mark)
                if s < 12:
                    yield from turn_steps(ps, mark, ps, lambda ap, m: v_ml_ready.append(
                        a_copy(v_ml[:, :, s - 8, 0:ML_D], ap, m)) or v_ml_ready[-1])
                elif s < 16:
                    t = a_copy(sig_o[s - 12].ap, ps.ap, mark)
                    ps.used(t)
                    sig_o[s - 12].written(t)
                else:
                    t = a_copy(gates_raw[:, :], ps.ap[0:36, :], mark)
                    ps.used(t)
                    gates_raw_ready.append(t)

        gates_raw_ready = []
        filler = value_and_gate_steps()

        at_scale = AT_DIM ** -0.5
        free = fence()
        for q in (act, dve):
            q.wait(free)
        HG = AT_H // AT_KV
        prob = [[Buf(sb_in(at, f"prob{i}{h}", [P, 2 * P])[:, :]) for h in range(HG)] for i in range(2)]
        prob_t = Ring([Buf(sb_in(at, f"prob_t{i}", [P, 4 * P])[:, :]) for i in range(2)])
        o_tok = Ring([Buf(sb_in(at, f"o_tok{i}", [P, D_SB])[:, :]) for i in range(2)])
        o_out = Ring([Buf(sb_in(at, f"o_out{i}", [P, 4, P])[:, :, :]) for i in range(2)])
        sq_tok = Buf(sb_in(at, "sq_tok", [P, D_SB])[:, :])
        small_mem = sb_in(at, "at_small", [P, 2, 6, AT_H])
        smalls = [Buf(small_mem[:, i]) for i in range(2)]
        pt_banks, o_bank, turn_bank = Ring([banks[2], banks[3]]), banks[4], banks[5]
        o_dma = [Dma(f"o_dma{i}") for i in range(2)]
        o_parked = []

        def attend_scores(n, g):
            first = P if n == 0 else 0
            k0, width = (n - 1) * P + first, 2 * P - first
            sm = smalls[n % 2]
            hs = slice(g * HG, (g + 1) * HG)
            row_max, neg_max, row_sum, sink_e = (sm.ap[:, i, hs] for i in range(4))
            ts = []
            for hh in range(HG):
                h = g * HG + hh
                bank, off = banks[hh // 2], (hh % 2) * 2 * P
                pad = k_pad[g][h % 2]
                s_ap = bank.ap[:, off:off + width]
                mm(s_ap, q_at[h // 2].ap[:, n * P:(n + 1) * P], pad.ap[:, k0:k0 + width], True, False,
                   q_at[h // 2].ready, pad.ready, bank.busy if hh % 2 == 0 else None)
                mark = mm_mark(s_ap, ident_bf[:, :], band_bf[:, first:2 * P], False, True)
                if hh % 2:
                    bank.written(mark)
                    s3 = bank.ap.rearrange("p (a c) -> p a c", a=2)[:, :, 0:width]
                    t = dve.mark((lambda o, i: lambda e: e.tensor_reduce(o, i, AX.X, ALU.max))(
                        row_max[:, hh - 1:hh + 1], s3), mark, sm.busy)
                    bank.ready = [t]
                    ts.append(t)
            sinks = vec("sinks", g * HG, HG)
            t = v_stt(neg_max, row_max, at_scale, sinks, ALU.mult, ALU.max, ts)
            t_sk = v_tt(sink_e, sinks, neg_max, ALU.subtract, t)
            t_m = v_ts(neg_max, neg_max, -1.0, ALU.mult, t, t_sk)
            t_sk = a_act(sink_e, sink_e, ACT.Exp, t_sk)
            exps = [t_sk]
            for hh in range(HG):
                bank, off, pr = banks[hh // 2], (hh % 2) * 2 * P, prob[g][hh]
                t = act.mark((lambda o, i, b, a: lambda e: e.activation(o, i, ACT.Exp, bias=b, scale=at_scale,
                                                                         accum_out=a))(
                    pr.ap[:, 0:width], bank.ap[:, off:off + width], neg_max[:, hh:hh + 1], row_sum[:, hh:hh + 1]),
                    bank.ready, t_m, pr.busy)
                bank.used(t)
                pr.written(t)
                exps.append(t)
            return exps

        def attend_mix(n, g):
            first = P if n == 0 else 0
            k0, width = (n - 1) * P + first, 2 * P - first
            kbs = range(width // P)
            for hp in range(HG // 2):
                bank, pt = pt_banks.take(), prob_t.take()
                for hh in range(2):
                    pr = prob[g][2 * hp + hh]
                    for kb in kbs:
                        mark = transpose(bank.ap[:, hh * 2 * P + kb * P:hh * 2 * P + (kb + 1) * P],
                                         pr.ap[:, kb * P:(kb + 1) * P], pr.ready, bank.busy)
                    pr.used(mark)
                bank.written(mark)
                i3, o3 = (x_.rearrange("p (a c) -> p a c", a=2)[:, :, 0:width] for x_ in (bank.ap, pt.ap))
                t = (a_copy if hp % 2 else v_copy)(o3, i3, mark, pt.busy)
                bank.used(t)
                pt.written(t)
                next(filler, None)
                for hh in range(2):
                    h = g * HG + 2 * hp + hh
                    for kb in kbs:
                        vb = (k0 // P + kb) * P + g * AT_DIM
                        mark = mm_mark(o_bank.ap[:, h * AT_DIM:(h + 1) * AT_DIM],
                                       pt.ap[:, hh * 2 * P + kb * P:hh * 2 * P + (kb + 1) * P],
                                       v_at.ap[:, vb:vb + AT_DIM], kb == 0, kb == kbs[-1], t, v_at.ready,
                                       o_bank.busy if h == 0 else None)
                pt.used(mark)
            return mark

        def attend_norm(n, mark, exps):
            sm, o = smalls[n % 2], o_tok.take()
            row_sum, sink_e, den, ssq = (sm.ap[:, i] for i in (2, 3, 4, 5))
            o_bank.written(mark)
            t = v_tt(den, row_sum, sink_e, ALU.add, exps)
            t = dve.mark(lambda e: e.reciprocal(den, den), t)
            t_o = v_tt(o.ap.rearrange("p (h d) -> p h d", h=AT_H), o_bank.ap.rearrange("p (h d) -> p h d", h=AT_H),
                       den.unsqueeze(2).to_broadcast([P, AT_H, AT_DIM]), ALU.mult, t, mark, o.busy)
            o_bank.used(t_o)
            t = act.mark(lambda e: e.activation(sq_tok.ap, o.ap, ACT.Square, accum_out=ssq[:, 0:1]),
                         t_o, sq_tok.ready)
            sq_tok.written(t)
            t = a_act(ssq[:, 1:2], ssq[:, 0:1], ACT.Ln, t, bias=eps_col[:, 0:1], scale=1.0 / D_SB)
            t = a_act(ssq[:, 2:3], ssq[:, 1:2], ACT.Exp, t, scale=-0.5)
            t = v_ts(o.ap, o.ap, ssq[:, 2:3], ALU.mult, t)
            sm.busy = [t]
            o.written(t)
            return o

        def attend_out(n, o):
            out = o_out.take()
            for j in range(4):
                mark = transpose(turn_bank.ap[:, j * P:(j + 1) * P], o.ap[:, j * P:(j + 1) * P], o.ready,
                                 turn_bank.busy)
            o.used(mark)
            turn_bank.written(mark)
            ts = []
            for j in range(4):
                ts.append(v_ts(out.ap[:, j, :], turn_bank.ap[:, j * P:(j + 1) * P], vec("attn_norm_g", j),
                               ALU.mult, mark, out.busy))
            turn_bank.used(*ts)
            t = o_dma[n % 2].start(sync, io["o_park"].rearrange("j p t -> p j t")[:, :, n * P:(n + 1) * P], out.ap, ts)
            out.written(*ts)
            out.used(t)
            o_parked.append(t)

        act.do(lambda e: e.preload_act_table_set("natural_log_exp_and_others"))
        steps = [(n, g) for n in range(NB) for g in range(AT_KV)]
        exps = attend_scores(*steps[0])
        normed, waiting = None, []
        for i, (n, g) in enumerate(steps):
            waiting = (waiting if g else []) + exps
            next(filler, None)
            next(filler, None)
            mark = attend_mix(n, g)
            if i + 1 < len(steps):
                exps = attend_scores(*steps[i + 1])
            if g == AT_KV - 1:
                if normed:
                    attend_out(*normed)
                normed = (n, attend_norm(n, mark, waiting))
            next(filler, None)
            if i % 2:
                next(filler, None)
        attend_out(*normed)
        for _ in filler:
            pass
        at.close()

        free = fence() + o_parked[-2:]
        for q in (act, dve, pool):
            q.wait(free)
        q_ml = [Buf(sb_in(ml, f"q_ml{i}", [P, T])[:, :]) for i in range(ML_H)]
        k_ml = [Buf(sb_in(ml, f"k_ml{i}", [P, T])[:, :]) for i in range(ML_H)]
        conv = ExitStack()
        CP = ML_CONV - 1
        conv_in = Ring([Buf(sb_in(conv, f"conv_in{i}", [P, CP + T])[:, :]) for i in range(2)])
        for b in conv_in.bufs:
            b.zero = dve.mark((lambda o: lambda e: e.memset(o, 0.0))(b.ap[:, 0:CP]))

        def conv_taps(src, dst, taps, weight, bias, *w):
            t = v_ts(dst.ap, src.ap[:, 0:T], weight(0), ALU.mult, *w, s2=bias, op1=ALU.add)
            for i in range(1, taps):
                t = v_stt(dst.ap, src.ap[:, i:i + T], weight(i), dst.ap, ALU.mult, ALU.add, t)
            return t

        gate_e = sb_in(conv, "gate_e", [36, T])
        g_mem = sb_in(conv, "gate_mem", [32, 8, P])
        g_small = sb_in(conv, "gate_small", [32, 16])
        m_mem = sb_in(conv, "m_mem", [4, 64])
        gate_tokens = []

        def gate_steps():
            F = slice(32, 36)
            t_i = v_ts(gates_raw[0:4, :], gates_raw[0:4, :], vec("gate_b")[0:4, :], ALU.add, gates_raw_ready)
            t_f = v_ts(gates_raw[F, :], gates_raw[F, :], vec("gate_b")[F, :], ALU.add, gates_raw_ready,
                       s2=-1.0, op1=ALU.mult)
            t = v_ts(gate_e[F, :], gates_raw[F, :], EXACT_FROM, ALU.min, t_f)
            act.do(lambda e: e.preload_act_table_set("natural_log_exp_and_others"))
            t = a_act(gate_e[F, :], gate_e[F, :], ACT.Exp, t)
            t = a_act(gate_e[F, :], gate_e[F, :], ACT.Ln, t, bias=1.0)
            t_f = v_tt(gates_raw[F, :], gate_e[F, :], gates_raw[F, :], ALU.max, t)
            dma_g = Dma("dma_gates")
            dma_g.start(sync, io["gate_i"], gates_raw[0:4, :], t_i)
            t = dma_g.start(sync, io["gate_f"], gates_raw[F, :], t_f)
            yield
            dma_g.start(sync, g_mem[:, 0, :], io["gate_i"].rearrange("h (c t) -> (h c) t", t=P), t)
            t_g = dma_g.start(sync, g_mem[:, 1, :], io["gate_f"].rearrange("h (c t) -> (h c) t", t=P))
            yield
            I, NF, B, G, CM, M, W, X = (g_mem[:, i, :] for i in range(8))
            t_one = dve.mark(lambda e: e.memset(X, 1.0))
            t = dve.mark(lambda e: e.tensor_tensor_scan(B, X, NF, 0.0, ALU.mult, ALU.subtract), t_g, t_one)
            t = v_tt(G, I, B, ALU.subtract, t)
            t_cm = dve.mark(lambda e: e.tensor_tensor_scan(CM, X, G, -3e38, ALU.mult, ALU.max), t)
            t1 = v_copy(g_small[:, 0:1], CM[:, P - 1:P], t_cm)
            t2 = v_copy(g_small[:, 1:2], B[:, P - 1:P], t_cm)
            dma_g.start(sync, io["chunk_end"][0].rearrange("(r o) -> r o", o=1), g_small[:, 0:1], t1)
            t = dma_g.start(sync, io["chunk_end"][1].rearrange("(r o) -> r o", o=1), g_small[:, 1:2], t2)
            yield
            dma_g.start(sync, m_mem[:, 0:8], io["chunk_end"][0:1, :].rearrange("a (h c) -> (a h) c", c=8), t)
            t = dma_g.start(sync, m_mem[:, 8:16], io["chunk_end"][1:2, :].rearrange("a (h c) -> (a h) c", c=8))
            yield
            t0 = dve.mark(lambda e: e.memset(m_mem[:, 16:17], 0.0))
            t = dve.mark(lambda e: e.tensor_tensor_scan(m_mem[:, 17:25], m_mem[:, 0:8], m_mem[:, 8:16], 0.0,
                                                        ALU.max, ALU.add), t, t0)
            dma_g.start(sync, io["chunk_m"][0], m_mem[:, 16:24], t)
            t = dma_g.start(sync, io["chunk_m"][1], m_mem[:, 17:25])
            yield
            dma_g.start(sync, g_small[:, 2:3], io["chunk_m"][0].rearrange("h (c o) -> (h c) o", o=1), t)
            t = dma_g.start(sync, g_small[:, 3:4], io["chunk_m"][1].rearrange("h (c o) -> (h c) o", o=1))
            yield
            m_old, m_new, end_b, shift_c, dec = (g_small[:, i:i + 1] for i in (2, 3, 1, 4, 5))
            t_M = v_ts(M, CM, m_old, ALU.max, t)
            t_m_dram = Dma("dma_m_rows").start(sync, io["m_rows"], M, t_M)
            t_w = a_act(W, M, ACT.Exp, t_M, bias=m_old, scale=-1.0)
            t = v_tt(NF, B, M, ALU.add, t_M)
            t_nm = a_act(NF, NF, ACT.Exp, t, scale=-1.0)
            t = v_tt(shift_c, end_b, m_new, ALU.subtract, t_M)
            t_ws = a_act(I, G, ACT.Exp, t, bias=shift_c)
            t_d = a_act(dec, shift_c, ACT.Exp, t, bias=m_old)
            t = dma_g.start(sync, io["decay_row"].rearrange("(r o) -> r o", o=1), dec, t_d)
            yield
            t_dec = dma_g.start(sync, decay[:, :], io["decay_row"].partition_broadcast(P), t)
            out = pairs.take()
            for i, (row, tok) in enumerate(((G, t_cm), (W, t_w), (NF, t_nm), (I, t_ws))):
                mark = transpose(out.ap[:, 32 * i:32 * i + 32], row, tok, out.busy, rows=32)
            out.written(mark)
            t_cols = v_copy(gate_cols[:, :, :].rearrange("p a b -> p (a b)"), out.ap[:, 0:128], mark)
            out.used(t_cols)
            gate_tokens.extend([t_m_dram, t_dec, t_cols])

        gating = gate_steps()
        for s in range(8):
            ps, mark = one("w_ml", h_rhs())
            h_used(mark)
            src, acc_ = conv_in.take(), tmps.take()
            t = a_copy(src.ap[:, CP:], ps.ap, mark, src.busy)
            ps.used(t)
            next(gating, None)
            t1 = conv_taps(src, acc_, ML_CONV, lambda i: vec("ml_conv_w", 8 * i + s), vec("ml_conv_b", s),
                           t, src.zero, acc_.busy)
            src.written(t)
            src.used(t1)
            out = q_ml[s] if s < 4 else k_ml[s - 4]
            t = a_act(out.ap, acc_.ap, ACT.Silu, t1)
            acc_.written(t1)
            acc_.used(t)
            out.written(t)
        for _ in gating:
            pass
        for b in sig_o:
            b.written(a_act(b.ap, b.ap, ACT.Sigmoid, b.ready))
        for j in range(4):
            t = tmps.take()
            t_in = o_dma[j % 2].start(sync, t.ap, io["o_park"][j], t.busy, o_parked[-2:])
            made = split(h_hi[:, 4 + j, :], h_lo[:, 4 + j, :], t.ap, t_in, h_busy[4 + j])
            t.written(t_in)
            t.used(*made)
            h_ready[4 + j], h_busy[4 + j] = made, []
        conv.close()

        free = fence() + gate_tokens
        for q in (act, dve, pool):
            q.wait(free)
        state = Buf(sb_in(ml, "state", [P, ML_H, W1])[:, :, :])
        state.written(pool.mark(lambda e: e.memset(state.ap, 0.0)))

        def ring(name, shape, n=2):
            return Ring([Buf(sb_in(ml, f"{name}{i}", shape)[tuple(slice(None) for _ in shape)]) for i in range(n)])

        d_ring = ring("d_tile", [P, ML_H, P])
        p_ring = ring("p_tile", [P, ML_H, P])
        kt_ring = ring("k_tok", [P, ML_H, P])
        vw_ring = ring("v_weighted", [P, ML_H, W1])
        num_ring = ring("num", [P, ML_H, W1])
        sq_ring = ring("num_sq", [P, ML_H, P], 1)
        hn_ring = ring("h_norm", [P, ML_H, P])
        sml_ring = ring("ml_small", [P, 4, ML_H])
        d_dma = [Dma(f"d_dma{i}") for i in range(2)]
        s_bank, tr_bank = banks[0], banks[7]
        k_scale = ML_D ** -0.5
        later = const("later_neg").unsqueeze(1).to_broadcast([P, ML_H, P])
        m_rows = io["m_rows"].rearrange("(h c) t -> c h t", c=NB)
        act.do(lambda e: e.preload_act_table_set("natural_log_exp_and_others"))

        def chunk_cols(kind, c, n):
            v = gate_cols[:, kind, :].rearrange("p (h c) -> p h c", c=NB)[:, :, c:c + 1]
            return v if n == 1 else v.to_broadcast([P, ML_H, n])

        def tokens_of(c):
            return slice(c * P, (c + 1) * P)

        def four(first_bank, lhsT, rhs, *w):
            mark = None
            for h in range(ML_H):
                bank = banks[first_bank + h // 2]
                mark = mm_mark(bank.ap[:, (h % 2) * W1:(h % 2 + 1) * W1], lhsT(h), rhs(h), True, True,
                               bank.busy if h % 2 == 0 else None, *w)
                if h % 2:
                    bank.written(mark)
            return mark

        def chunk_weights(c):
            d = d_ring.take()
            t = d_dma[c % 2].start(sync, d.ap, m_rows[c].partition_broadcast(P), d.busy, free)
            t = g_tt(d.ap, later, d.ap, ALU.subtract, t)
            t = v_tt(d.ap, d.ap, chunk_cols(0, c, P), ALU.add, t)
            d.written(a_act(d.ap, d.ap, ACT.Exp, t))
            return d

        def chunk_scores(c, d):
            tok = tokens_of(c)
            for h in range(ML_H):
                mark = mm_mark(s_bank.ap[:, h * P:(h + 1) * P], k_ml[h].ap[:, tok], q_ml[h].ap[:, tok], True, True,
                               s_bank.busy, k_ml[h].ready, q_ml[h].ready)
            s_bank.written(mark)
            p = p_ring.take()
            t = v_stt(p.ap, s_bank.ap.rearrange("p (h t) -> p h t", h=ML_H), k_scale, d.ap, ALU.mult, ALU.mult,
                      mark, d.ready, p.busy)
            s_bank.used(t)
            d.used(t)
            p.written(t)
            for h in range(ML_H):
                mark = transpose(tr_bank.ap[:, h * P:(h + 1) * P], k_ml[h].ap[:, tok], tr_bank.busy)
            tr_bank.written(mark)
            kt = kt_ring.take()
            t = act.mark((lambda o, i: lambda e: e.activation(o, i, ACT.Copy, scale=k_scale))(
                kt.ap.rearrange("p h t -> p (h t)"), tr_bank.ap), mark, kt.busy)
            tr_bank.used(t)
            kt.written(t)
            vw = vw_ring.take()
            t = g_tt(vw.ap, v_ml[:, c, :, :], chunk_cols(3, c, W1), ALU.mult, v_ml_ready, vw.busy)
            vw.written(t)
            return p, kt, vw

        def chunk_sums(c, p, kt, vw):
            tok = tokens_of(c)
            t_inter = four(3, lambda h: q_ml[h].ap[:, tok], lambda h: state.ap[:, h, :], state.ready)
            state.used(t_inter)
            t_next = four(5, lambda h: kt.ap[:, h, :], lambda h: vw.ap[:, h, :], kt.ready, vw.ready)
            t_intra = four(1, lambda h: p.ap[:, h, :], lambda h: v_ml[:, c, h, :], p.ready, v_ml_ready)
            kt.used(t_next)
            vw.used(t_next)
            p.used(t_intra)
            num = num_ring.take()
            ts = []
            for h in range(ML_H):
                bank = banks[3 + h // 2]
                t = act.mark((lambda o, i, s: lambda e: e.activation(o, i, ACT.Copy, scale=s))(
                    num.ap[:, h, :], bank.ap[:, (h % 2) * W1:(h % 2 + 1) * W1],
                    gate_cols[:, 1, h * NB + c:h * NB + c + 1]), t_inter, num.busy)
                bank.used(t)
                ts.append(t)
            t_st = []
            for h in range(ML_H):
                bank = banks[5 + h // 2]
                t = v_stt(state.ap[:, h, :], state.ap[:, h, :], decay[:, h * NB + c:h * NB + c + 1],
                          bank.ap[:, (h % 2) * W1:(h % 2 + 1) * W1], ALU.mult, ALU.add, t_next, state.busy, state.ready)
                bank.used(t)
                t_st.append(t)
            state.written(*t_st)
            t_n = []
            for b in range(2):
                bank = banks[1 + b]
                part = num.ap[:, 2 * b:2 * b + 2, :]
                t = v_tt(part, part, bank.ap[:, 0:2 * W1].rearrange("p (h w) -> p h w", h=2), ALU.add, ts, t_intra)
                bank.used(t)
                t_n.append(t)
            num.written(*t_n)
            return num

        def chunk_norm(c, num):
            sml = sml_ring.take()
            den_c = num.ap[:, :, ML_D:W1]
            dn, r, ss, sc = (sml.ap[:, i, :] for i in range(4))

            def as3(a):
                return a.unsqueeze(2)

            sq = sq_ring.take()
            t_sq = a_act(sq.ap, num.ap[:, :, 0:ML_D], ACT.Square, num.ready, sq.busy)
            t = v_stt(as3(dn), den_c, -1.0, den_c, ALU.mult, ALU.max, num.ready, sml.busy)
            t = v_tt(as3(dn), as3(dn), chunk_cols(2, c, 1), ALU.max, t)
            t_r = dve.mark((lambda o, i: lambda e: e.reciprocal(o, i))(r, dn), t)
            t_rr = v_tt(sc, r, r, ALU.mult, t_r)
            t = dve.mark((lambda o, i: lambda e: e.tensor_reduce(o, i, AX.X, ALU.add))(ss, sq.ap), t_sq)
            sq.written(t_sq)
            sq.used(t)
            t = v_tt(ss, ss, sc, ALU.mult, t, t_rr)
            t = a_act(ss, ss, ACT.Ln, t, bias=eps_col[:, 0:1], scale=1.0 / ML_D)
            t = a_act(ss, ss, ACT.Exp, t, scale=-0.5)
            return sml, t

        def chunk_out(c, num, sml, t):
            hn = hn_ring.take()
            r, ss, sc = (sml.ap[:, i, :] for i in (1, 2, 3))
            t = v_tt(sc, ss, r, ALU.mult, t)
            t = v_tt(hn.ap, num.ap[:, :, 0:ML_D], sc.unsqueeze(2).to_broadcast([P, ML_H, ML_D]), ALU.mult, t, hn.busy)
            hn.written(t)
            sml.busy = [t]
            num.used(t)
            for h in range(ML_H):
                mark = transpose(tr_bank.ap[:, h * P:(h + 1) * P], hn.ap[:, h, :], hn.ready, tr_bank.busy)
            tr_bank.written(mark)
            ts = []
            tok = tokens_of(c)
            for h in range(ML_H):
                ts.append(v_stt(hn.ap[:, h, :], tr_bank.ap[:, h * P:(h + 1) * P], vec("ml_norm_g", h),
                                sig_o[h].ap[:, tok], ALU.mult, ALU.mult, mark, sig_o[h].ready))
            tr_bank.used(*ts)
            t_hi = a_copy(h_hi[:, 0:ML_H, tok], hn.ap, ts, h_busy[0])
            t_lo = g_tt(h_lo[:, 0:ML_H, tok], hn.ap, h_hi[:, 0:ML_H, tok].bitcast(F32), ALU.subtract, t_hi, ts)
            hn.used(t_hi, t_lo)
            for k in range(ML_H):
                h_parts[k] += [t_hi, t_lo]

        h_parts = [[] for _ in range(ML_H)]
        d = [chunk_weights(0), chunk_weights(1)]
        parts = chunk_scores(0, d[0])
        last = None
        for c in range(NB):
            num = chunk_sums(c, *parts)
            if c + 1 < NB:
                parts = chunk_scores(c + 1, d[(c + 1) % 2])
            if c + 2 < NB:
                d[c % 2] = chunk_weights(c + 2)
            sml, t = chunk_norm(c, num)
            if last:
                chunk_out(*last)
            last = (c, num, sml, t)
        chunk_out(*last)
        ml.close()
        for k in range(ML_H):
            h_ready[k], h_busy[k] = h_parts[k], []

        def normed_sum(y, x, g0, total, done):
            total.inverse()
            for k in range(KD):
                t = tmps.take()
                t1 = v_stt(t.ap, y[k].ap, gain[:, g0 + k:g0 + k + 1], norm_row.ap, ALU.mult, ALU.mult,
                           y[k].ready, norm_row.ready, t.busy)
                norm_row.used(t1)
                add = g_tt if k % 3 == 2 else v_tt
                t2 = add(x[k].ap, x[k].ap, t.ap, ALU.add, t1, x[k].ready, x[k].busy)
                t.written(t1)
                t.used(t2)
                x[k].written(t2)
                done(k)

        ys = ExitStack()
        free = fence()
        for q in (act, dve, pool):
            q.wait(free)
        y_mem = sb_in(ys, "y_mem", [P, KD, T])
        y = [Buf(y_mem[:, k, :]) for k in range(KD)]
        xs = ExitStack()
        next_row = Buf(sb_in(xs, "next_row", [P, T])[:, :])
        x = load_x(xs, "x_mid", io["x_park"], free + parked)
        plain_row = Buf(sb_in(xs, "plain_row_back", [P, T])[:, :])
        t_row = row_dma.start(sync, plain_row.ap, io["row_park"], free, parked)
        total = SquareSum(norm_row)
        order = (4, 5, 6, 7, 0, 1, 2, 3)
        for m in range(KD):
            ps, mark = one("w_out2", h_rhs(order), order)
            h_used(mark)
            t = a_copy(y[m].ap, ps.ap, mark)
            ps.used(t)
            y[m].written(t)
            y[m].used(total.add(y[m].ap, t))
            if m == 0:
                SquareSum(plain_row).inverse(total=t_row)
            t = v_stt(x[m].ap, x[m].ap, vec("norm_final", m), plain_row.ap, ALU.mult, ALU.mult,
                      x[m].ready, plain_row.ready)
            x[m].written(t)
        next_total = SquareSum(next_row)
        normed_sum(y, x, KD, total, lambda k: x[k].used(next_total.add(x[k].ap, x[k].ready)))
        next_total.inverse()
        normed_to_h(x, next_row, lambda k: gain[:, 2 * KD + k:2 * KD + k + 1],
                    lambda k: mod[:, 3 * KD + k:3 * KD + k + 1])
        first_ffn = two(("w_gate2", "w_up2"), h_rhs())
        parked = park(x)
        xs.close()

        ff = ExitStack()
        free = fence() + parked
        act.wait(free)
        dve.wait(free)
        FP = FFN_CONV - 1
        conv_in = Ring([Buf(sb_in(ff, f"ffn_conv_in{i}", [P, FP + T])[:, :]) for i in range(2)])
        val = Ring([Buf(sb_in(ff, "ffn_value", [P, T])[:, :])])
        for b in conv_in.bufs:
            b.zero = dve.mark((lambda o: lambda e: e.memset(o, 0.0))(b.ap[:, 0:FP]))

        def convolved_chunk(i, start):
            outs = []
            for n, (name, c, ring_) in enumerate((("w_gate2", i, tmps), ("w_up2", KF + i, val))):
                ps, mark = first_ffn[n] if i == 0 else one(name, h_rhs())
                h_used(mark)
                src, dst = conv_in.take(), ring_.take()
                t = a_copy(src.ap[:, FP:], ps.ap, mark, src.busy)
                ps.used(t)
                t1 = conv_taps(src, dst, FFN_CONV, lambda j: vec("ffn_conv_w", 2 * KF * j + c), vec("ffn_conv_b", c),
                               t, src.zero, dst.busy)
                src.written(t)
                src.used(t1)
                dst.written(t1)
                if name == "w_gate2":
                    t1 = a_act(dst.ap, dst.ap, ACT.Gelu_apprx_tanh, t1)
                    dst.written(t1)
                outs.append(dst)
            a, b = outs
            t = v_tt(a.ap, a.ap, b.ap, ALU.mult, a.ready, b.ready)
            b.used(t)
            a.written(t)
            return a

        def add_to_y(g, m, ps, mark):
            if g == 0:
                t = a_copy(y[m].ap, ps.ap, mark, y[m].busy, y[m].ready)
            else:
                t = v_tt(y[m].ap, y[m].ap, ps.ap, ALU.add, mark, y[m].ready)
            ps.used(t)
            y[m].written(t)
            if g == n_groups - 1:
                y[m].used(total.add(y[m].ap, t))

        total = SquareSum(norm_row)
        feed_forward(("b",), convolved_chunk, add_to_y, None)
        ff.close()
        xs = ExitStack()
        x = load_x(xs, "x_last", io["x_park"], fence() + parked)
        done = []
        normed_sum(y, x, 3 * KD, total,
                   lambda k: done.append(out_dma.start(sync, io["out"][k], x[k].ap, x[k].ready)))
        sync.wait(done[-1])
        xs.close()
        ys.close()
        return play(nc, sync, act, dve, pe, pool)


def play(nc, sync, act, dve, pe, pool):
    with nc.Block() as block:
        @block.sync
        def _(e):
            sync.play(e)

        @block.scalar
        def _(e):
            act.play(e)

        @block.vector
        def _(e):
            dve.play(e)

        @block.tensor
        def _(e):
            pe.play(e)

        @block.gpsimd
        def _(e):
            pool.play(e)


def stripes(w, first=0, last=None, k=KD, m=1):
    w = w[:, first:last]
    kk, mm_ = w.shape[0] // (P * k), w.shape[1] // (P * m)
    w = w.reshape(kk, k, P, mm_, m, P).transpose(0, 3, 2, 4, 1, 5)
    return np.ascontiguousarray(w.reshape(kk * mm_, P, m * k * P))


def columns(v):
    return v.reshape(-1, P).T


def layout(a):
    out = {}
    out["x"] = np.ascontiguousarray(a["x"][0].T).reshape(KD, P, T)
    out["p"] = np.ascontiguousarray(a["p"][0, 0].T).reshape(2, P, T)
    out["w_in_a"] = stripes(a["w_in"][0])
    out["w_pool"] = a["w_pool"][0]
    out["w_branch_a"] = stripes(a["w_branch_a"][0], k=4)
    out["w_branch_b"] = stripes(a["w_branch_b"][0], k=4)
    out["w_out"] = stripes(a["w_out"][0])
    out["w_ffn_gate"] = stripes(a["w_ffn_gate"][0])
    out["w_ffn_up"] = stripes(a["w_ffn_up"][0])
    out["w_ffn_down"] = stripes(a["w_ffn_down"][0], k=FFN_GROUP, m=8 // FFN_GROUP)
    out["w_ple_gate"] = stripes(a["w_ple_gate"][0])
    out["w_ple_proj"] = stripes(a["w_ple_proj"][0], k=2, m=4)
    w = a["w_in_2"][0]
    out["w_in_b_ml"] = stripes(w, 0, 2048)
    out["w_in_b_at"] = stripes(w, 2056, 2824)
    g = np.zeros((KD, P, P), w.dtype)
    g[:, :, 0:4] = w[:, 2048:2052].reshape(KD, P, 4)
    g[:, :, 32:36] = w[:, 2052:2056].reshape(KD, P, 4)
    out["w_in_b_gates"] = np.ascontiguousarray(g.transpose(1, 0, 2).reshape(P, KD * P))
    out["w_out_b"] = stripes(a["w_out_2"][0])
    out["w_up_b"] = stripes(a["w_up_2"][0])
    out["w_down_b"] = stripes(a["w_down_2"][0], k=FFN_GROUP, m=8 // FFN_GROUP)
    out["w_ada"] = np.ascontiguousarray(a["w_ada_2"][0].reshape(KD, P, 6, D).transpose(2, 0, 1, 3))
    vecs = np.zeros((P, N_VEC), np.float32)

    def put(name, value, rows=P):
        vecs[0:rows, VEC[name]:VEC[name] + value.shape[1]] = value

    for name, key in (("norm_mix", "norm_mix"), ("norm_ffn", "norm_ffn"), ("norm_ple", "norm_ple"),
                      ("norm_final", "norm_final"), ("pool_scale", "pool_scale"), ("pre_mix_g", "pre_mix_g_2"),
                      ("ml_conv_w", "ml_conv_w_2"), ("ml_conv_b", "ml_conv_b_2"), ("ml_norm_g", "ml_norm_g_2"),
                      ("attn_norm_g", "attn_norm_g_2"), ("post_mix_g", "post_mix_g_2"),
                      ("pre_ffn_g", "pre_ffn_g_2"), ("ffn_conv_w", "ffn_conv_w_2"), ("ffn_conv_b", "ffn_conv_b_2"),
                      ("post_ffn_g", "post_ffn_g_2"), ("b_ada", "b_ada_2"), ("c", "c_2")):
        put(name, columns(a[key].reshape(-1)))
    vecs[0:4, VEC["gate_b"]] = a["ml_i_b_2"][0]
    vecs[32:36, VEC["gate_b"]] = a["ml_f_b_2"][0]
    put("sinks", np.broadcast_to(a["attn_sinks_2"], (P, AT_H)))
    out["vecs"] = vecs
    out["consts"], out["rope"] = constants()
    return out


SCRATCH = {"row_park": (P, T), "o_park": (4, P, T), "x_park": (KD, P, T), "gate_i": (4, T), "gate_f": (4, T), "chunk_end": (2, 32), "chunk_m": (2, 4, 8),
           "m_rows": (32, P), "decay_row": (32,)}


def build(nc, arrays):
    io = {}
    for name, v in arrays.items():
        io[name] = nc.dram_tensor(f"in_{name}", v.shape, F32, kind="ExternalInput").ap()
    for name, shape in SCRATCH.items():
        io[name] = nc.dram_tensor(name, shape, F32, kind="Internal").ap()
    io["out"] = nc.dram_tensor("out_dram", (KD, P, T), F32, kind="ExternalOutput").ap()
    two_blocks(nc, io)


def kernel(**inputs):
    import concourse.bacc as bacc
    from concourse.bass_utils import run_bass_kernel_spmd

    nc = bacc.Bacc("TRN2", target_bir_lowering=False, num_devices=1)
    arrays = layout({k: np.asarray(v) for k, v in inputs.items()})
    build(nc, arrays)
    r = run_bass_kernel_spmd(nc, [{f"in_{k}": v for k, v in arrays.items()}], core_ids=[0])
    return np.ascontiguousarray(r.results[0]["out_dram"].reshape(D, T).T)[None]
```

```python
from contextlib import ExitStack

import numpy as np

import concourse.bass as bass
from concourse import mybir

F32 = mybir.dt.float32
F32R = mybir.dt.float32r
BF16 = mybir.dt.bfloat16
ACT = mybir.ActivationFunctionType
ALU = mybir.AluOpType
AX = mybir.AxisListType

P = 128
T = 1024
D = 1024
KD = D // P
NB = T // P
HALF = 512
NH = T // HALF
EPS = 1e-6
NEG = -1e30

WINDOWS = (2, 4, 8, 16)
D_SB = 512
SB_DIM = 64
D_FF = 2816
KF = D_FF // P

ML_H, ML_D = 4, 128
ML_CONV = 4
AT_H, AT_KV, AT_DIM = 8, 2, 64
FFN_CONV = 3
TAIL = 3
FFN_GROUP = 2

EXACT_FROM = 16.0

VEC = {}


def _columns():
    at = 0
    for name, n in (
        ("norm_mix", KD), ("norm_ffn", KD), ("norm_ple", KD), ("norm_final", KD), ("pool_scale", 4),
        ("pre_mix_g", KD), ("ml_conv_w", ML_CONV * 8), ("ml_conv_b", 8), ("gate_b", 1), ("ml_norm_g", ML_H),
        ("attn_norm_g", 4), ("post_mix_g", KD), ("pre_ffn_g", KD), ("ffn_conv_w", FFN_CONV * 2 * KF),
        ("ffn_conv_b", 2 * KF), ("post_ffn_g", KD), ("b_ada", 6 * KD), ("c", KD), ("sinks", AT_H),
    ):
        VEC[name] = at
        at += n
    return at


N_VEC = _columns()

CONST = {}
N_CONST = 0
for _name, _n in (("ident", P), ("ones", P), ("inv_count", 4 * 16)):
    CONST[_name] = N_CONST
    N_CONST += _n


def constants():
    p, j = np.arange(P)[:, None], np.arange(P)[None, :]
    table = np.zeros((P, N_CONST), np.float32)

    def put(name, value):
        table[:, CONST[name]:CONST[name] + value.shape[1]] = value

    put("ident", (p == j).astype(np.float32))
    put("ones", np.ones((P, P), np.float32))
    k2 = np.arange(2 * P)[None, :]
    masks = np.concatenate([
        -(p >= j).astype(np.float32),
        -np.ones((P, P), np.float32),
        np.where(p >= j, NEG, 0.0).astype(np.float32),
    ], axis=1)
    half = AT_DIM // 2
    rot = np.zeros((P, P), np.float32)
    for to in range(P):
        d = to % AT_DIM
        rot[to + half if d < half else to - half, to] = -1.0 if d < half else 1.0
    late = np.concatenate([
        rot,
        np.where(p > j, NEG, 0.0).astype(np.float32),
        np.where((k2 > p) & (k2 <= p + P), 0.0, NEG).astype(np.float32),
    ], axis=1)
    counts = np.concatenate([1.0 / np.minimum(np.arange(16) + 1, w) for w in WINDOWS])
    put("inv_count", np.broadcast_to(counts.astype(np.float32), (P, 64)))
    inv = (np.float32(10000.0) ** (-np.arange(half, dtype=np.float32) / np.float32(half))).astype(np.float32)
    ang = (np.arange(T, dtype=np.float32)[None, :] * inv[:, None]).astype(np.float32).astype(np.float64)
    cos, sin = np.cos(ang).astype(np.float32), np.sin(ang).astype(np.float32)
    rope = np.concatenate([np.tile(cos, (4, 1)), np.tile(sin, (4, 1))], axis=1)
    return table, masks, late, np.ascontiguousarray(rope)


class Queue:

    def __init__(self, sem):
        self.sem, self.count, self.steps, self.passed = sem, 0, [], {}

    def wait(self, *tokens):
        for t in tokens:
            if t is None:
                continue
            if isinstance(t, list):
                self.wait(*t)
            elif self.passed.get(id(t[0]), 0) < t[1]:
                self.passed[id(t[0])] = t[1]
                self.steps.append(("wait", t[0], t[1]))

    def do(self, step, *tokens):
        self.wait(*tokens)
        self.steps.append(("do", step, None))

    def mark(self, step, *tokens):
        self.wait(*tokens)
        self.count += 1
        self.steps.append(("do", step, (self.sem, 1)))
        return (self.sem, self.count)

    def now(self):
        return (self.sem, self.count) if self.count else None

    def play(self, engine):
        for kind, a, b in self.steps:
            if kind == "wait":
                engine.wait_ge(a, b)
            else:
                made = a(engine)
                if b is not None:
                    made.then_inc(b[0], b[1])


class Buf:

    def __init__(self, ap, busy=None):
        self.ap, self.ready, self.busy = ap, [], list(busy or [])

    def written(self, *tokens):
        self.ready, self.busy = list(tokens), []

    def used(self, *tokens):
        self.busy += tokens


class Ring:
    def __init__(self, bufs):
        self.bufs, self.at = bufs, 0

    def take(self):
        b = self.bufs[self.at % len(self.bufs)]
        self.at += 1
        return b


def two_blocks(nc, io):
    with ExitStack() as ctx:
        def sb_in(scope, name, shape, dt=F32):
            return scope.enter_context(nc.sbuf_tensor(name, shape, dt))

        def sb(name, shape, dt=F32):
            return sb_in(ctx, name, shape, dt)

        def sem(name):
            return ctx.enter_context(nc.semaphore(name))

        sync = Queue(sem("s_sync"))
        act = Queue(sem("s_scalar"))
        dve = Queue(sem("s_vector"))
        pe = Queue(sem("s_tensor"))
        pool = Queue(sem("s_gpsimd"))

        class Dma:

            def __init__(self, name):
                self.sem, self.count = sem(name), 0

            def start(self, queue, out, in_, *tokens):
                queue.wait(*tokens)
                self.count += 16
                queue.steps.append(("do", lambda e: e.dma_start(out, in_), (self.sem, 16)))
                return (self.sem, self.count)

        def fence():
            return [q.now() for q in (act, dve, pe, pool) if q.now()]

        consts = sb("consts", [P, N_CONST])
        vecs = sb("vecs", [P, N_VEC])
        ident_bf = sb("ident_bf", [P, P], BF16)
        causal_bf = sb("causal_bf", [P, P], BF16)
        minus_from = sb("minus_from", [P, P])
        minus_ones = sb("minus_ones", [P, P])
        mod = sb("mod", [P, 6 * KD])
        gain = sb("gain", [P, 4 * KD])
        w_raw = sb("w_raw", [P, 2, 1024])
        w_hi = sb("w_hi", [P, 2, 1024], F32R)
        w_lo = sb("w_lo", [P, 2, 1024], F32R)
        tmp_mem = sb("tmp_mem", [P, 2, T])
        norm_row = Buf(sb("norm_row", [P, T])[:, :])
        h_hi = sb("h_hi", [P, KD, T], F32R)
        h_lo = sb("h_lo", [P, KD, T], F32R)
        psum_mem = ctx.enter_context(nc.psum_tensor("psum_mem", [P, 8, HALF], F32))

        tmps = Ring([Buf(tmp_mem[:, i, :]) for i in range(2)])
        banks = [Buf(psum_mem[:, b, :]) for b in range(8)]

        class Pair:

            def __init__(self, i):
                self.i = i
                self.ap = psum_mem[:, 2 * i:2 * i + 2, :].rearrange("p a b -> p (a b)")

            @property
            def busy(self):
                return banks[2 * self.i].busy + banks[2 * self.i + 1].busy

            def half(self, n):
                return psum_mem[:, 2 * self.i + n, :]

            def written(self, *tokens):
                for b in (2 * self.i, 2 * self.i + 1):
                    banks[b].written(*tokens)

            @property
            def ready(self):
                return banks[2 * self.i].ready

            def used(self, *tokens):
                for b in (2 * self.i, 2 * self.i + 1):
                    banks[b].used(*tokens)

        pairs = Ring([Pair(i) for i in range(4)])

        def const(name, n=P, rows=P):
            return consts[0:rows, CONST[name]:CONST[name] + n]

        def vec(name, i=0, n=1):
            return vecs[:, VEC[name] + i:VEC[name] + i + n]

        def load(dma, out, in_, *w):
            return dma.start(sync, out, in_, *w)

        def a_act(out, in_, func, *w, bias=0.0, scale=1.0):
            return act.mark(lambda e: e.activation(out, in_, func, bias=bias, scale=scale), *w)

        def a_copy(out, in_, *w):
            return act.mark(lambda e: e.copy(out, in_), *w)

        def v_copy(out, in_, *w):
            return dve.mark(lambda e: e.tensor_copy(out, in_), *w)

        def v_tt(out, a, b, op, *w):
            return dve.mark(lambda e: e.tensor_tensor(out, a, b, op), *w)

        def v_ts(out, a, s1, op0, *w, s2=None, op1=None):
            if op1 is None:
                return dve.mark(lambda e: e.tensor_scalar(out, a, s1, None, op0), *w)
            return dve.mark(lambda e: e.tensor_scalar(out, a, s1, s2, op0, op1), *w)

        def v_stt(out, a, s, b, op0, op1, *w):
            return dve.mark(lambda e: e.scalar_tensor_tensor(out=out, in0=a, scalar=s, in1=b, op0=op0, op1=op1), *w)

        def g_tt(out, a, b, op, *w):
            return pool.mark(lambda e: e.tensor_tensor(out, a, b, op), *w)

        def mm(out, lhsT, rhs, start, stop, *w):
            pe.do(lambda e: e.matmul(out, lhsT, rhs, start=start, stop=stop, skip_group_check=True), *w)

        def mm_mark(out, lhsT, rhs, start, stop, *w):
            return pe.mark(lambda e: e.matmul(out, lhsT, rhs, start=start, stop=stop, skip_group_check=True), *w)

        def transpose(out, in_, *w, rows=P):
            ident = consts[0:rows, CONST["ident"]:CONST["ident"] + rows]
            return pe.mark(lambda e: e.transpose(out, in_, ident), *w)

        def split(hi, lo, src, *w, bias=None):
            if bias is None:
                t_hi = a_copy(hi, src, *w)
                t_lo = v_tt(lo, src, hi.bitcast(F32), ALU.subtract, t_hi)
            else:
                t_hi = a_act(hi, src, ACT.Identity, *w, bias=bias)
                t_lo = v_stt(lo, src, bias, hi.bitcast(F32), ALU.add, ALU.subtract, t_hi)
            return [t_hi, t_lo]

        units = []
        for j in range(4):
            for part in range(3):
                units.append(("w_qkv", io["w_in_a"][4 + 4 * part + j]))
        for g in range(4):
            units.append(("w_u", io["w_in_a"][g]))
            if g > 0:
                units.append(("w_pool", io["w_pool"][g - 1]))
        for m in range(KD):
            units.append(("w_ga", io["w_in_a"][16 + m]))
            units.append(("w_gb", io["w_in_a"][24 + m]))
            if m == 0:
                units.append(("w_pool", io["w_pool"][3]))
            units.append(("w_ba", io["w_branch_a"][m]))
            units.append(("w_bb", io["w_branch_b"][m]))
        for m in range(KD):
            units.append(("w_out", io["w_out"][m]))
        n_groups = KF // FFN_GROUP

        def ffn_order(names, down):
            order = []
            for g in range(n_groups + 1):
                if g < n_groups:
                    for i in range(g * FFN_GROUP, (g + 1) * FFN_GROUP):
                        for name, source in names:
                            order.append((name, source[i]))
                if g > 0:
                    for m in range(2):
                        order.append(("w_down", down[2 * (g - 1) + m]))
            return order

        units += ffn_order([("w_gate", io["w_ffn_gate"]), ("w_up", io["w_ffn_up"])], io["w_ffn_down"])
        for m in range(KD):
            if m % 4 == 0:
                units.append(("w_pp", io["w_ple_proj"][m // 4]))
            units.append(("w_pg", io["w_ple_gate"][m]))
        for s in range(5):
            units.append(("w_qk_at", io["w_in_b_at"][s]))
        units.append(("w_v_at", io["w_in_b_at"][5]))
        for s in range(8, 16):
            units.append(("w_ml", io["w_in_b_ml"][s]))
        units.append(("w_gates", io["w_in_b_gates"]))
        for s in range(8):
            units.append(("w_ml", io["w_in_b_ml"][s]))
        for m in range(KD):
            units.append(("w_out2", io["w_out_b"][m]))
        units += ffn_order([("w_gate2", io["w_up_b"][0:KF]), ("w_up2", io["w_up_b"][KF:2 * KF])], io["w_down_b"])

        class Weights:
            def __init__(self):
                self.raw = [Buf(w_raw[:, i, :]) for i in range(2)]
                self.dma = [Dma(f"w_load{i}") for i in range(2)]
                self.hi = [Buf(w_hi[:, i, :]) for i in range(2)]
                self.lo = [Buf(w_lo[:, i, :]) for i in range(2)]
                self.loaded = self.cut = self.taken = 0

            def load(self):
                n, i = self.loaded, self.loaded % 2
                if n >= len(units):
                    return
                self.loaded += 1
                width = units[n][1].shape[-1]
                t = load(self.dma[i], self.raw[i].ap[:, 0:width], units[n][1], self.raw[i].busy)
                self.raw[i].written(t)

            def split(self):
                n, i = self.cut, self.cut % 2
                if n >= len(units):
                    return
                if self.loaded == self.cut:
                    self.load()
                self.cut += 1
                width = units[n][1].shape[-1]
                raw, hi, lo = self.raw[i], self.hi[i], self.lo[i]
                t_hi = a_copy(hi.ap[:, 0:width], raw.ap[:, 0:width], raw.ready, hi.busy)
                t_lo = g_tt(lo.ap[:, 0:width], raw.ap[:, 0:width], hi.ap[:, 0:width].bitcast(F32), ALU.subtract,
                            t_hi, raw.ready, lo.busy)
                raw.used(t_hi, t_lo)
                hi.written(t_hi)
                lo.written(t_lo)

            def take(self, name):
                n, i = self.taken, self.taken % 2
                assert units[n][0] == name, (units[n][0], name)
                self.taken += 1
                while self.cut < self.taken:
                    self.split()
                return self.hi[i], self.lo[i]

            def ahead(self, n=1):
                while self.cut < min(self.taken + n, len(units)):
                    self.split()

        weights = Weights()

        def project_steps(out, unit, blocks, rhs, waits):
            hi, lo = unit
            mark = None
            n = len(blocks)
            for k, b in enumerate(blocks):
                w_h, w_l = hi.ap[:, b * P:(b + 1) * P], lo.ap[:, b * P:(b + 1) * P]
                x_h, x_l, ready = rhs[k]
                for part, (w, x) in enumerate(((w_h, x_h), (w_h, x_l), (w_l, x_h))):
                    for half in range(NH):
                        cols = slice(half * HALF, (half + 1) * HALF)
                        last = k == n - 1 and part == 2
                        args = (out.half(half), w, x[:, cols], k == 0 and part == 0, last,
                                waits, ready, lo.ready if part == 2 else hi.ready)
                        if last and half == NH - 1:
                            mark = mm_mark(*args)
                        else:
                            mm(*args)
                yield
            hi.used(mark)
            lo.used(mark)
            out.written(mark)

        def one(name, rhs, blocks=tuple(range(KD)), unit=None):
            out = pairs.take()
            if unit is None:
                unit = weights.take(name)
                weights.ahead()
            for _ in project_steps(out, unit, blocks, rhs, out.busy):
                pass
            return out, out.ready[0]

        def two(names, rhs):
            outs, steps = [], []
            for name in names:
                out = pairs.take()
                outs.append(out)
                steps.append(project_steps(out, weights.take(name), tuple(range(KD)), rhs, out.busy))
            for _ in range(KD - TAIL):
                for st in steps:
                    next(st)
            for st in steps:
                for _ in st:
                    pass
                weights.ahead()
            return [(out, out.ready[0]) for out in outs]

        dma_x = [Dma(f"dma_x{k}") for k in range(KD)]
        out_dma = Dma("dma_out")

        h_busy = [[] for _ in range(KD)]
        h_ready = [[] for _ in range(KD)]

        def h_rhs(ks=range(KD)):
            return [(h_hi[:, k, :], h_lo[:, k, :], h_ready[k]) for k in ks]

        def h_used(mark):
            for k in range(KD):
                h_busy[k].append(mark)

        class SquareSum:

            def __init__(self, row, on_pe=False):
                self.row, self.n, self.total = row, 0, None
                self.out = pairs.take() if on_pe else None

            def add(self, ap, ready, scale=1.0):
                row = self.row
                self.n += 1
                if self.n == 1 and not self.out:
                    self.total = t_sq = a_act(row.ap, ap, ACT.Square, ready, row.busy, scale=scale)
                    return t_sq
                t = tmps.take()
                t_sq = a_act(t.ap, ap, ACT.Square, ready, t.busy, scale=scale)
                t.written(t_sq)
                if self.out:
                    self.total = self.sum_partitions(self.out, t.ap, self.n == 1, self.n == KD, t_sq)
                    t.used(*self.total)
                else:
                    add = v_tt if self.n >= KD - 1 else g_tt
                    self.total = add(row.ap, row.ap, t.ap, ALU.add, self.total, t_sq)
                    t.used(self.total)
                return t_sq

            def sum_partitions(self, out, ap, start, stop, *w):
                return [mm_mark(out.half(half), const("ones"), ap[:, half * HALF:(half + 1) * HALF], start, stop,
                                out.busy if start else None, *w) for half in range(NH)]

            def inverse(self, eps=EPS, total=None):
                row, total, out, square = self.row, total or self.total, self.out, tmps.take()
                act.do(lambda e: e.preload_act_table_set("natural_log_exp_and_others"))
                if not out:
                    out = pairs.take()
                    total = self.sum_partitions(out, row.ap, True, True, total)
                out.written(*total)
                eps_ap = eps_col[:, 0:1] if eps == EPS else eps_col[:, 1:2]
                marks, made = [], []
                for half in range(NH):
                    cols = slice(half * HALF, (half + 1) * HALF)
                    r, v, sq = row.ap[:, cols], out.half(half), square.ap[:, cols]
                    t = a_act(r, v, ACT.Ln, total[half], row.busy, bias=eps_ap, scale=1.0 / D)
                    t_r = a_act(r, r, ACT.Exp, t, scale=-0.5)
                    t = a_act(sq, r, ACT.Square, t_r, square.busy, scale=(0.5 / D) ** 0.5)
                    t = v_stt(sq, v, D * eps, sq, ALU.add, ALU.mult, t)
                    marks.append(t)
                    made.append(dve.mark((lambda r, sq: lambda e: e.scalar_tensor_tensor(
                        out=r, in0=sq, scalar=1.5, in1=r, op0=ALU.subtract, op1=ALU.mult, reverse0=True))(r, sq), t))
                out.used(*marks)
                square.written(*marks)
                square.used(*made)
                row.written(*made)

        eps_col = sb("eps_col", [P, 2])
        t_eps = [dve.mark(lambda e: e.memset(eps_col[:, 0:1], EPS)),
                 dve.mark(lambda e: e.memset(eps_col[:, 1:2], EPS * EPS))]
        act.wait(t_eps)

        def scaled_to_h(k, c, g):
            t_hi = a_act(h_hi[:, k, :], c.ap, ACT.Copy, c.ready, h_busy[k], scale=g)
            t_lo = v_stt(h_lo[:, k, :], c.ap, g, h_hi[:, k, :].bitcast(F32), ALU.mult, ALU.subtract, t_hi,
                         h_busy[k])
            c.used(t_hi, t_lo)
            h_ready[k], h_busy[k] = [t_hi, t_lo], []

        def unscale(out, ps, *w, factor=1.0, rows=slice(0, P)):
            if factor == 1.0:
                t = v_tt(out, ps.ap[rows, :], norm_row.ap[rows, :], ALU.mult, norm_row.ready, *w)
            else:
                t = v_stt(out, ps.ap[rows, :], factor, norm_row.ap[rows, :], ALU.mult, ALU.mult, norm_row.ready, *w)
            norm_row.used(t)
            return t

        def normed_to_h(chunks, row, gains, shifts):
            def low_part(k, t, t_hi):
                t_lo = v_stt(h_lo[:, k, :], t.ap, shifts(k), h_hi[:, k, :].bitcast(F32), ALU.add, ALU.subtract, t_hi)
                t.used(t_hi, t_lo)
                h_ready[k], h_busy[k] = [t_hi, t_lo], []

            before = None
            for k, c in enumerate(chunks):
                t = tmps.take()
                t_h = v_stt(t.ap, c.ap, gains(k), row.ap, ALU.mult, ALU.mult, c.ready, row.ready, t.busy)
                c.used(t_h)
                row.used(t_h)
                t.written(t_h)
                t_hi = a_act(h_hi[:, k, :], t.ap, ACT.Identity, t_h, h_busy[k], bias=shifts(k))
                if before:
                    low_part(*before)
                before = (k, t, t_hi)
            low_part(*before)

        def load_x(scope, name, source, busy):
            mem = sb_in(scope, name, [P, KD, T])
            chunks = []
            for k in range(KD):
                c = Buf(mem[:, k, :])
                c.written(load(dma_x[k], c.ap, source[k], busy))
                chunks.append(c)
            return chunks

        t_vec = load(Dma("dma_vec"), vecs[:, :], io["vecs"])
        weights.split()
        weights.split()
        act.wait(t_vec)
        dve.wait(t_vec)
        scope = ExitStack()
        x = load_x(scope, "x_first", io["x"], None)
        masks = sb_in(scope, "masks", [P, 3 * P])
        t_const = load(Dma("dma_const"), consts[:, :], io["consts"])
        t = load(Dma("dma_masks"), masks[:, :], io["masks"])
        total = SquareSum(norm_row)
        for k, c in enumerate(x):
            scaled_to_h(k, c, vec("norm_mix", k))
            c.used(total.add(c.ap, c.ready))
        t_masks = [v_copy(out[:, :], masks[:, a * P:b * P], t) for out, a, b in (
            (minus_from, 0, 1), (minus_ones, 1, 2), (causal_bf, 2, 3))]
        t_ident = v_copy(ident_bf[:, :], const("ident"), t_const)
        first_qk = two(("w_qkv", "w_qkv"), h_rhs())
        pe.wait(t_const, t_ident, t_masks)
        total.inverse()
        scope.close()

        outer = ExitStack()
        yb_hi = sb_in(outer, "yb_hi", [P, 4, T], F32R)
        yb_lo = sb_in(outer, "yb_lo", [P, 4, T], F32R)
        attn = ExitStack()
        free = fence()
        act.wait(free)
        dve.wait(free)
        pool.wait(free)

        def halves(mem):
            return [Buf(mem[:, i * HALF:(i + 1) * HALF]) for i in range(NH)]

        q_both = [halves(sb_in(attn, f"q_both{par}", [P, T], F32R)) for par in range(2)]
        k_twice = [halves(sb_in(attn, f"k_twice{par}", [P, T], F32R)) for par in range(2)]
        k_low_mem = sb_in(attn, "k_low", [P, T], F32R)
        k_low = [[Buf(k_low_mem[64 * par:64 * par + 64, half * HALF:(half + 1) * HALF]) for par in range(2)]
                 for half in range(NH)]
        v_parts = [sb_in(attn, f"v_parts{i}", [P, NB, 2, P], F32R) for i in range(2)]
        v_ready, v_busy = [[], []], [[], []]
        q_raw, k_raw = (halves(tmp_mem[:, i, :]) for i in range(2))
        v_raw = Buf(sb_in(attn, "v_raw", [P, HALF])[:, :])
        z_banks, o_banks, proj_banks = Ring(banks[0:4]), banks[4:6], Ring(banks[6:8])

        def head_rows(par):
            return slice(64 * par, 64 * par + 64)

        def norm_half(half):
            return norm_row.ap[:, half * HALF:(half + 1) * HALF]

        def take_raw(dst, src, half, factor, mark):
            d = dst[half]
            t = v_stt(d.ap, src.ap, factor, norm_half(half), ALU.mult, ALU.mult, mark, d.busy, norm_row.ready)
            norm_row.used(t)
            src.used(t)
            d.written(t)

        def cut_q(half, par):
            raw, b = q_raw[half], q_both[par][half]
            rows, other = head_rows(par), head_rows(1 - par)
            t_hi = a_copy(b.ap[rows, :], raw.ap[rows, :], raw.ready, b.busy)
            t_lo = v_tt(b.ap[other, :], raw.ap[rows, :], b.ap[rows, :].bitcast(F32), ALU.subtract, t_hi)
            b.written(t_hi, t_lo)
            raw.used(t_hi, t_lo)

        def cut_k(half, par):
            raw, b, low = k_raw[half], k_twice[par][half], k_low[half][par]
            rows, other = head_rows(par), head_rows(1 - par)
            t_hi = a_copy(b.ap[rows, :], raw.ap[rows, :], raw.ready, b.busy)
            t_2 = v_copy(b.ap[other, :], raw.ap[rows, :], raw.ready, b.busy)
            t_lo = v_tt(low.ap, raw.ap[rows, :], b.ap[rows, :].bitcast(F32), ALU.subtract, t_hi, low.busy)
            b.written(t_hi, t_2)
            low.written(t_lo)
            raw.used(t_2, t_lo)

        def take_v(j, src, half, mark, turned):
            t = v_tt(v_raw.ap, src.ap, norm_half(half), ALU.mult, mark, v_raw.busy, norm_row.ready)
            norm_row.used(t)
            src.used(t)
            v_raw.written(t)
            yield
            for b in range(4):
                mark = transpose(turned.ap[:, b * P:(b + 1) * P], v_raw.ap[:, b * P:(b + 1) * P], t, turned.busy)
            v_raw.used(mark)
            turned.written(mark)
            side = j % 2
            keys = turned.ap.rearrange("p (b h d) -> p b h d", b=4, h=2)
            outs = [v_parts[side][:, 4 * half:4 * half + 4, par, :] for par in range(2)]
            t_hi = [a_copy(outs[par][:, :, head_rows(par)], keys[:, :, par, :], mark, v_busy[side])
                    for par in range(2)]
            t_lo = [v_tt(outs[par][:, :, head_rows(1 - par)], keys[:, :, par, :],
                         outs[par][:, :, head_rows(par)].bitcast(F32), ALU.subtract, t_hi) for par in range(2)]
            turned.used(*t_lo)
            v_ready[side] += t_hi + t_lo

        def qkv_steps(j):
            for part in range(3):
                unit = weights.take("w_qkv")
                weights.ahead()
                hi, lo = unit
                for half in range(NH):
                    cols = slice(half * HALF, (half + 1) * HALF)
                    proj_bank = proj_banks.take()
                    busy = proj_bank.busy
                    for k in range(KD):
                        w_h, w_l = hi.ap[:, k * P:(k + 1) * P], lo.ap[:, k * P:(k + 1) * P]
                        x_h, x_l = h_hi[:, k, cols], h_lo[:, k, cols]
                        mm(proj_bank.ap, w_h, x_h, k == 0, False, busy, h_ready[k], hi.ready)
                        mm(proj_bank.ap, w_h, x_l, False, False)
                        mark = mm_mark(proj_bank.ap, w_l, x_h, False, k == KD - 1, lo.ready)
                        yield
                    proj_bank.written(mark)
                    if part == 0:
                        take_raw(q_raw, proj_bank, half, SB_DIM ** -0.5, mark)
                    elif part == 1:
                        take_raw(k_raw, proj_bank, half, 1.0, mark)
                    else:
                        if half == 0:
                            v_ready[j % 2] = []
                        yield from take_v(j, proj_bank, half, mark, proj_bank)
                hi.used(mark)
                lo.used(mark)
                h_used(mark)

        def tile_ring(name, n, dt=F32):
            return Ring([Buf(sb_in(attn, f"{name}{i}", [P, HALF], dt)[:, :]) for i in range(n)])

        sp_ring, a_ring = tile_ring("softplus", 4), tile_ring("weight", 2)
        acc = [[Buf(sb_in(attn, f"acc{par}{i}", [P, HALF])[:, :]) for i in range(2)] for par in range(2)]
        a_hi_ring, a_lo_ring = tile_ring("weight_hi", 2, F32R), tile_ring("weight_lo", 2, F32R)
        yb_split = [[] for _ in range(4)]
        act.do(lambda e: e.preload_act_table_set("natural_log_exp_and_others"))

        def score(tile):
            j, par, g, kb, c0, n = tile["at"]
            bank = z_banks.take()
            rows, keys = head_rows(par), slice((kb % 4) * P, (kb % 4 + 1) * P)
            q, k2, kl = q_both[par][g], k_twice[par][kb // 4], k_low[kb // 4][par]
            mm(bank.ap[:, 0:n], k2.ap[:, keys], q.ap[:, c0:HALF], True, False, bank.busy, q.ready, k2.ready)
            mark = mm_mark(bank.ap[:, 0:n], kl.ap[:, keys], q.ap[rows, c0:HALF], False, not tile["diag"], kl.ready)
            if tile["diag"]:
                mark = mm_mark(bank.ap[:, 0:P], ident_bf[:, :], causal_bf[:, :], False, True)
            for b in (q, k2, kl):
                b.used(mark)
            bank.written(mark)
            tile["z"] = bank

        def softplus(tile):
            n, z = tile["at"][5], tile["z"]
            sp = tile["sp"] = sp_ring.take()
            t = v_ts(sp.ap[:, 0:n], z.ap[:, 0:n], EXACT_FROM, ALU.min, z.ready, sp.busy)
            t = a_act(sp.ap[:, 0:n], sp.ap[:, 0:n], ACT.Exp, t)
            sp.written(a_act(sp.ap[:, 0:n], sp.ap[:, 0:n], ACT.Ln, t, bias=1.0))

        def softplus_end(tile):
            n, z, sp = tile["at"][5], tile["z"], tile["sp"]
            t = v_tt(sp.ap[:, 0:n], sp.ap[:, 0:n], z.ap[:, 0:n], ALU.max, sp.ready)
            sp.written(t)
            z.ready = [t]

        def sums(tile):
            j, par, g, kb, c0, n = tile["at"]
            z, sp = tile["z"], tile["sp"]
            old, new = acc[par]
            first = kb == 4 * g + 3
            wide = P if tile["diag"] else 0
            mark = mm_mark(z.ap[:, 0:n], minus_from[:, :], sp.ap[:, 0:n], False, first, sp.ready, z.ready)
            if not first:
                mark = mm_mark(z.ap[:, wide:n], minus_ones[:, :], old.ap[:, c0 + wide:HALF], False, True, old.ready)
                old.used(mark)
            sp.used(mark)
            z.written(mark)
            if kb > 0:
                tokens = []
                if wide:
                    tokens.append(pool.mark(
                        lambda e: e.tensor_copy(new.ap[:, c0:c0 + P], sp.ap[:, 0:P]), sp.ready, new.busy))
                if not first:
                    tokens.append(g_tt(new.ap[:, c0 + wide:HALF], old.ap[:, c0 + wide:HALF], sp.ap[:, wide:n],
                                       ALU.add, sp.ready, old.ready, new.busy))
                    old.used(tokens[-1])
                sp.used(*tokens)
                new.written(*tokens)
                acc[par] = [new, old]

        def weigh(tile):
            n, z = tile["at"][5], tile["z"]
            a = tile["a"] = a_ring.take()
            t = a_act(a.ap[:, 0:n], z.ap[:, 0:n], ACT.Exp, z.ready, a.busy)
            z.used(t)
            a.written(t)

        def cut_weight(tile):
            n, a = tile["at"][5], tile["a"]
            hi, lo = tile["a_parts"] = a_hi_ring.take(), a_lo_ring.take()
            t_hi = v_copy(hi.ap[:, 0:n], a.ap[:, 0:n], a.ready, hi.busy)
            t_lo = g_tt(lo.ap[:, 0:n], a.ap[:, 0:n], hi.ap[:, 0:n].bitcast(F32), ALU.subtract, t_hi, a.ready, lo.busy)
            a.used(t_hi, t_lo)
            hi.written(t_hi)
            lo.written(t_lo)

        def mix(tile):
            j, par, g, kb, c0, n = tile["at"]
            (hi, lo), o, side = tile["a_parts"], o_banks[par], j % 2
            v = v_parts[side][:, kb, par, :]
            first = kb == 4 * g + 3
            mm(o.ap[:, c0:HALF], v, hi.ap[:, 0:n], first, False, hi.ready, v_ready[side], o.busy if first else None)
            mark = mm_mark(o.ap[:, c0:HALF], v, lo.ap[:, 0:n], False, kb == 0, lo.ready)
            hi.used(mark)
            lo.used(mark)
            v_busy[side] = [mark]
            if kb == 0:
                o.written(mark)
                rows, cols = head_rows(par), slice(g * HALF, (g + 1) * HALF)
                y = v_raw
                t = a_copy(y.ap[rows, :], o.ap[head_rows(1 - par), :], mark, y.busy)
                t = v_tt(y.ap[rows, :], y.ap[rows, :], o.ap[rows, :], ALU.add, t)
                o.used(t)
                y.written(t)
                made = split(yb_hi[rows, j, cols], yb_lo[rows, j, cols], y.ap[rows, :], t)
                y.used(*made)
                yb_split[j] += made

        tiles = []
        for j in range(4):
            for g in reversed(range(NH)):
                for kb in range(4 * g + 3, -1, -1):
                    for par in range(2):
                        c0 = max(0, kb - 4 * g) * P
                        tiles.append({"at": (j, par, g, kb, c0, HALF - c0), "diag": kb >= 4 * g})
        per_pair = len(tiles) // 4
        (ps_q, mark_q), (ps_k, mark_k) = first_qk
        h_used(mark_k)
        ps_v, mark_v = one("w_qkv", h_rhs())
        h_used(mark_v)

        def bank_of(pair, half):
            return banks[2 * pair.i + half]

        for half in (1, 0):
            take_raw(q_raw, bank_of(ps_q, half), half, SB_DIM ** -0.5, mark_q)
            take_raw(k_raw, bank_of(ps_k, half), half, 1.0, mark_k)
            for par in range(2):
                cut_q(half, par)
                cut_k(half, par)
        for half in (1, 0):
            for _ in take_v(0, bank_of(ps_v, half), half, mark_v, banks[6 + half]):
                pass
        filler = iter(())
        score(tiles[0])
        for i in range(len(tiles) + 4):
            j, step = divmod(i, per_pair)
            if step == 0:
                for _ in filler:
                    pass
                filler = qkv_steps(j + 1) if j < 3 else iter(())
            if i < len(tiles):
                softplus(tiles[i])
            next(filler, None)
            if 0 <= i - 1 < len(tiles):
                softplus_end(tiles[i - 1])
            if 0 <= i - 2 < len(tiles):
                sums(tiles[i - 2])
                weigh(tiles[i - 2])
            if i + 1 < len(tiles):
                score(tiles[i + 1])
            if 0 <= i - 3 < len(tiles):
                cut_weight(tiles[i - 3])
            if 0 <= i - 4 < len(tiles):
                mix(tiles[i - 4])
            next(filler, None)
            if j < 3 and step in (15, 16):
                cut_q(1, step - 15)
            elif j < 3 and step in (17, 18):
                cut_k(1, step - 17)
            elif 0 < j < 4 and step in (0, 1):
                cut_q(0, step)
            elif 0 < j < 4 and step in (2, 3):
                cut_k(0, step - 2)
        attn.close()
        proj_pair = Pair(3)

        free = fence()
        for b in tmps.bufs:
            b.busy = []
        for q in (act, dve, pool):
            q.wait(free)
        ya_hi = sb_in(outer, "ya_hi", [P, 4, T], F32R)
        ya_lo = sb_in(outer, "ya_lo", [P, 4, T], F32R)
        pool_scope = ExitStack()
        PAD = 16
        u_mem = [sb_in(pool_scope, f"u_mem{i}", [P, PAD + T]) for i in range(3)]
        pl_hi = [Buf(sb_in(pool_scope, f"pl_hi{i}", [P, T], F32R)[:, :]) for i in range(2)]
        pl_lo = [Buf(sb_in(pool_scope, f"pl_lo{i}", [P, T], F32R)[:, :]) for i in range(2)]
        t_zero = [dve.mark((lambda o: lambda e: e.memset(o, 0.0))(u[:, 0:PAD])) for u in u_mem]
        u_busy = []
        ya_ready = []

        def map_group(g):
            hi, lo = pl_hi[g % 2], pl_lo[g % 2]
            ps, mark = one("w_pool", [(hi.ap, lo.ap, [hi.ready, lo.ready])], (0,))
            hi.used(mark)
            lo.used(mark)
            s = tmps.take()
            t = v_ts(s.ap, ps.ap, vec("pool_scale", g), ALU.mult, mark, s.busy)
            ps.used(t)
            s.written(t)
            made = split(ya_hi[:, g, :], ya_lo[:, g, :], s.ap, t)
            s.used(*made)
            ya_ready.append(made)

        for g, window in enumerate(WINDOWS):
            ps, mark = one("w_u", h_rhs())
            h_used(mark)
            u, a, b = u_mem
            t = unscale(u[:, PAD:], ps, mark, u_busy)
            ps.used(t)
            if g > 0:
                map_group(g - 1)
            src, width = u, 1
            dst = a
            t = v_tt(dst[:, PAD:], src[:, PAD:], src[:, PAD - 1:PAD - 1 + T], ALU.add, t, t_zero)
            width = 2
            while width < window:
                src, dst = dst, (b if dst is a else a)
                t = v_tt(dst[:, PAD:], src[:, PAD:], src[:, PAD - width:PAD - width + T], ALU.add, t)
                width *= 2
            s = tmps.take()
            t1 = v_ts(s.ap, dst[:, PAD:], 1.0 / window, ALU.mult, t, s.busy)
            t1 = v_tt(s.ap[:, 0:window], dst[:, PAD:PAD + window],
                      consts[:, CONST["inv_count"] + 16 * g:CONST["inv_count"] + 16 * g + window], ALU.mult, t1)
            t1 = v_tt(s.ap, s.ap, u[:, PAD:], ALU.subtract, t1)
            s.written(t1)
            hi, lo = pl_hi[g % 2], pl_lo[g % 2]
            made = split(hi.ap, lo.ap, s.ap, t1, hi.busy, lo.busy)
            s.used(*made)
            hi.written(made[0])
            lo.written(made[1])
            u_busy = made

        merged_ready = []

        def merged_to_h(k):
            t_hi = a_copy(h_hi[:, k, :], merged[:, k, :], merged_ready[k], h_busy[k])
            sub = g_tt if k % 3 == 2 else v_tt
            t_lo = sub(h_lo[:, k, :], merged[:, k, :], h_hi[:, k, :].bitcast(F32), ALU.subtract, t_hi, h_busy[k],
                       merged_ready[k])
            h_ready[k], h_busy[k] = [t_hi, t_lo], []

        rhs_b = [(yb_hi[:, k, :], yb_lo[:, k, :], yb_split[k]) for k in range(4)]
        for m in range(KD):
            products = [one("w_ga", h_rhs()), one("w_gb", h_rhs())]
            h_used(products[1][1])
            if m == 0:
                map_group(3)
                pool_scope.close()
                free = fence()
                dve.wait(free)
                merged = sb_in(outer, "merged", [P, KD, T])
            gates = []
            for ps, mark in products:
                g = tmps.take()
                t = unscale(g.ap, ps, mark, g.busy)
                ps.used(t)
                t = a_act(g.ap, g.ap, ACT.Sigmoid, t)
                g.written(t)
                gates.append(g)
            g_a, g_b = gates
            if m == KD - 1:
                for k in range(KD - 1):
                    merged_to_h(k)
            rhs_a = [(ya_hi[:, k, :], ya_lo[:, k, :], ya_ready[k]) for k in range(4)]
            ps, mark = one("w_ba", rhs_a, tuple(range(4)))
            t = v_tt(merged[:, m, :], g_a.ap, ps.ap, ALU.mult, mark, g_a.ready)
            ps.used(t)
            g_a.used(t)
            ps, mark = one("w_bb", rhs_b, tuple(range(4)))
            t2 = v_tt(g_b.ap, g_b.ap, ps.ap, ALU.mult, mark, g_b.ready)
            ps.used(t2)
            t3 = v_tt(merged[:, m, :], merged[:, m, :], g_b.ap, ALU.add, t, t2)
            g_b.used(t3)
            merged_ready.append(t3)

        merged_to_h(KD - 1)
        weights.ahead(2)
        outer.close()
        free = fence()
        resident = ExitStack()
        x = load_x(resident, "x_block1", io["x"], free)

        total = SquareSum(norm_row)
        for m in range(KD):
            ps, mark = one("w_out", h_rhs())
            h_used(mark)
            t = v_tt(x[m].ap, x[m].ap, ps.ap, ALU.add, mark, x[m].ready)
            ps.used(t)
            x[m].written(t)
            x[m].used(total.add(x[m].ap, t))

        for k in range(KD):
            if k == KD - 1:
                weights.ahead(2)
            scaled_to_h(k, x[k], vec("norm_ffn", k))

        def feed_forward(name, activate, add, start):
            with ExitStack() as s:
                hid_hi = [sb_in(s, f"hid_hi_{name}{i}", [P, FFN_GROUP, T], F32R) for i in range(2)]
                hid_lo = [sb_in(s, f"hid_lo_{name}{i}", [P, FFN_GROUP, T], F32R) for i in range(2)]
                free = fence()
                act.wait(free)
                dve.wait(free)
                ready = [[None] * FFN_GROUP for _ in range(2)]
                busy = [[], []]
                for g in range(n_groups + 1):
                    if g < n_groups:
                        side = g % 2
                        for i in range(FFN_GROUP):
                            t = activate(g * FFN_GROUP + i, start if g + i == 0 else None)
                            made = split(hid_hi[side][:, i, :], hid_lo[side][:, i, :], t.ap, t.ready, busy[side])
                            t.used(*made)
                            ready[side][i] = made
                    if g > 0:
                        side = (g - 1) % 2
                        rhs = [(hid_hi[side][:, i, :], hid_lo[side][:, i, :], ready[side][i])
                               for i in range(FFN_GROUP)]
                        for half in range(2):
                            unit = weights.take("w_down")
                            weights.ahead()
                            for mi in range(4):
                                m = 4 * half + mi
                                ps, mark = one("w_down", rhs, tuple(mi * FFN_GROUP + i for i in range(FFN_GROUP)), unit)
                                add(g - 1, m, ps, mark)
                        busy[side] = [mark]

        def gated_chunk(i, start):
            if start:
                (ps, mark), (ps2, mark2) = two(("w_gate", "w_up"), h_rhs())
                start()
            else:
                ps, mark = one("w_gate", h_rhs())
            h_used(mark)
            s = tmps.take()
            t = unscale(s.ap, ps, mark, s.busy)
            ps.used(t)
            t = a_act(s.ap, s.ap, ACT.Silu, t)
            t = v_tt(s.ap, s.ap, norm_row.ap, ALU.mult, norm_row.ready, t)
            norm_row.used(t)
            if not start:
                ps2, mark2 = one("w_up", h_rhs())
            h_used(mark2)
            t = v_tt(s.ap, s.ap, ps2.ap, ALU.mult, mark2, t)
            ps2.used(t)
            s.written(t)
            return s

        def add_to_x(g, m, ps, mark):
            t = v_tt(x[m].ap, x[m].ap, ps.ap, ALU.add, mark, x[m].ready, x[m].busy)
            ps.used(t)
            x[m].written(t)
            if g == n_groups - 1:
                x[m].used(ple_total.add(x[m].ap, t))
                scaled_to_h(m, x[m], vec("norm_ple", m))

        ple = ExitStack()
        p_hi = sb_in(ple, "p_hi", [P, 2, T], F32R)
        p_lo = sb_in(ple, "p_lo", [P, 2, T], F32R)
        p_dma = Dma("dma_p")
        free = fence()
        rhs_p = []

        def cut_p(k):
            t = tmps.take()
            t_in = p_dma.start(sync, t.ap, io["p"][k], free, t.busy)
            made = split(p_hi[:, k, :], p_lo[:, k, :], t.ap, t_in)
            t.written(t_in)
            t.used(*made)
            rhs_p.append((p_hi[:, k, :], p_lo[:, k, :], made))

        ada = ExitStack()
        ada_raw = Ring([Buf(sb_in(ada, f"ada_raw{i}", [P, 1024])[:, :], free) for i in range(2)])
        ada_dma = [Dma(f"ada_dma{i}") for i in range(2)]
        ada_sum = Buf(sb_in(ada, "ada_sum", [P, 1024])[:, :], free)
        c_silu = sb_in(ada, "c_silu", [P, KD])
        t_c = a_act(c_silu[:, :], vec("c", 0, KD), ACT.Silu, free)
        mod_ready = []

        def modulation_steps():
            for part in range(6):
                for k in range(KD):
                    n = part * KD + k
                    raw = ada_raw.take()
                    t = ada_dma[n % 2].start(sync, raw.ap, io["w_ada"][part, k], raw.busy)
                    raw.written(t)
                    if k == 0:
                        t = v_ts(ada_sum.ap, raw.ap, c_silu[:, 0:1], ALU.mult, t, t_c, ada_sum.busy)
                    else:
                        t = v_stt(ada_sum.ap, raw.ap, c_silu[:, k:k + 1], ada_sum.ap, ALU.mult, ALU.add, t,
                                  ada_sum.ready)
                    raw.used(t)
                    ada_sum.written(t)
                    yield
                out = pairs.take()
                for j in range(KD):
                    mark = mm_mark(out.ap[:, j:j + 1], ada_sum.ap[:, j * P:(j + 1) * P], const("ones", 1), True, True,
                                   ada_sum.ready, out.busy)
                ada_sum.used(mark)
                out.written(mark)
                cols_ = slice(part * KD, (part + 1) * KD)
                t = v_tt(mod[:, cols_], out.ap[:, 0:KD], vec("b_ada", part * KD, KD), ALU.add, mark)
                out.used(t)
                mod_ready.append(t)

        modulation = modulation_steps()

        def gated_chunk_and_more(i, start):
            out = gated_chunk(i, start)
            if 0 < i < KF - 2:
                for _ in range(3):
                    next(modulation, None)
            if KF - 3 < i:
                cut_p(i - (KF - 2))
            return out

        def park(chunks, ks=range(KD)):
            done = []
            for k in ks:
                c = chunks[k]
                t = dma_x[k].start(sync, io["x_park"][k], c.ap, c.ready)
                c.used(t)
                done.append(t)
            return done

        parked = []
        ple_total = SquareSum(norm_row)
        feed_forward("a", gated_chunk_and_more, add_to_x, total.inverse)
        for _ in modulation:
            pass
        ada.close()
        t = v_stt(gain[:, 0:KD], mod[:, KD:2 * KD], 1.0, vec("pre_mix_g", 0, KD), ALU.add, ALU.mult, mod_ready)
        t = [v_tt(gain[:, 0:KD], gain[:, 0:KD], vec("norm_final", 0, KD), ALU.mult, t),
             v_tt(gain[:, KD:2 * KD], mod[:, 2 * KD:3 * KD], vec("post_mix_g", 0, KD), ALU.mult),
             v_stt(gain[:, 2 * KD:3 * KD], mod[:, 4 * KD:5 * KD], 1.0, vec("pre_ffn_g", 0, KD), ALU.add, ALU.mult),
             v_tt(gain[:, 3 * KD:4 * KD], mod[:, 5 * KD:6 * KD], vec("post_ffn_g", 0, KD), ALU.mult)]
        act.wait(t, mod_ready)
        dve.wait(t)

        free = fence()
        dve.wait(free)
        act.wait(free)
        pool.wait(free)
        row2 = Buf(sb_in(ple, "norm_row2", [P, T])[:, :])
        plain_row = Buf(sb_in(ple, "plain_row", [P, T])[:, :])
        final_total, next_total = SquareSum(plain_row), SquareSum(row2)
        emb = [Buf(sb_in(ple, f"emb{i}", [P, T])[:, :]) for i in range(4)]
        for m in range(KD):
            if m % 4 == 0:
                unit = weights.take("w_pp")
                weights.ahead()
                for mi in range(4):
                    ps, mark = one("w_pp", rhs_p, (2 * mi, 2 * mi + 1), unit)
                    t = a_copy(emb[mi].ap, ps.ap, mark, emb[mi].busy)
                    ps.used(t)
                    emb[mi].written(t)
            if m == 0:
                ple_total.inverse()
            ps, mark = one("w_pg", h_rhs())
            h_used(mark)
            s = tmps.take()
            t = unscale(s.ap, ps, mark, s.busy)
            ps.used(t)
            t = a_act(s.ap, s.ap, ACT.Sigmoid, t)
            t = v_tt(s.ap, s.ap, emb[m % 4].ap, ALU.mult, t, emb[m % 4].ready)
            emb[m % 4].used(t)
            t2 = v_tt(x[m].ap, x[m].ap, s.ap, ALU.add, t, x[m].ready, x[m].busy)
            s.written(t)
            s.used(t2)
            x[m].written(t2)
            x[m].used(final_total.add(x[m].ap, t2), next_total.add(x[m].ap, t2, vec("norm_final", m)))
            parked += park(x, [m])

        t = v_stt(row2.ap, plain_row.ap, EPS, row2.ap, ALU.mult, ALU.add, final_total.total, next_total.total)
        plain_row.busy = [t]
        weights.ahead(2)
        next_total.inverse(eps=EPS * EPS, total=t)
        normed_to_h(x, row2, lambda k: gain[:, k:k + 1], lambda k: mod[:, k:k + 1])
        first_at = two(("w_qk_at", "w_qk_at"), h_rhs())
        row_dma = Dma("row_dma")
        parked.append(row_dma.start(sync, io["row_park"], plain_row.ap, final_total.total))
        ple.close()

        resident.close()
        free = fence() + parked
        for q in (act, dve, pool):
            q.wait(free)
        ml = ExitStack()
        W1 = ML_D + 1
        v_ml = sb_in(ml, "v_ml", [P, NB, ML_H, W1])
        sig_o = [Buf(sb_in(ml, f"sig_o{i}", [P, T])[:, :]) for i in range(ML_H)]
        gate_cols = sb_in(ml, "gate_cols", [P, 4, 32])
        decay = sb_in(ml, "decay", [P, 32])
        gates_raw = sb_in(ml, "gates_raw", [36, T])
        late = sb_in(ml, "late_consts", [P, 4 * P])
        rotate_mat, later_neg = late[:, 0:P], late[:, P:2 * P]
        band_bf = sb_in(ml, "band_bf", [P, 2 * P], BF16)
        t_late = load(Dma("dma_late"), late[:, :], io["late_consts"], free)
        pe.wait(t_late, v_copy(band_bf[:, :], late[:, 2 * P:4 * P], t_late))
        pool.wait(t_late)
        t_ones = pool.mark(lambda e: e.memset(v_ml[:, :, :, ML_D:W1], 1.0))
        v_ml_ready = [t_ones]

        at = ExitStack()
        q_at = [Buf(sb_in(at, f"q_at{i}", [P, T])[:, :]) for i in range(4)]
        k_pad = [[Buf(sb_in(at, f"k_pad{g}{par}", [P, T])[:, :]) for par in range(2)] for g in range(AT_KV)]
        v_at = Buf(sb_in(at, "v_at", [P, T])[:, :])
        turn = ExitStack()
        rope_mem = sb_in(turn, "rope_mem", [P, 2 * T])
        dma_rope = Dma("dma_rope")
        t_rope = load(dma_rope, rope_mem[:, :], io["rope"], free)
        rope_in = Ring([Buf(sb_in(turn, f"rope_in{i}", [P, T])[:, :]) for i in range(2)])
        pad_zeros = []
        for g in range(AT_KV):
            for par in range(2):
                pad_zeros.append(dve.mark((lambda o: lambda e: e.memset(o, 0.0))(k_pad[g][par].ap[head_rows(1 - par), :])))

        def rotate(s, ps, mark):
            raw = rope_in.take()
            t = a_copy(raw.ap, ps.ap, mark, raw.busy)
            ps.used(t)
            raw.written(t)
            rot = pairs.take()
            for half in range(NH):
                cols = slice(half * HALF, (half + 1) * HALF)
                mark = mm_mark(rot.half(half), rotate_mat, raw.ap[:, cols], True, True, t, rot.busy)
            rot.written(mark)
            w = tmps.take()
            t_s = v_tt(w.ap, rot.ap, rope_mem[:, T:2 * T], ALU.mult, mark, t_rope, w.busy)
            rot.used(t_s)
            t_c = g_tt(raw.ap, raw.ap, rope_mem[:, 0:T], ALU.mult, mark, t, t_rope)
            if s < 4:
                t = v_tt(q_at[s].ap, raw.ap, w.ap, ALU.add, t_s, t_c)
                q_at[s].written(t)
            else:
                t = v_tt(w.ap, raw.ap, w.ap, ALU.add, t_s, t_c)
                for g in range(AT_KV):
                    for par in range(2):
                        pad = k_pad[g][par]
                        t1 = v_copy(pad.ap[head_rows(par), :], w.ap[head_rows(g), :], t)
                        pad.written(pad_zeros, t1)
                t = t1
            raw.written(t_c)
            raw.used(t)
            w.written(t_s)
            w.used(t)

        def turn_steps(ps, mark, turned, write):
            f = tmps.take()
            t = a_copy(f.ap, ps.ap, mark, f.busy)
            ps.used(t)
            f.written(t)
            yield
            for b in range(NB):
                mark = transpose(turned.ap[:, b * P:(b + 1) * P], f.ap[:, b * P:(b + 1) * P], t, turned.busy)
            f.used(mark)
            turned.written(mark)
            turned.used(write(turned.ap.rearrange("p (b d) -> p b d", b=NB), mark))

        for s in range(5):
            ps, mark = first_at[s] if s < 2 else one("w_qk_at", h_rhs())
            h_used(mark)
            if s > 0:
                rotate(s - 1, *previous)
            previous = (ps, mark)
        ps, mark = one("w_v_at", h_rhs())
        h_used(mark)
        rotate(4, *previous)
        for _ in turn_steps(ps, mark, pairs.take(), lambda ap, m: v_at.written(
                a_copy(v_at.ap.rearrange("p (b d) -> p b d", b=NB), ap, m)) or v_at.ready[0]):
            pass
        turn.close()

        def value_and_gate_steps():
            for s in range(8, 17):
                unit = weights.take("w_ml" if s < 16 else "w_gates")
                weights.ahead()
                ps = proj_pair
                yield from project_steps(ps, unit, tuple(range(KD)), h_rhs(), ps.busy)
                mark = ps.ready[0]
                h_used(mark)
                if s < 12:
                    yield from turn_steps(ps, mark, ps, lambda ap, m: v_ml_ready.append(
                        a_copy(v_ml[:, :, s - 8, 0:ML_D], ap, m)) or v_ml_ready[-1])
                elif s < 16:
                    t = a_copy(sig_o[s - 12].ap, ps.ap, mark)
                    ps.used(t)
                    sig_o[s - 12].written(t)
                else:
                    t = a_copy(gates_raw[:, :], ps.ap[0:36, :], mark)
                    ps.used(t)
                    gates_raw_ready.append(t)

        gates_raw_ready = []
        filler = value_and_gate_steps()

        at_scale = AT_DIM ** -0.5
        free = fence()
        for q in (act, dve):
            q.wait(free)
        HG = AT_H // AT_KV
        prob = [[Buf(sb_in(at, f"prob{i}{h}", [P, 2 * P])[:, :]) for h in range(HG)] for i in range(2)]
        prob_t = Ring([Buf(sb_in(at, f"prob_t{i}", [P, 4 * P])[:, :]) for i in range(2)])
        o_tok = Ring([Buf(sb_in(at, f"o_tok{i}", [P, D_SB])[:, :]) for i in range(2)])
        o_out = Ring([Buf(sb_in(at, f"o_out{i}", [P, 4, P])[:, :, :]) for i in range(2)])
        sq_tok = Buf(sb_in(at, "sq_tok", [P, D_SB])[:, :])
        small_mem = sb_in(at, "at_small", [P, 2, 6, AT_H])
        smalls = [Buf(small_mem[:, i]) for i in range(2)]
        pt_banks, o_bank, turn_bank = Ring([banks[2], banks[3]]), banks[4], banks[5]
        o_dma = [Dma(f"o_dma{i}") for i in range(2)]
        o_parked = []

        def attend_scores(n, g):
            first = P if n == 0 else 0
            k0, width = (n - 1) * P + first, 2 * P - first
            sm = smalls[n % 2]
            hs = slice(g * HG, (g + 1) * HG)
            row_max, neg_max, row_sum, sink_e = (sm.ap[:, i, hs] for i in range(4))
            ts = []
            for hh in range(HG):
                h = g * HG + hh
                bank, off = banks[hh // 2], (hh % 2) * 2 * P
                pad = k_pad[g][h % 2]
                s_ap = bank.ap[:, off:off + width]
                mm(s_ap, q_at[h // 2].ap[:, n * P:(n + 1) * P], pad.ap[:, k0:k0 + width], True, False,
                   q_at[h // 2].ready, pad.ready, bank.busy if hh % 2 == 0 else None)
                mark = mm_mark(s_ap, ident_bf[:, :], band_bf[:, first:2 * P], False, True)
                if hh % 2:
                    bank.written(mark)
                    s3 = bank.ap.rearrange("p (a c) -> p a c", a=2)[:, :, 0:width]
                    t = dve.mark((lambda o, i: lambda e: e.tensor_reduce(o, i, AX.X, ALU.max))(
                        row_max[:, hh - 1:hh + 1], s3), mark, sm.busy)
                    bank.ready = [t]
                    ts.append(t)
            sinks = vec("sinks", g * HG, HG)
            t = v_stt(neg_max, row_max, at_scale, sinks, ALU.mult, ALU.max, ts)
            t_sk = v_tt(sink_e, sinks, neg_max, ALU.subtract, t)
            t_m = v_ts(neg_max, neg_max, -1.0, ALU.mult, t, t_sk)
            t_sk = a_act(sink_e, sink_e, ACT.Exp, t_sk)
            exps = [t_sk]
            for hh in range(HG):
                bank, off, pr = banks[hh // 2], (hh % 2) * 2 * P, prob[g][hh]
                t = act.mark((lambda o, i, b, a: lambda e: e.activation(o, i, ACT.Exp, bias=b, scale=at_scale,
                                                                         accum_out=a))(
                    pr.ap[:, 0:width], bank.ap[:, off:off + width], neg_max[:, hh:hh + 1], row_sum[:, hh:hh + 1]),
                    bank.ready, t_m, pr.busy)
                bank.used(t)
                pr.written(t)
                exps.append(t)
            return exps

        def attend_mix(n, g):
            first = P if n == 0 else 0
            k0, width = (n - 1) * P + first, 2 * P - first
            kbs = range(width // P)
            for hp in range(HG // 2):
                bank, pt = pt_banks.take(), prob_t.take()
                for hh in range(2):
                    pr = prob[g][2 * hp + hh]
                    for kb in kbs:
                        mark = transpose(bank.ap[:, hh * 2 * P + kb * P:hh * 2 * P + (kb + 1) * P],
                                         pr.ap[:, kb * P:(kb + 1) * P], pr.ready, bank.busy)
                    pr.used(mark)
                bank.written(mark)
                i3, o3 = (x_.rearrange("p (a c) -> p a c", a=2)[:, :, 0:width] for x_ in (bank.ap, pt.ap))
                t = (a_copy if hp % 2 else v_copy)(o3, i3, mark, pt.busy)
                bank.used(t)
                pt.written(t)
                next(filler, None)
                for hh in range(2):
                    h = g * HG + 2 * hp + hh
                    for kb in kbs:
                        vb = (k0 // P + kb) * P + g * AT_DIM
                        mark = mm_mark(o_bank.ap[:, h * AT_DIM:(h + 1) * AT_DIM],
                                       pt.ap[:, hh * 2 * P + kb * P:hh * 2 * P + (kb + 1) * P],
                                       v_at.ap[:, vb:vb + AT_DIM], kb == 0, kb == kbs[-1], t, v_at.ready,
                                       o_bank.busy if h == 0 else None)
                pt.used(mark)
            return mark

        def attend_norm(n, mark, exps):
            sm, o = smalls[n % 2], o_tok.take()
            row_sum, sink_e, den, ssq = (sm.ap[:, i] for i in (2, 3, 4, 5))
            o_bank.written(mark)
            t = v_tt(den, row_sum, sink_e, ALU.add, exps)
            t = dve.mark(lambda e: e.reciprocal(den, den), t)
            t_o = v_tt(o.ap.rearrange("p (h d) -> p h d", h=AT_H), o_bank.ap.rearrange("p (h d) -> p h d", h=AT_H),
                       den.unsqueeze(2).to_broadcast([P, AT_H, AT_DIM]), ALU.mult, t, mark, o.busy)
            o_bank.used(t_o)
            t = act.mark(lambda e: e.activation(sq_tok.ap, o.ap, ACT.Square, accum_out=ssq[:, 0:1]),
                         t_o, sq_tok.ready)
            sq_tok.written(t)
            t = a_act(ssq[:, 1:2], ssq[:, 0:1], ACT.Ln, t, bias=eps_col[:, 0:1], scale=1.0 / D_SB)
            t = a_act(ssq[:, 2:3], ssq[:, 1:2], ACT.Exp, t, scale=-0.5)
            t = v_ts(o.ap, o.ap, ssq[:, 2:3], ALU.mult, t)
            sm.busy = [t]
            o.written(t)
            return o

        def attend_out(n, o):
            out = o_out.take()
            for j in range(4):
                mark = transpose(turn_bank.ap[:, j * P:(j + 1) * P], o.ap[:, j * P:(j + 1) * P], o.ready,
                                 turn_bank.busy)
            o.used(mark)
            turn_bank.written(mark)
            ts = []
            for j in range(4):
                ts.append(v_ts(out.ap[:, j, :], turn_bank.ap[:, j * P:(j + 1) * P], vec("attn_norm_g", j),
                               ALU.mult, mark, out.busy))
            turn_bank.used(*ts)
            t = o_dma[n % 2].start(sync, io["o_park"].rearrange("j p t -> p j t")[:, :, n * P:(n + 1) * P], out.ap, ts)
            out.written(*ts)
            out.used(t)
            o_parked.append(t)

        act.do(lambda e: e.preload_act_table_set("natural_log_exp_and_others"))
        steps = [(n, g) for n in range(NB) for g in range(AT_KV)]
        exps = attend_scores(*steps[0])
        normed, waiting = None, []
        for i, (n, g) in enumerate(steps):
            waiting = (waiting if g else []) + exps
            next(filler, None)
            next(filler, None)
            mark = attend_mix(n, g)
            if i + 1 < len(steps):
                exps = attend_scores(*steps[i + 1])
            if g == AT_KV - 1:
                if normed:
                    attend_out(*normed)
                normed = (n, attend_norm(n, mark, waiting))
            next(filler, None)
        attend_out(*normed)
        for _ in filler:
            pass
        at.close()

        free = fence() + o_parked[-2:]
        for q in (act, dve, pool):
            q.wait(free)
        q_ml = [Buf(sb_in(ml, f"q_ml{i}", [P, T])[:, :]) for i in range(ML_H)]
        k_ml = [Buf(sb_in(ml, f"k_ml{i}", [P, T])[:, :]) for i in range(ML_H)]
        d_ring = Ring([Buf(sb_in(ml, f"d_tile{i}", [P, ML_H, P])[:, :, :]) for i in range(2)])
        conv = ExitStack()
        CP = ML_CONV - 1
        conv_in = Ring([Buf(sb_in(conv, f"conv_in{i}", [P, CP + T])[:, :]) for i in range(2)])
        for b in conv_in.bufs:
            b.zero = dve.mark((lambda o: lambda e: e.memset(o, 0.0))(b.ap[:, 0:CP]))

        def conv_taps(src, dst, taps, weight, bias, *w):
            t = v_ts(dst.ap, src.ap[:, 0:T], weight(0), ALU.mult, *w, s2=bias, op1=ALU.add)
            for i in range(1, taps):
                t = v_stt(dst.ap, src.ap[:, i:i + T], weight(i), dst.ap, ALU.mult, ALU.add, t)
            return t

        gate_e = sb_in(conv, "gate_e", [36, T])
        g_mem = sb_in(conv, "gate_mem", [32, 8, P])
        g_small = sb_in(conv, "gate_small", [32, 16])
        m_mem = sb_in(conv, "m_mem", [4, 64])
        gate_tokens = []

        def gate_steps():
            F = slice(32, 36)
            t_i = v_ts(gates_raw[0:4, :], gates_raw[0:4, :], vec("gate_b")[0:4, :], ALU.add, gates_raw_ready)
            t_f = v_ts(gates_raw[F, :], gates_raw[F, :], vec("gate_b")[F, :], ALU.add, gates_raw_ready,
                       s2=-1.0, op1=ALU.mult)
            t = v_ts(gate_e[F, :], gates_raw[F, :], EXACT_FROM, ALU.min, t_f)
            act.do(lambda e: e.preload_act_table_set("natural_log_exp_and_others"))
            t = a_act(gate_e[F, :], gate_e[F, :], ACT.Exp, t)
            t = a_act(gate_e[F, :], gate_e[F, :], ACT.Ln, t, bias=1.0)
            t_f = v_tt(gates_raw[F, :], gate_e[F, :], gates_raw[F, :], ALU.max, t)
            dma_g = Dma("dma_gates")
            dma_g.start(sync, io["gate_i"], gates_raw[0:4, :], t_i)
            t = dma_g.start(sync, io["gate_f"], gates_raw[F, :], t_f)
            yield
            dma_g.start(sync, g_mem[:, 0, :], io["gate_i"].rearrange("h (c t) -> (h c) t", t=P), t)
            t_g = dma_g.start(sync, g_mem[:, 1, :], io["gate_f"].rearrange("h (c t) -> (h c) t", t=P))
            yield
            I, NF, B, G, CM, M, W, X = (g_mem[:, i, :] for i in range(8))
            t_one = dve.mark(lambda e: e.memset(X, 1.0))
            t = dve.mark(lambda e: e.tensor_tensor_scan(B, X, NF, 0.0, ALU.mult, ALU.subtract), t_g, t_one)
            t = v_tt(G, I, B, ALU.subtract, t)
            t_cm = dve.mark(lambda e: e.tensor_tensor_scan(CM, X, G, -3e38, ALU.mult, ALU.max), t)
            t1 = v_copy(g_small[:, 0:1], CM[:, P - 1:P], t_cm)
            t2 = v_copy(g_small[:, 1:2], B[:, P - 1:P], t_cm)
            dma_g.start(sync, io["chunk_end"][0].rearrange("(r o) -> r o", o=1), g_small[:, 0:1], t1)
            t = dma_g.start(sync, io["chunk_end"][1].rearrange("(r o) -> r o", o=1), g_small[:, 1:2], t2)
            yield
            dma_g.start(sync, m_mem[:, 0:8], io["chunk_end"][0:1, :].rearrange("a (h c) -> (a h) c", c=8), t)
            t = dma_g.start(sync, m_mem[:, 8:16], io["chunk_end"][1:2, :].rearrange("a (h c) -> (a h) c", c=8))
            yield
            t0 = dve.mark(lambda e: e.memset(m_mem[:, 16:17], 0.0))
            t = dve.mark(lambda e: e.tensor_tensor_scan(m_mem[:, 17:25], m_mem[:, 0:8], m_mem[:, 8:16], 0.0,
                                                        ALU.max, ALU.add), t, t0)
            dma_g.start(sync, io["chunk_m"][0], m_mem[:, 16:24], t)
            t = dma_g.start(sync, io["chunk_m"][1], m_mem[:, 17:25])
            yield
            dma_g.start(sync, g_small[:, 2:3], io["chunk_m"][0].rearrange("h (c o) -> (h c) o", o=1), t)
            t = dma_g.start(sync, g_small[:, 3:4], io["chunk_m"][1].rearrange("h (c o) -> (h c) o", o=1))
            yield
            m_old, m_new, end_b, shift_c, dec = (g_small[:, i:i + 1] for i in (2, 3, 1, 4, 5))
            t_M = v_ts(M, CM, m_old, ALU.max, t)
            t_m_dram = Dma("dma_m_rows").start(sync, io["m_rows"], M, t_M)
            t_w = a_act(W, M, ACT.Exp, t_M, bias=m_old, scale=-1.0)
            t = v_tt(NF, B, M, ALU.add, t_M)
            t_nm = a_act(NF, NF, ACT.Exp, t, scale=-1.0)
            t = v_tt(shift_c, end_b, m_new, ALU.subtract, t_M)
            t_ws = a_act(I, G, ACT.Exp, t, bias=shift_c)
            t_d = a_act(dec, shift_c, ACT.Exp, t, bias=m_old)
            t = dma_g.start(sync, io["decay_row"].rearrange("(r o) -> r o", o=1), dec, t_d)
            yield
            t_dec = dma_g.start(sync, decay[:, :], io["decay_row"].partition_broadcast(P), t)
            out = pairs.take()
            for i, (row, tok) in enumerate(((G, t_cm), (W, t_w), (NF, t_nm), (I, t_ws))):
                mark = transpose(out.ap[:, 32 * i:32 * i + 32], row, tok, out.busy, rows=32)
            out.written(mark)
            t_cols = v_copy(gate_cols[:, :, :].rearrange("p a b -> p (a b)"), out.ap[:, 0:128], mark)
            out.used(t_cols)
            gate_tokens.extend([t_m_dram, t_dec, t_cols])

        gating = gate_steps()
        for s in range(8):
            ps, mark = one("w_ml", h_rhs())
            h_used(mark)
            src, acc_ = conv_in.take(), tmps.take()
            t = a_copy(src.ap[:, CP:], ps.ap, mark, src.busy)
            ps.used(t)
            if s == 0:
                for b in sig_o:
                    b.written(a_act(b.ap, b.ap, ACT.Sigmoid, b.ready))
            next(gating, None)
            t1 = conv_taps(src, acc_, ML_CONV, lambda i: vec("ml_conv_w", 8 * i + s), vec("ml_conv_b", s),
                           t, src.zero, acc_.busy)
            src.written(t)
            src.used(t1)
            out = q_ml[s] if s < 4 else k_ml[s - 4]
            t = a_act(out.ap, acc_.ap, ACT.Silu, t1)
            acc_.written(t1)
            acc_.used(t)
            out.written(t)
        for _ in gating:
            pass
        d_dma = [Dma(f"d_dma{i}") for i in range(2)]
        later = later_neg.unsqueeze(1).to_broadcast([P, ML_H, P])
        m_rows = io["m_rows"].rearrange("(h c) t -> c h t", c=NB)
        pool.wait(gate_tokens)
        dve.wait(gate_tokens)

        def chunk_cols(kind, c, n):
            v = gate_cols[:, kind, :].rearrange("p (h c) -> p h c", c=NB)[:, :, c:c + 1]
            return v if n == 1 else v.to_broadcast([P, ML_H, n])

        def weights_begin(c):
            d = d_ring.take()
            t = d_dma[c % 2].start(sync, d.ap, m_rows[c].partition_broadcast(P), d.busy, gate_tokens)
            d.written(g_tt(d.ap, later, d.ap, ALU.subtract, t))
            return c, d

        def weights_end(c, d):
            t = v_tt(d.ap, d.ap, chunk_cols(0, c, P), ALU.add, d.ready)
            d.written(a_act(d.ap, d.ap, ACT.Exp, t))
            return d

        d = [weights_end(*weights_begin(c)) for c in range(2)]
        conv.close()

        free = fence() + gate_tokens
        for q in (act, dve, pool):
            q.wait(free)
        state = Buf(sb_in(ml, "state", [P, ML_H, W1])[:, :, :])
        state.written(pool.mark(lambda e: e.memset(state.ap, 0.0)))

        def ring(name, shape, n=2):
            return Ring([Buf(sb_in(ml, f"{name}{i}", shape)[tuple(slice(None) for _ in shape)]) for i in range(n)])

        p_ring = ring("p_tile", [P, ML_H, P])
        kt_ring = ring("k_tok", [P, ML_H, P])
        vw_ring = ring("v_weighted", [P, ML_H, W1])
        num_ring = ring("num", [P, ML_H, W1])
        sq_ring = ring("num_sq", [P, ML_H, P], 1)
        hn_ring = ring("h_norm", [P, ML_H, P])
        sml_ring = ring("ml_small", [P, 4, ML_H])
        s_bank, tr_bank = banks[0], banks[7]
        k_scale = ML_D ** -0.5
        act.do(lambda e: e.preload_act_table_set("natural_log_exp_and_others"))

        def tokens_of(c):
            return slice(c * P, (c + 1) * P)

        def four(first_bank, lhsT, rhs, *w):
            mark = None
            for h in range(ML_H):
                bank = banks[first_bank + h // 2]
                mark = mm_mark(bank.ap[:, (h % 2) * W1:(h % 2 + 1) * W1], lhsT(h), rhs(h), True, True,
                               bank.busy if h % 2 == 0 else None, *w)
                if h % 2:
                    bank.written(mark)
            return mark

        def chunk_scores(c, d):
            tok = tokens_of(c)
            for h in range(ML_H):
                mark = mm_mark(s_bank.ap[:, h * P:(h + 1) * P], k_ml[h].ap[:, tok], q_ml[h].ap[:, tok], True, True,
                               s_bank.busy, k_ml[h].ready, q_ml[h].ready)
            s_bank.written(mark)
            p = p_ring.take()
            t = v_stt(p.ap, s_bank.ap.rearrange("p (h t) -> p h t", h=ML_H), k_scale, d.ap, ALU.mult, ALU.mult,
                      mark, d.ready, p.busy)
            s_bank.used(t)
            d.used(t)
            p.written(t)
            for h in range(ML_H):
                mark = transpose(tr_bank.ap[:, h * P:(h + 1) * P], k_ml[h].ap[:, tok], tr_bank.busy)
            tr_bank.written(mark)
            kt = kt_ring.take()
            t = act.mark((lambda o, i: lambda e: e.activation(o, i, ACT.Copy, scale=k_scale))(
                kt.ap.rearrange("p h t -> p (h t)"), tr_bank.ap), mark, kt.busy)
            tr_bank.used(t)
            kt.written(t)
            vw = vw_ring.take()
            t = g_tt(vw.ap, v_ml[:, c, :, :], chunk_cols(3, c, W1), ALU.mult, v_ml_ready, vw.busy)
            vw.written(t)
            return p, kt, vw

        def chunk_sums(c, p, kt, vw):
            tok = tokens_of(c)
            t_inter = four(3, lambda h: q_ml[h].ap[:, tok], lambda h: state.ap[:, h, :], state.ready)
            state.used(t_inter)
            t_next = four(5, lambda h: kt.ap[:, h, :], lambda h: vw.ap[:, h, :], kt.ready, vw.ready)
            t_intra = four(1, lambda h: p.ap[:, h, :], lambda h: v_ml[:, c, h, :], p.ready, v_ml_ready)
            kt.used(t_next)
            vw.used(t_next)
            p.used(t_intra)
            num = num_ring.take()
            ts = []
            for h in range(ML_H):
                bank = banks[3 + h // 2]
                t = act.mark((lambda o, i, s: lambda e: e.activation(o, i, ACT.Copy, scale=s))(
                    num.ap[:, h, :], bank.ap[:, (h % 2) * W1:(h % 2 + 1) * W1],
                    gate_cols[:, 1, h * NB + c:h * NB + c + 1]), t_inter, num.busy)
                bank.used(t)
                ts.append(t)
            t_st = []
            for h in range(ML_H):
                bank = banks[5 + h // 2]
                t = v_stt(state.ap[:, h, :], state.ap[:, h, :], decay[:, h * NB + c:h * NB + c + 1],
                          bank.ap[:, (h % 2) * W1:(h % 2 + 1) * W1], ALU.mult, ALU.add, t_next, state.busy, state.ready)
                bank.used(t)
                t_st.append(t)
            state.written(*t_st)
            t_n = []
            for b in range(2):
                bank = banks[1 + b]
                part = num.ap[:, 2 * b:2 * b + 2, :]
                t = v_tt(part, part, bank.ap[:, 0:2 * W1].rearrange("p (h w) -> p h w", h=2), ALU.add, ts, t_intra)
                bank.used(t)
                t_n.append(t)
            num.written(*t_n)
            return num

        def chunk_norm(c, num):
            sml = sml_ring.take()
            den_c = num.ap[:, :, ML_D:W1]
            dn, r, ss, sc = (sml.ap[:, i, :] for i in range(4))

            def as3(a):
                return a.unsqueeze(2)

            sq = sq_ring.take()
            t_sq = a_act(sq.ap, num.ap[:, :, 0:ML_D], ACT.Square, num.ready, sq.busy)
            t = v_stt(as3(dn), den_c, -1.0, den_c, ALU.mult, ALU.max, num.ready, sml.busy)
            t = v_tt(as3(dn), as3(dn), chunk_cols(2, c, 1), ALU.max, t)
            t_r = dve.mark((lambda o, i: lambda e: e.reciprocal(o, i))(r, dn), t)
            t_rr = v_tt(sc, r, r, ALU.mult, t_r)
            t = dve.mark((lambda o, i: lambda e: e.tensor_reduce(o, i, AX.X, ALU.add))(ss, sq.ap), t_sq)
            sq.written(t_sq)
            sq.used(t)
            t = v_tt(ss, ss, sc, ALU.mult, t, t_rr)
            t = a_act(ss, ss, ACT.Ln, t, bias=eps_col[:, 0:1], scale=1.0 / ML_D)
            t = a_act(ss, ss, ACT.Exp, t, scale=-0.5)
            return sml, t

        def chunk_scale(c, num, sml, t):
            hn = hn_ring.take()
            r, ss, sc = (sml.ap[:, i, :] for i in (1, 2, 3))
            t = v_tt(sc, ss, r, ALU.mult, t)
            t = v_tt(hn.ap, num.ap[:, :, 0:ML_D], sc.unsqueeze(2).to_broadcast([P, ML_H, ML_D]), ALU.mult, t, hn.busy)
            hn.written(t)
            sml.busy = [t]
            num.used(t)
            return c, hn

        def chunk_out(c, hn):
            for h in range(ML_H):
                mark = transpose(tr_bank.ap[:, h * P:(h + 1) * P], hn.ap[:, h, :], hn.ready, tr_bank.busy)
            tr_bank.written(mark)
            ts = []
            tok = tokens_of(c)
            for h in range(ML_H):
                ts.append(v_stt(hn.ap[:, h, :], tr_bank.ap[:, h * P:(h + 1) * P], vec("ml_norm_g", h),
                                sig_o[h].ap[:, tok], ALU.mult, ALU.mult, mark, sig_o[h].ready))
            tr_bank.used(*ts)
            t_hi = a_copy(h_hi[:, 0:ML_H, tok], hn.ap, ts, h_busy[0])
            t_lo = g_tt(h_lo[:, 0:ML_H, tok], hn.ap, h_hi[:, 0:ML_H, tok].bitcast(F32), ALU.subtract, t_hi, ts)
            hn.used(t_hi, t_lo)
            for k in range(ML_H):
                h_parts[k] += [t_hi, t_lo]

        def attention_back(j):
            t = tmps.take()
            t_in = o_dma[j % 2].start(sync, t.ap, io["o_park"][j], t.busy, o_parked[-2:])
            made = split(h_hi[:, 4 + j, :], h_lo[:, 4 + j, :], t.ap, t_in, h_busy[4 + j])
            t.written(t_in)
            t.used(*made)
            h_ready[4 + j], h_busy[4 + j] = made, []

        h_parts = [[] for _ in range(ML_H)]
        parts = chunk_scores(0, d[0])
        last = None
        for c in range(NB):
            scaled = chunk_scale(*last) if last else None
            num = chunk_sums(c, *parts)
            if c + 1 < NB:
                parts = chunk_scores(c + 1, d[(c + 1) % 2])
            if c + 2 < NB:
                begun = weights_begin(c + 2)
            if scaled:
                chunk_out(*scaled)
            if 0 < c < 5:
                attention_back(c - 1)
            last = (c, num, *chunk_norm(c, num))
            if c + 2 < NB:
                d[c % 2] = weights_end(*begun)
        chunk_out(*chunk_scale(*last))
        weights.ahead(2)
        ml.close()
        for k in range(ML_H):
            h_ready[k], h_busy[k] = h_parts[k], []

        def normed_sum(y, x, total, done):
            total.inverse()
            for k in range(KD):
                e_tt = g_tt if k % 3 == 2 else v_tt
                t = e_tt(y[k].ap, y[k].ap, norm_row.ap, ALU.mult, y[k].ready, y[k].busy, norm_row.ready)
                norm_row.used(t)
                y[k].written(t)
                t = e_tt(x[k].ap, x[k].ap, y[k].ap, ALU.add, t, x[k].ready, x[k].busy)
                y[k].used(t)
                x[k].written(t)
                done(k)

        ys = ExitStack()
        free = fence()
        for q in (act, dve, pool):
            q.wait(free)
        y_mem = sb_in(ys, "y_mem", [P, KD, T])
        y = [Buf(y_mem[:, k, :]) for k in range(KD)]
        xs = ExitStack()
        next_row = Buf(sb_in(xs, "next_row", [P, T])[:, :])
        x = load_x(xs, "x_mid", io["x_park"], free + parked)
        plain_row = Buf(sb_in(xs, "plain_row_back", [P, T])[:, :])
        t_row = row_dma.start(sync, plain_row.ap, io["row_park"], free, parked)
        total = SquareSum(norm_row)
        order = (4, 5, 6, 7, 0, 1, 2, 3)
        for m in range(KD):
            ps, mark = one("w_out2", h_rhs(order), order)
            h_used(mark)
            t_sq = total.add(ps.ap, mark)
            t = act.mark((lambda o, i, g: lambda e: e.activation(o, i, ACT.Copy, scale=g))(
                y[m].ap, ps.ap, gain[:, KD + m:KD + m + 1]), mark)
            ps.used(t_sq, t)
            y[m].written(t)
            if m == 0:
                SquareSum(plain_row).inverse(total=t_row)
            t = v_stt(x[m].ap, x[m].ap, vec("norm_final", m), plain_row.ap, ALU.mult, ALU.mult,
                      x[m].ready, plain_row.ready)
            x[m].written(t)
        next_total = SquareSum(next_row, on_pe=True)
        normed_sum(y, x, total, lambda k: x[k].used(next_total.add(x[k].ap, x[k].ready)))
        weights.ahead(2)
        next_total.inverse()
        normed_to_h(x, next_row, lambda k: gain[:, 2 * KD + k:2 * KD + k + 1],
                    lambda k: mod[:, 3 * KD + k:3 * KD + k + 1])
        first_ffn = two(("w_gate2", "w_up2"), h_rhs())
        parked = park(x)
        xs.close()

        ff = ExitStack()
        free = fence() + parked
        act.wait(free)
        dve.wait(free)
        FP = FFN_CONV - 1
        conv_in = Ring([Buf(sb_in(ff, f"ffn_conv_in{i}", [P, FP + T])[:, :]) for i in range(2)])
        val = Ring([Buf(sb_in(ff, "ffn_value", [P, T])[:, :])])
        for b in conv_in.bufs:
            b.zero = dve.mark((lambda o: lambda e: e.memset(o, 0.0))(b.ap[:, 0:FP]))

        def convolved_chunk(i, start):
            outs = []
            for n, (name, c, ring_) in enumerate((("w_gate2", i, tmps), ("w_up2", KF + i, val))):
                ps, mark = first_ffn[n] if i == 0 else one(name, h_rhs())
                h_used(mark)
                src, dst = conv_in.take(), ring_.take()
                t = a_copy(src.ap[:, FP:], ps.ap, mark, src.busy)
                ps.used(t)
                t1 = conv_taps(src, dst, FFN_CONV, lambda j: vec("ffn_conv_w", 2 * KF * j + c), vec("ffn_conv_b", c),
                               t, src.zero, dst.busy)
                src.written(t)
                src.used(t1)
                dst.written(t1)
                if name == "w_gate2":
                    t1 = a_act(dst.ap, dst.ap, ACT.Gelu_apprx_tanh, t1)
                    dst.written(t1)
                outs.append(dst)
            a, b = outs
            t = v_tt(a.ap, a.ap, b.ap, ALU.mult, a.ready, b.ready)
            b.used(t)
            a.written(t)
            return a

        def add_to_y(g, m, ps, mark):
            if g == 0:
                t = a_copy(y[m].ap, ps.ap, mark, y[m].busy, y[m].ready)
            else:
                t = v_tt(y[m].ap, y[m].ap, ps.ap, ALU.add, mark, y[m].ready)
            ps.used(t)
            y[m].written(t)
            if g == n_groups - 1:
                t_sq = total.add(y[m].ap, t)
                y[m].written(act.mark((lambda o, g_: lambda e: e.activation(o, o, ACT.Copy, scale=g_))(
                    y[m].ap, gain[:, 3 * KD + m:3 * KD + m + 1]), t, t_sq))

        total = SquareSum(norm_row)
        feed_forward("b", convolved_chunk, add_to_y, None)
        ff.close()
        xs = ExitStack()
        x = load_x(xs, "x_last", io["x_park"], fence() + parked)
        done = []
        normed_sum(y, x, total,
                   lambda k: done.append(out_dma.start(sync, io["out"][k], x[k].ap, x[k].ready)))
        sync.wait(done[-1])
        xs.close()
        ys.close()
        return play(nc, sync, act, dve, pe, pool)


def play(nc, sync, act, dve, pe, pool):
    with nc.Block() as block:
        @block.sync
        def _(e):
            sync.play(e)

        @block.scalar
        def _(e):
            act.play(e)

        @block.vector
        def _(e):
            dve.play(e)

        @block.tensor
        def _(e):
            pe.play(e)

        @block.gpsimd
        def _(e):
            pool.play(e)


def stripes(w, first=0, last=None, k=KD, m=1):
    w = w[:, first:last]
    kk, mm_ = w.shape[0] // (P * k), w.shape[1] // (P * m)
    w = w.reshape(kk, k, P, mm_, m, P).transpose(0, 3, 2, 4, 1, 5)
    return np.ascontiguousarray(w.reshape(kk * mm_, P, m * k * P))


def columns(v):
    return v.reshape(-1, P).T


def layout(a):
    out = {}
    out["x"] = np.ascontiguousarray(a["x"][0].T).reshape(KD, P, T)
    out["p"] = np.ascontiguousarray(a["p"][0, 0].T).reshape(2, P, T)
    out["w_in_a"] = stripes(a["w_in"][0])
    out["w_pool"] = a["w_pool"][0]
    out["w_branch_a"] = stripes(a["w_branch_a"][0], k=4)
    out["w_branch_b"] = stripes(a["w_branch_b"][0], k=4)
    out["w_out"] = stripes(a["w_out"][0])
    out["w_ffn_gate"] = stripes(a["w_ffn_gate"][0])
    out["w_ffn_up"] = stripes(a["w_ffn_up"][0])
    out["w_ffn_down"] = stripes(a["w_ffn_down"][0], k=FFN_GROUP, m=8 // FFN_GROUP)
    out["w_ple_gate"] = stripes(a["w_ple_gate"][0])
    out["w_ple_proj"] = stripes(a["w_ple_proj"][0], k=2, m=4)
    w = a["w_in_2"][0]
    out["w_in_b_ml"] = stripes(w, 0, 2048)
    out["w_in_b_at"] = stripes(w, 2056, 2824)
    g = np.zeros((KD, P, P), w.dtype)
    g[:, :, 0:4] = w[:, 2048:2052].reshape(KD, P, 4)
    g[:, :, 32:36] = w[:, 2052:2056].reshape(KD, P, 4)
    out["w_in_b_gates"] = np.ascontiguousarray(g.transpose(1, 0, 2).reshape(P, KD * P))
    out["w_out_b"] = stripes(a["w_out_2"][0])
    out["w_up_b"] = stripes(a["w_up_2"][0])
    out["w_down_b"] = stripes(a["w_down_2"][0], k=FFN_GROUP, m=8 // FFN_GROUP)
    out["w_ada"] = np.ascontiguousarray(a["w_ada_2"][0].reshape(KD, P, 6, D).transpose(2, 0, 1, 3))
    vecs = np.zeros((P, N_VEC), np.float32)

    def put(name, value, rows=P):
        vecs[0:rows, VEC[name]:VEC[name] + value.shape[1]] = value

    for name, key in (("norm_mix", "norm_mix"), ("norm_ffn", "norm_ffn"), ("norm_ple", "norm_ple"),
                      ("norm_final", "norm_final"), ("pool_scale", "pool_scale"), ("pre_mix_g", "pre_mix_g_2"),
                      ("ml_conv_w", "ml_conv_w_2"), ("ml_conv_b", "ml_conv_b_2"), ("ml_norm_g", "ml_norm_g_2"),
                      ("attn_norm_g", "attn_norm_g_2"), ("post_mix_g", "post_mix_g_2"),
                      ("pre_ffn_g", "pre_ffn_g_2"), ("ffn_conv_w", "ffn_conv_w_2"), ("ffn_conv_b", "ffn_conv_b_2"),
                      ("post_ffn_g", "post_ffn_g_2"), ("b_ada", "b_ada_2"), ("c", "c_2")):
        put(name, columns(a[key].reshape(-1)))
    vecs[0:4, VEC["gate_b"]] = a["ml_i_b_2"][0]
    vecs[32:36, VEC["gate_b"]] = a["ml_f_b_2"][0]
    put("sinks", np.broadcast_to(a["attn_sinks_2"], (P, AT_H)))
    out["vecs"] = vecs
    out["consts"], out["masks"], out["late_consts"], out["rope"] = constants()
    return out


SCRATCH = {"x_park": (KD, P, T), "row_park": (P, T), "o_park": (4, P, T), "gate_i": (4, T), "gate_f": (4, T),
           "chunk_end": (2, 32), "chunk_m": (2, 4, 8), "m_rows": (32, P), "decay_row": (32,)}



def build(nc, arrays):
    io = {}
    for name, v in arrays.items():
        io[name] = nc.dram_tensor(f"in_{name}", v.shape, F32, kind="ExternalInput").ap()
    for name, shape in SCRATCH.items():
        io[name] = nc.dram_tensor(name, shape, F32, kind="Internal").ap()
    io["out"] = nc.dram_tensor("out_dram", (KD, P, T), F32, kind="ExternalOutput").ap()
    two_blocks(nc, io)


def kernel(**inputs):
    import concourse.bacc as bacc
    from concourse.bass_utils import run_bass_kernel_spmd

    nc = bacc.Bacc("TRN2", target_bir_lowering=False, num_devices=1)
    arrays = layout({k: np.asarray(v) for k, v in inputs.items()})
    build(nc, arrays)
    r = run_bass_kernel_spmd(nc, [{f"in_{k}": v for k, v in arrays.items()}], core_ids=[0])
    return np.ascontiguousarray(r.results[0]["out_dram"].reshape(D, T).T)[None]
```
